# Optimizing a Trainium2 kernel written in Bass

```python
import jax
import jax.numpy as jnp
from jax import lax
import numpy as np

D_MODEL = 1024
BATCH = 1
SEQ = 1024
DEPTH = 2

N_MIXERS = 3
ROPE_THETA = 500000.0
EPS = 1e-6
BLOCK = 128

A_HEADS = 16
A_KV_HEADS = 4
A_HEAD_DIM = D_MODEL // A_HEADS
A_ROT_DIM = A_HEAD_DIM // 4
A_WINDOW = 128

B_CONV_WIDTH = 3

C_HEADS = 16
C_NOPE_DIM = 64
C_ROPE_DIM = 32
C_V_DIM = 64
C_Q_RANK = 384
C_KV_RANK = 256

D_FF = ((8 * D_MODEL + 767) // 768) * 256

N_LAYERS_A = (DEPTH + N_MIXERS - 1) // N_MIXERS
N_LAYERS_B = (DEPTH + N_MIXERS - 2) // N_MIXERS
N_LAYERS_C = DEPTH // N_MIXERS

kernel_name = 'hybrid_swa_sink_shortconv_mla_swiglu'

def rms_norm(x, g):
    xf = x.astype(jnp.float32)
    y = xf * lax.rsqrt(jnp.mean(xf * xf, axis=-1, keepdims=True) + EPS)
    return (y * g.astype(jnp.float32)).astype(x.dtype)

def rotate(x, pos):
    r = x.shape[-1]
    inv_freq = ROPE_THETA ** (-jnp.arange(0, r, 2, dtype=jnp.float32) / r)
    ang = pos.astype(jnp.float32)[:, :, None] * inv_freq
    cos = jnp.cos(ang)[:, :, None, :]
    sin = jnp.sin(ang)[:, :, None, :]
    x1, x2 = jnp.split(x.astype(jnp.float32), 2, axis=-1)
    out = jnp.concatenate([x1 * cos - x2 * sin, x2 * cos + x1 * sin], axis=-1)
    return out.astype(x.dtype)

def swa_sink_attention(h, pos, w_qkv, q_norm, k_norm, sinks, w_o):
    b, s, _ = h.shape
    hq, hkv, hd = A_HEADS, A_KV_HEADS, A_HEAD_DIM
    grp = hq // hkv
    nblk = s // BLOCK
    q, k, v = jnp.split(h @ w_qkv, [hq * hd, (hq + hkv) * hd], axis=-1)
    q = rms_norm(q.reshape(b, s, hq, hd), q_norm)
    k = rms_norm(k.reshape(b, s, hkv, hd), k_norm)
    v = v.reshape(b, s, hkv, hd)
    q = jnp.concatenate([rotate(q[..., :A_ROT_DIM], pos), q[..., A_ROT_DIM:]], axis=-1)
    k = jnp.concatenate([rotate(k[..., :A_ROT_DIM], pos), k[..., A_ROT_DIM:]], axis=-1)
    qb = q.reshape(b, nblk, BLOCK, hkv, grp, hd)
    kb = k.reshape(b, nblk, BLOCK, hkv, hd)
    vb = v.reshape(b, nblk, BLOCK, hkv, hd)
    pad = ((0, 0), (1, 0), (0, 0), (0, 0), (0, 0))
    kw = jnp.concatenate([jnp.pad(kb, pad)[:, :-1], kb], axis=2)
    vw = jnp.concatenate([jnp.pad(vb, pad)[:, :-1], vb], axis=2)
    scores = jnp.einsum('bnqkgd,bnjkd->bnkgqj', qb, kw).astype(jnp.float32) * (hd ** -0.5)
    qi = jnp.arange(BLOCK)[:, None]
    kj = jnp.arange(2 * BLOCK)[None, :]
    delta = qi + BLOCK - kj
    band = (delta >= 0) & (delta < A_WINDOW)
    has_prev = (jnp.arange(nblk) > 0)[:, None, None] | (kj >= BLOCK)[None]
    valid = band[None] & has_prev
    scores = jnp.where(valid[None, :, None, None], scores, -jnp.inf)
    sink = sinks.astype(jnp.float32).reshape(hkv, grp)[None, None, :, :, None, None]
    m = jnp.maximum(jnp.max(scores, axis=-1, keepdims=True), sink)
    p = jnp.exp(scores - m)
    p = p / (jnp.sum(p, axis=-1, keepdims=True) + jnp.exp(sink - m))
    o = jnp.einsum('bnkgqj,bnjkd->bnqkgd', p.astype(vw.dtype), vw)
    return o.reshape(b, s, hq * hd) @ w_o

def short_conv_mixer(h, w_in, conv_w, w_out):
    s = h.shape[1]
    b_gate, c_gate, u = jnp.split(h @ w_in, 3, axis=-1)
    z = c_gate * u
    zp = jnp.pad(z, ((0, 0), (B_CONV_WIDTH - 1, 0), (0, 0)))
    y = sum(conv_w[i] * zp[:, i:i + s] for i in range(B_CONV_WIDTH))
    return (b_gate * y) @ w_out

def mla_attention(h, pos, w_down, q_a_norm, kv_a_norm, w_q_up, w_kv_up, q_norm, k_norm, w_o):
    b, s, _ = h.shape
    nh = C_HEADS
    dqk = C_NOPE_DIM + C_ROPE_DIM
    nblk = s // BLOCK
    cq, ckv, k_rope = jnp.split(h @ w_down, [C_Q_RANK, C_Q_RANK + C_KV_RANK], axis=-1)
    cq = rms_norm(cq, q_a_norm)
    ckv = rms_norm(ckv, kv_a_norm)
    q = (cq @ w_q_up).reshape(b, s, nh, dqk)
    k_nope, v = jnp.split((ckv @ w_kv_up).reshape(b, s, nh, C_NOPE_DIM + C_V_DIM), [C_NOPE_DIM], axis=-1)
    k = jnp.concatenate([k_nope, jnp.broadcast_to(k_rope[:, :, None, :], (b, s, nh, C_ROPE_DIM))], axis=-1)
    q = rms_norm(q, q_norm)
    k = rms_norm(k, k_norm)
    q = jnp.concatenate([q[..., :C_NOPE_DIM], rotate(q[..., C_NOPE_DIM:], pos)], axis=-1)
    k = jnp.concatenate([k[..., :C_NOPE_DIM], rotate(k[..., C_NOPE_DIM:], pos)], axis=-1)
    scale = dqk ** -0.5
    kpos = jnp.arange(s)
    qblocks = jnp.moveaxis(q.reshape(b, nblk, BLOCK, nh, dqk), 1, 0)

    def block_attn(args):
        qblk, j = args
        sc = jnp.einsum('bqhd,bkhd->bhqk', qblk, k).astype(jnp.float32) * scale
        qpos = j * BLOCK + jnp.arange(BLOCK)
        sc = jnp.where(kpos[None, :] <= qpos[:, None], sc, -jnp.inf)
        p = jax.nn.softmax(sc, axis=-1)
        return jnp.einsum('bhqk,bkhd->bqhd', p.astype(v.dtype), v)

    o = lax.map(block_attn, (qblocks, jnp.arange(nblk)))
    o = jnp.moveaxis(o, 0, 1).reshape(b, s, nh * C_V_DIM)
    return o @ w_o

def swiglu_ffn(h, w_gate_up, w_down):
    gate, up = jnp.split(h @ w_gate_up, 2, axis=-1)
    return (jax.nn.silu(gate) * up) @ w_down

def _normal(key, shape, scale):
    return jax.random.normal(key, shape, jnp.float32) * scale

def setup_inputs(seed: int = 0) -> dict:
    key = jax.random.key(seed)
    ks = jax.random.split(key, 24)
    d = D_MODEL
    out_scale = (2 * DEPTH) ** -0.5
    qkv_width = (A_HEADS + 2 * A_KV_HEADS) * A_HEAD_DIM
    dqk = C_NOPE_DIM + C_ROPE_DIM
    return {
        'x': _normal(ks[0], (BATCH, SEQ, d), 1.0),
        'positions': jax.random.randint(ks[1], (BATCH, 1), 0, 4096, dtype=jnp.int32) + jnp.arange(SEQ, dtype=jnp.int32)[None, :],
        'mix_norm': 1.0 + _normal(ks[2], (DEPTH, d), 0.02),
        'ffn_norm': 1.0 + _normal(ks[3], (DEPTH, d), 0.02),
        'a_w_qkv': _normal(ks[4], (N_LAYERS_A, d, qkv_width), d ** -0.5),
        'a_q_norm': 1.0 + _normal(ks[5], (N_LAYERS_A, A_HEAD_DIM), 0.02),
        'a_k_norm': 1.0 + _normal(ks[6], (N_LAYERS_A, A_HEAD_DIM), 0.02),
        'a_sinks': _normal(ks[7], (N_LAYERS_A, A_HEADS), 0.5),
        'a_w_o': _normal(ks[8], (N_LAYERS_A, A_HEADS * A_HEAD_DIM, d), (A_HEADS * A_HEAD_DIM) ** -0.5 * out_scale),
        'b_w_in': _normal(ks[9], (N_LAYERS_B, d, 3 * d), d ** -0.5),
        'b_conv_w': _normal(ks[10], (N_LAYERS_B, B_CONV_WIDTH, d), B_CONV_WIDTH ** -0.5),
        'b_w_out': _normal(ks[11], (N_LAYERS_B, d, d), d ** -0.5 * out_scale),
        'c_w_down': _normal(ks[12], (N_LAYERS_C, d, C_Q_RANK + C_KV_RANK + C_ROPE_DIM), d ** -0.5),
        'c_q_a_norm': 1.0 + _normal(ks[13], (N_LAYERS_C, C_Q_RANK), 0.02),
        'c_kv_a_norm': 1.0 + _normal(ks[14], (N_LAYERS_C, C_KV_RANK), 0.02),
        'c_w_q_up': _normal(ks[15], (N_LAYERS_C, C_Q_RANK, C_HEADS * dqk), C_Q_RANK ** -0.5),
        'c_w_kv_up': _normal(ks[16], (N_LAYERS_C, C_KV_RANK, C_HEADS * (C_NOPE_DIM + C_V_DIM)), C_KV_RANK ** -0.5),
        'c_q_norm': 1.0 + _normal(ks[17], (N_LAYERS_C, dqk), 0.02),
        'c_k_norm': 1.0 + _normal(ks[18], (N_LAYERS_C, dqk), 0.02),
        'c_w_o': _normal(ks[19], (N_LAYERS_C, C_HEADS * C_V_DIM, d), (C_HEADS * C_V_DIM) ** -0.5 * out_scale),
        'f_w_gate_up': _normal(ks[20], (DEPTH, d, 2 * D_FF), d ** -0.5),
        'f_w_down': _normal(ks[21], (DEPTH, D_FF, d), D_FF ** -0.5 * out_scale),
    }

def reference(x, positions, mix_norm, ffn_norm, a_w_qkv, a_q_norm, a_k_norm, a_sinks, a_w_o, b_w_in, b_conv_w, b_w_out, c_w_down, c_q_a_norm, c_kv_a_norm, c_w_q_up, c_w_kv_up, c_q_norm, c_k_norm, c_w_o, f_w_gate_up, f_w_down):
    for i in range(DEPTH):
        kind = i % N_MIXERS
        j = i // N_MIXERS
        h = rms_norm(x, mix_norm[i])
        if kind == 0:
            y = swa_sink_attention(h, positions, a_w_qkv[j], a_q_norm[j], a_k_norm[j], a_sinks[j], a_w_o[j])
        elif kind == 1:
            y = short_conv_mixer(h, b_w_in[j], b_conv_w[j], b_w_out[j])
        else:
            y = mla_attention(h, positions, c_w_down[j], c_q_a_norm[j], c_kv_a_norm[j], c_w_q_up[j], c_w_kv_up[j], c_q_norm[j], c_k_norm[j], c_w_o[j])
        x = x + y
        h = rms_norm(x, ffn_norm[i])
        x = x + swiglu_ffn(h, f_w_gate_up[i], f_w_down[i])
    return x


_drawn_inputs = setup_inputs


def setup_inputs(seed=0):
    import zlib

    import numpy as np

    out = dict(_drawn_inputs(seed))
    spreads = {}
    factors = {'mix_norm': 3.528, 'ffn_norm': 4.784, 'a_q_norm': 8.0, 'a_k_norm': 8.0, 'a_sinks': 29.915}
    for name, (base, spread) in spreads.items():
        noise = np.random.default_rng([zlib.crc32(name.encode()), seed]).standard_normal(out[name].shape)
        drawn = base * np.exp(spread * noise) if base else spread * noise
        out[name] = jnp.asarray(drawn.astype(out[name].dtype))
    for name, factor in factors.items():
        out[name] = (out[name] * factor).astype(out[name].dtype)
    return out
```

```python
import concourse.bass as bass
import numpy as np
from concourse import mybir

F32 = mybir.dt.float32
F32R = mybir.dt.float32r
I32 = mybir.dt.int32
ALU = mybir.AluOpType
ACT = mybir.ActivationFunctionType
AX_X = mybir.AxisListType.X

P = 128
D = 1024
S = 1024
KT = D // P
NBLK = S // P
HALF = 512
HB = HALF // P
EPS = 1e-6
FF = ((8 * D + 767) // 768) * 256
HQ, HKV, HD = 16, 4, 64
GRP = HQ // HKV
NQK = HQ + HKV
QKW = NQK * HD
QKVW = (HQ + 2 * HKV) * HD
ROT = HD // 4
THETA = 500000.0
CW = 3
PIECE = 1024
NEG = -1e30

AHEAD = 3
Q_PIECES = QKVW * D // P // PIECE
O_PIECES = D // P
F_CHUNKS = FF // P // 2
F_PER = 6
C_CHUNKS = D // P // 2
C_PER = 8


class Phase:

    def __init__(self, base, n, per, ring, stages, landed):
        self.base, self.n, self.per, self.ring, self.stages = base, n, per, ring, stages
        self.landed = list(landed)
        self.after = [v + (n // stages if s < stages else 0) for s, v in enumerate(landed)]

    def piece(self, c, j):
        return c * self.per + (self.base + j)

    def slot(self, j):
        return j % self.ring

    def stage(self, j):
        return j % self.stages

    def arrival(self, c, j):
        return c * (16 * (self.per // self.stages)) + 16 * (self.landed[j % self.stages] + j // self.stages + 1)


PH_Q = Phase(0, Q_PIECES, 4, 4, 4, [0, 0, 0, 0])
PH_O = Phase(PH_Q.base + PH_Q.n, O_PIECES, 4, 4, 4, PH_Q.after)
PH_F0 = Phase(PH_O.base + PH_O.n, F_CHUNKS * F_PER, F_PER, 6, 3, PH_O.after)
PH_C = Phase(PH_F0.base + PH_F0.n, C_CHUNKS * C_PER, C_PER, 4, 4, PH_F0.after)
PH_F1 = Phase(PH_C.base + PH_C.n, F_CHUNKS * F_PER, F_PER, 6, 3, PH_C.after)
PH_F = [PH_F0, PH_F1]
N_PIECES = PH_F1.base + PH_F1.n

D_O, D_F0 = 0, 16 * 4
D_C = D_F0 + 16 * F_CHUNKS
D_F1 = D_C + 16 * C_CHUNKS
D_F = [D_F0, D_F1]
T_F = [0, 2 * F_CHUNKS]
A_F = [0, 2 * F_CHUNKS + 2 * C_CHUNKS]
A_C = 2 * F_CHUNKS
U_C = 2 * 2 * F_CHUNKS

U_F = [0, 2 * F_CHUNKS + 2 * C_CHUNKS]
INV_FREQ = np.float32(THETA) ** (-np.arange(0, ROT, 2, dtype=np.float32) / np.float32(ROT))
ROUND = 1.5 * 2.0 ** 23
PI_IN = 3.1415925
C_ANGLES = 13


def parts_of(x, bits, n):
    out = []
    for _ in range(n):
        e = 2.0 ** (np.floor(np.log2(abs(x))) - bits + 1)
        out.append(np.round(x / e) * e)
        x -= out[-1]
    return out


TWO_PI = parts_of(2 * np.pi, 8, 4)


def pt_count(n, last):
    done = min(n, HKV) + 2 * max(n - HKV, 0)
    return done + (1 if n < HKV or not last else 2)


def split_ahead(split, eng, ph, c, j):
    split(eng, ph, c, j + AHEAD)


G_MIX, G_FFN, G_CONV, G_ROWS = 0, 2 * KT, 4 * KT, 4 * KT + CW * KT


def decoder_kernel(nc, ctx, t, out):
    KB = 1024
    base = (nc.sbuf_base + 127) // 128 * 128

    def sb(name, shape, dt, kb):
        return nc.alloc_sbuf_tensor_at(name, [P] + shape, dt, offset=int(base + kb * KB))

    X = sb("X", [KT, S], F32, 0)
    H = sb("H", [2, KT, S], F32R, 32)
    STG = sb("STG", [4, PIECE], F32, 96)
    WR = sb("WR", [6, 2, PIECE], F32R, 112)
    A = sb("A", [2, 2, S], F32R, 160)
    SG = sb("SG", [2, HALF], F32, 176)
    A32 = sb("A32", [2, HALF], F32, 180)
    BG = sb("BG", [S], F32, 144)
    CG = sb("CG", [S], F32, 148)
    ZC = sb("ZC", [CW - 1 + S], F32, 152)
    YC = sb("YC", [HALF], F32, 157)
    XN = sb("XN", [NBLK, D], F32, 144)
    QKV = sb("QKV", [NBLK, QKVW], F32, 144)
    QS = sb("QS", [24, P], F32R, 96)
    QT = sb("QT", [HQ, P], F32R, 108)
    KTT = sb("KTT", [2, HKV, 2, P], F32R, 116)
    PR = sb("PR", [2, GRP, 2 * P], F32, 124)
    PT = sb("PT", [2, 2, GRP * P], F32, 132)
    SQ = sb("SQ", [2, HALF], F32, 192)
    ACC = sb("ACC", [HALF], F32, 196)
    DG = sb("DG", [HALF], F32, 198)
    RS = sb("RS", [HALF], F32, 200)
    XR = sb("XR", [2, HALF], F32, 202)
    IDN = sb("IDN", [P], F32, 206)
    ONE = sb("ONE", [P], F32, 206.5)
    GT = sb("GT", [G_ROWS], F32, 207)
    NS = sb("NS", [16], F32, 207.25)
    GRAW = sb("GRAW", [P], F32, 198)
    ASQ = sb("ASQ", [QKW], F32, 192)
    o = 197
    COS = sb("COS", [NBLK, ROT], F32, o)
    SIN = sb("SIN", [NBLK, ROT], F32, o + 0.5)
    MASK = sb("MASK", [3 * P], F32, o + 1)
    GBC = sb("GBC", [2 * HD + HQ], F32, o + 2.5)
    RT = sb("RT", [NQK, ROT], F32, o + 3.125)
    RU = sb("RU", [NQK, ROT], F32, o + 4.375)
    SSQ = sb("SSQ", [NBLK, NQK], F32, o + 5.625)
    RR = sb("RR", [NBLK, NQK], F32, o + 6.25)
    MH = sb("MH", [NQK], F32, o + 6.875)
    STAT = sb("STAT", [2, 6, GRP], F32, o + 7)
    ROWS = sb("ROWS", [2 * HD + HQ], F32, o + 7.25)
    ANG = sb("ANG", [4, 2, NBLK * ROT // 2], F32, 192)
    POSI = sb("POSI", [P], I32, 194)
    POSF = sb("POSF", [P], F32, 194.5)
    POST = sb("POST", [NBLK], F32, 195)
    INVF = sb("INVF", [ROT // 2], F32, 195.25)

    OUTB = sb("OUTB", [NBLK, D], F32, 32)

    PS = nc.alloc_psum_tensor("PS", [P, 8, HALF], F32)

    def sem(name):
        return ctx.enter_context(nc.semaphore(name))

    s_x = [sem(f"s_x{b}") for b in range(NBLK)]
    s_row, s_pos, s_gain = sem("s_row"), sem("s_pos"), sem("s_gain")
    s_idn0, s_idn, s_one = sem("s_idn0"), sem("s_idn"), sem("s_one")
    s_gt_ps, s_gt_sb, s_half = sem("s_gt_ps"), sem("s_gt_sb"), sem("s_half")
    stg = [sem(f"stg{s}") for s in range(4)]
    w_hi, w_split, w_used = sem("w_hi"), sem("w_split"), sem("w_used")
    x_tr, x_act, x_dve = sem("x_tr"), sem("x_act"), sem("x_dve")
    n_sq, n_acc, n_ss, n_v, n_r, n_dg, n_bc, n_rs, n_xp, n_xd, n_hi, n_lo = (
        sem("n_" + s) for s in "sq acc ss v r dg bc rs xp xd hi lo".split())
    q_done, q_act, q_dve = sem("q_done"), sem("q_act"), sem("q_dve")
    c_row, c_bc, c_pos, c_post, c_dve, c_trig, c_pool, c_inv = (
        sem("c_" + s) for s in "row bc pos post dve trig pool inv".split())
    f_sq, f_red, f_v, f_g, f_rr, f_qn, f_rot, f_ru = (sem("f_" + s) for s in "sq red v g rr qn rot ru".split())
    qs_hi, qs_ready, r_done, r_act, r_dve = (sem(s) for s in "qs_hi qs_ready r_done r_act r_dve".split())
    a_sc, a_ttr, a_nm, a_exp, a_den, a_p, a_pt, a_pt_act, a_pt_dve, a_pv, o_hi, o_lo = (
        sem(s) for s in "a_sc a_ttr a_nm a_exp a_den a_p a_pt a_pt_act a_pt_dve a_pv o_hi o_lo".split())
    g_done, u_done, silu_done, mul_done, a_hi, a_ready = (
        sem(s) for s in "g_done u_done silu_done mul_done a_hi a_ready".split())
    b_done, c_done, bc_copied, z_halo, z_done, y_done = (
        sem(s) for s in "b_done c_done bc_copied z_halo z_done y_done".split())
    d_done, add_done = sem("d_done"), sem("add_done")
    t_done, t_act, t_dve, s_out = sem("t_done"), sem("t_act"), sem("t_dve"), sem("s_out")

    c_mask0, c_mask, y_step = sem("c_mask0"), sem("c_mask"), sem("y_step")

    def angle(i):
        return ANG[:, 0, i, :].rearrange("p (b f) -> p b f", b=NBLK)

    def half(h):
        return slice(h * HALF, (h + 1) * HALF)

    def blk(b):
        return slice(b * P, (b + 1) * P)

    w_qkv, w_o = t["a_w_qkv"][0], t["a_w_o"][0]
    w_gu, w_dn = t["f_w_gate_up"], t["f_w_down"]
    w_in, w_out = t["b_w_in"][0], t["b_w_out"][0]
    x_dram, out_dram = t["x"][0], out[0]

    def sync_program(sp):
        def load(ph, c, j, src, cols=None):
            p = ph.piece(c, j)
            if not isinstance(p, int) or p >= AHEAD:
                sp.wait_ge(w_split, p + (1 - AHEAD))
            dst = STG[:, ph.stage(j), :]
            if cols:
                dst = dst.rearrange("p (k n) -> p k n", n=cols)
            sp.dma_start(dst, src).then_inc(stg[ph.stage(j)], 16)

        def columns(w, at, n):
            return w[:, bass.ds(at, n)].rearrange("(k p) n -> p k n", p=P)

        def load_q(c, j):
            rows = w_qkv[j * 2 * P:(j + 1) * 2 * P, c * HALF:(c + 1) * HALF]
            load(PH_Q, c, j, rows.rearrange("(k p) n -> p k n", p=P), HALF)

        sp.dma_start(GRAW[0:2 * KT, :], t["mix_norm"].rearrange("l (k p) -> (l k) p", p=P)).then_inc(s_gain, 16)
        sp.dma_start(GRAW[G_FFN:G_CONV, :], t["ffn_norm"].rearrange("l (k p) -> (l k) p", p=P)).then_inc(s_gain, 16)
        sp.dma_start(GRAW[G_CONV:G_ROWS, :], t["b_conv_w"][0].rearrange("l (k p) -> (l k) p", p=P)).then_inc(s_gain, 16)
        for b in range(NBLK):
            sp.dma_start(XN[:, b, :], x_dram[blk(b), :]).then_inc(s_x[b], 16)
            if b == HB - 1:
                for j in range(AHEAD):
                    load_q(0, j)
        for n in range(AHEAD, Q_PIECES):
            load_q(n // 4, n % 4)
            if n == AHEAD:
                sp.wait_ge(n_lo, 2 * KT)
                sp.dma_start(ROWS[0:1, 0:HD], t["a_q_norm"]).then_inc(s_row, 16)
                sp.dma_start(ROWS[0:1, HD:2 * HD], t["a_k_norm"]).then_inc(s_row, 16)
                sp.dma_start(ROWS[0:1, 2 * HD:2 * HD + HQ], t["a_sinks"]).then_inc(s_row, 16)
                sp.dma_start(POSI[0:NBLK, :], t["positions"][0].rearrange("(b p) -> b p", p=P)).then_inc(s_pos, 16)
        sp.wait_ge(o_lo, NBLK * HKV)
        for n in range(O_PIECES):
            load(PH_O, n // 4, n % 4, w_o[n * P:(n + 1) * P, :])

        def load_ffn(l):
            with sp.Fori(0, F_CHUNKS) as c:
                for j in range(2):
                    load(PH_F[l], c, 2 * j, columns(w_gu[l], c * (2 * P) + j * P, P), P)
                    load(PH_F[l], c, 2 * j + 1, columns(w_gu[l], c * (2 * P) + (FF + j * P), P), P)
                for j in range(2):
                    load(PH_F[l], c, 4 + j, w_dn[l][bass.ds(c * (2 * P) + j * P, P), :])

        load_ffn(0)
        with sp.Fori(0, C_CHUNKS) as c:
            for j in range(2):
                for i in range(3):
                    load(PH_C, c, 3 * j + i, columns(w_in, c * (2 * P) + (i * D + j * P), P), P)
            for j in range(2):
                load(PH_C, c, 6 + j, w_out[bass.ds(c * (2 * P) + j * P, P), :])
        load_ffn(1)
        for b in range(NBLK):
            sp.wait_ge(t_act, b + 1)
            sp.wait_ge(t_dve, b + 1)
            sp.dma_start(out_dram[blk(b), :], OUTB[:, b, :]).then_inc(s_out, 16)
        sp.wait_ge(s_out, 16 * NBLK)

    def split_hi(act, ph, c, j):
        p = ph.piece(c, j)
        act.wait_ge(stg[ph.stage(j)], ph.arrival(c, j))
        if not isinstance(p, int) or p >= 4:
            act.wait_ge(w_used, p - 3)
        nc.scalar.activation(WR[:, ph.slot(j), 0, :], STG[:, ph.stage(j), :], ACT.Copy).then_inc(w_hi, 1)

    def split_lo(dve, ph, c, j):
        dve.wait_ge(w_hi, ph.piece(c, j) + 1)
        nc.vector.tensor_tensor(WR[:, ph.slot(j), 1, :], STG[:, ph.stage(j), :],
                                WR[:, ph.slot(j), 0, :].bitcast(F32), ALU.subtract).then_inc(w_split, 1)

    def gain(n, k):
        at = (G_FFN if n % 2 else G_MIX) + (n // 2) * KT + k
        return GT[:, at:at + 1]

    def norm_square(act, n, h, m):
        i = 2 * n + h
        if m == 0:
            if i:
                act.wait_ge(n_ss, i)
            nc.scalar.activation(ACC[:], X[:, m, half(h)], ACT.Square).then_inc(n_sq, 1)
        else:
            if m > 2:
                act.wait_ge(n_acc, 7 * i + m - 2)
            nc.scalar.activation(SQ[:, m % 2, :], X[:, m, half(h)], ACT.Square).then_inc(n_sq, 1)

    def norm_accumulate(pool, n, h):
        i = 2 * n + h
        for m in range(1, KT):
            pool.wait_ge(n_sq, KT * i + m + 1)
            if m > 1:
                pool.wait_ge(n_acc, 7 * i + m - 1)
            nc.gpsimd.tensor_tensor(ACC[:], ACC[:], SQ[:, m % 2, :], ALU.add).then_inc(n_acc, 1)

    def norm_sum(pe, n, h):
        i = 2 * n + h
        pe.wait_ge(n_acc, 7 * (i + 1))
        for j in range(HB):
            mm = nc.tensor.matmul(PS[:, 6, j:j + 1], ACC[:, blk(j)], ONE[:, 0:1], start=True, stop=True)
        mm.then_inc(n_ss, 1)

    def norm_mean(dve, n, h):
        i = 2 * n + h
        dve.wait_ge(n_ss, i + 1)
        nc.vector.tensor_scalar(NS[:, 0:4], PS[:, 6, 0:4], 1.0 / D, EPS, ALU.mult, ALU.add).then_inc(n_v, 1)

    def norm_root(pool, n, h):
        i = 2 * n + h
        pool.wait_ge(n_v, i + 1)
        nc.gpsimd.tensor_tensor(NS[:, 4:8], NS[:, 0:4], NS[:, 8:12], ALU.pow).then_inc(n_r, 1)

    def norm_diagonal(dve, n, h):
        i = 2 * n + h
        dve.wait_ge(n_r, i + 1)
        for j in range(HB):
            v = nc.vector.tensor_scalar(DG[:, blk(j)], IDN[:], NS[:, 4 + j:5 + j], None, ALU.mult)
        v.then_inc(n_dg, 1)

    def norm_spread(pe, n, h):
        pe.wait_ge(n_dg, 2 * n + h + 1)
        nc.tensor.matmul(PS[:, 7, :], ONE[:], DG[:], start=True, stop=True).then_inc(n_bc, 1)

    def norm_take(act, n, h):
        act.wait_ge(n_bc, 2 * n + h + 1)
        nc.scalar.activation(RS[:], PS[:, 7, :], ACT.Copy).then_inc(n_rs, 1)

    def norm_scale(eng, ns, n, h, k):
        i = 2 * n + h
        if k < 2:
            eng.wait_ge(n_rs, i + 1)
        if KT * i + k >= 2:
            eng.wait_ge(n_lo, KT * i + k - 1)
        ns.tensor_tensor(XR[:, k % 2, :], X[:, k, half(h)], RS[:], ALU.mult).then_inc(n_xp if k % 2 else n_xd, 1)

    def norm_hi(act, n, h, k):
        i = 2 * n + h
        act.wait_ge(n_xp if k % 2 else n_xd, 4 * i + k // 2 + 1)
        nc.scalar.activation(H[:, 0, k, half(h)], XR[:, k % 2, :], ACT.Copy, scale=gain(n, k)).then_inc(n_hi, 1)

    def norm_lo(dve, n, h, k):
        dve.wait_ge(n_hi, KT * (2 * n + h) + k + 1)
        nc.vector.scalar_tensor_tensor(H[:, 1, k, half(h)], XR[:, k % 2, :], gain(n, k),
                                       H[:, 0, k, half(h)].bitcast(F32), ALU.mult, ALU.subtract).then_inc(n_lo, 1)

    def norm_pool(pool, n, h):
        norm_accumulate(pool, n, h)
        norm_root(pool, n, h)
        for k in range(1, KT, 2):
            norm_scale(pool, nc.gpsimd, n, h, k)

    def norm_act_split(act, n, h):
        norm_take(act, n, h)
        for k in range(KT):
            norm_hi(act, n, h, k)

    def norm_dve_split(dve, n, h, ks=range(KT)):
        for k in ks:
            if k == 0:
                norm_scale(dve, nc.vector, n, h, 0)
            if k % 2 == 1 and k + 1 < KT:
                norm_scale(dve, nc.vector, n, h, k + 1)
            norm_lo(dve, n, h, k)

    PASSES = ((0, 0), (0, 1), (1, 0))

    def tensor_program(pe):
        pe.wait_ge(s_idn, 1)
        pe.wait_ge(s_one, 1)
        pe.wait_ge(s_gain, 48)
        nc.tensor.transpose(PS[:, 7, 0:G_ROWS], GRAW[0:G_ROWS, :], IDN[0:G_ROWS, 0:G_ROWS]).then_inc(s_gt_ps, 1)

        def transpose_x(b):
            pe.wait_ge(s_x[b], 16)
            for q in range(2):
                i = 2 * b + q
                if i >= 4:
                    pe.wait_ge(x_dve if q else x_act, i // 2 - 1)
                for j in range(4):
                    mm = nc.tensor.transpose(PS[:, i % 4, blk(j)], XN[:, b, blk(4 * q + j)], IDN[:])
                mm.then_inc(x_tr, 1)

        for b in range(HB):
            transpose_x(b)
        norm_sum(pe, 0, 0)
        norm_spread(pe, 0, 0)
        for b in range(HB, NBLK):
            transpose_x(b)
        pe.wait_ge(x_act, NBLK)
        pe.wait_ge(x_dve, NBLK)

        def qkv_product(c, kp, b, normed=None):
            for k in (2 * kp, 2 * kp + 1):
                if normed is not None:
                    pe.wait_ge(n_lo, normed + k + 1)
                for w, a in PASSES:
                    mm = nc.tensor.matmul(
                        PS[:, b, :], H[:, a, k, blk(b)],
                        WR[:, PH_Q.slot(kp), w, (k % 2) * HALF:(k % 2 + 1) * HALF],
                        start=(k == 0 and (w, a) == (0, 0)), stop=(k == KT - 1 and (w, a) == (1, 0)))
            if b == NBLK - 1:
                mm.then_inc(w_used, 1)
            elif kp == 3:
                mm.then_inc(q_done, 1)

        for h in range(2):
            for kp in range(4):
                if h == 0:
                    pe.wait_ge(w_split, PH_Q.piece(0, kp) + 1)
                for b in range(h * HB, (h + 1) * HB):
                    qkv_product(0, kp, b, normed=KT * h if b % HB == 0 else None)
                if h == 0 and kp == 0:
                    norm_sum(pe, 0, 1)
                if h == 0 and kp == 1:
                    norm_spread(pe, 0, 1)
        with pe.Fori(1, QKVW // HALF) as c:
            for kp in range(4):
                pe.wait_ge(w_split, PH_Q.piece(c, kp) + 1)
                for b in range(NBLK):
                    if kp == 0:
                        pe.wait_ge(q_dve if b % 2 else q_act, c * 4 + (b // 2 - 3))
                    qkv_product(c, kp, b)

        pe.wait_ge(q_act, 12)
        pe.wait_ge(q_dve, 12)
        pe.wait_ge(s_row, 48)
        nc.tensor.matmul(PS[:, 7, 0:2 * HD + HQ], ONE[0:1, :], ROWS[0:1, :], start=True, stop=True).then_inc(c_bc, 1)
        pe.wait_ge(c_pos, 1)
        nc.tensor.transpose(PS[:, 6, 0:NBLK], POSF[0:NBLK, :], IDN[0:NBLK, 0:NBLK]).then_inc(c_post, 1)
        pe.wait_ge(c_pool, 1)
        pe.wait_ge(c_dve, 2)

        def round_trip(b, r):
            i = 6 * b + r
            pe.wait_ge(qs_ready, 5 * b + min(r, 4) + 1)
            if i:
                pe.wait_ge(r_act if r % 2 else r_dve, 3 * b + r // 2 + (1 if r % 2 else 0))
            for j in range(4):
                mm = nc.tensor.transpose(PS[:, 0, blk(j)], QS[:, 4 * r + j, :].bitcast(F32), IDN[:])
            mm.then_inc(r_done, 1)

        def scores(n):
            b, g = n // HKV, n % HKV
            width = P if b == 0 else 2 * P
            at = 0 if b else 0
            if g % 2:
                pe.wait_ge(r_dve, 3 * b + g // 2 + 1)
            else:
                pe.wait_ge(r_act, 3 * b + g // 2 + 1)
            if g == 0:
                pe.wait_ge(r_act, 3 * b + 3)
                pe.wait_ge(r_dve, 3 * b + 3)
            if n >= 2:
                pe.wait_ge(a_ttr, 4 * (n - 1))
            for j in range(GRP):
                dst = PS[:, 1 + 2 * (n % 2) + j // 2, (j % 2) * 2 * P:(j % 2) * 2 * P + width]
                for part in range(2):
                    k = KTT[:, part, g, :, :].rearrange("p s n -> p (s n)")[:, at:at + width]
                    mm = nc.tensor.matmul(dst, QT[:, GRP * g + j, :], k, start=(part == 0), stop=(part == 1))
            mm.then_inc(a_sc, 1)

        def slots(b):
            return (0,) if b == 0 else (0, 1)

        def probs_transposed(n):
            b = n // HKV
            pe.wait_ge(a_p, n + 1)
            for s in slots(b):
                if s == 0 and n:
                    pe.wait_ge(a_pt_act, n)
                if s == 1 and n > HKV:
                    pe.wait_ge(a_pt_dve, n - HKV)
                for i, j in enumerate((0, 2, 1, 3)):
                    mm = nc.tensor.transpose(PS[:, 5 + s, blk(i)], PR[:, n % 2, j, blk(s)], IDN[:])
                mm.then_inc(a_pt, 1)

        def values(n):
            b, g = n // HKV, n % HKV
            pe.wait_ge(a_pt_act, n + 1)
            if b:
                pe.wait_ge(a_pt_dve, n - HKV + 1)
            if n:
                pe.wait_ge(o_lo, n)
            for s in slots(b):
                of = b if s == b % 2 else b - 1
                v = QKV[:, of, QKW + HD * g:QKW + HD * (g + 1)]
                for odd in range(2):
                    mm = nc.tensor.matmul(PS[HD * odd:HD * (odd + 1), 7, 0:2 * P], v,
                                          PT[:, n % 2, s, 2 * P * odd:2 * P * (odd + 1)],
                                          start=(s == 0), stop=(s == slots(b)[-1]))
            mm.then_inc(a_pv, 1)

        n_groups = NBLK * HKV
        for r in range(6):
            round_trip(0, r)
        for n in range(n_groups + 2):
            b, g = n // HKV, n % HKV
            if n < n_groups:
                scores(n)
                if b + 1 < NBLK:
                    round_trip(b + 1, g)
            if 1 <= n <= n_groups:
                probs_transposed(n - 1)
            if g == HKV - 1 and b + 1 < NBLK:
                round_trip(b + 1, 4)
            if n >= 2:
                values(n - 2)
            if g == HKV - 1 and b + 1 < NBLK:
                round_trip(b + 1, 5)

        def add_product(ph, c, j0, d0, h, m, operand):
            i = HB * 2 * h + m
            d = c * 16 + (d0 + i)
            if not (isinstance(d, int) and d < 2):
                pe.wait_ge(add_done, d - 1)
            for j in range(2):
                for w, a in PASSES:
                    mm = nc.tensor.matmul(PS[:, 4 + i % 2, :], WR[:, ph.slot(j0 + j), w, blk(m)],
                                          operand(j, a, h), start=(j == 0 and (w, a) == (0, 0)),
                                          stop=(j == 1 and (w, a) == (1, 0)))
            if i == 15:
                mm.then_inc(w_used, 2)
            else:
                mm.then_inc(d_done, 1)

        def inner(j, a, h):
            return A[:, j, a, half(h)]

        def add_products(ph, c, j0, d0, tiles, norm=None):
            pe.wait_ge(w_split, ph.piece(c, j0 + 1) + 1)
            for h in range(2):
                pe.wait_ge(a_ready, c * 4 + (2 * tiles + 3 + h))
                for m in range(KT):
                    add_product(ph, c, j0, d0, h, m, inner)
                    if norm is not None and h == 1 and m == 3:
                        norm_sum(pe, norm, 0)
                    if norm is not None and h == 1 and m == 6:
                        norm_spread(pe, norm, 0)

        pe.wait_ge(o_lo, n_groups)
        for c in range(4):
            pe.wait_ge(w_split, PH_O.piece(0, 2 * c + 1) + 1)
            for h in range(2):
                for m in range(KT):
                    add_product(PH_O, 0, 2 * c, D_O + 16 * c, h, m, lambda j, a, h: H[:, a, 2 * c + j, half(h)])
                    if c == 3 and h == 1 and m == 3:
                        norm_sum(pe, 1, 0)
                    if c == 3 and h == 1 and m == 6:
                        norm_spread(pe, 1, 0)

        def product(ph, c, j, h, bank, done, norm=None):
            for k in range(KT):
                if norm is not None:
                    pe.wait_ge(n_lo, KT * (2 * norm + h) + k + 1)
                for w, a in PASSES:
                    mm = nc.tensor.matmul(PS[:, bank, :], WR[:, ph.slot(j), w, blk(k)], H[:, a, k, half(h)],
                                          start=(k == 0 and (w, a) == (0, 0)), stop=(k == KT - 1 and (w, a) == (1, 0)))
            mm.then_inc(*((done, 1) if h == 0 else (w_used, 1)))

        def gate_up(l, c, norm=None):
            ph = PH_F[l]
            for j in range(2):
                order = [(u, h) for u in range(2) for h in range(2)]
                first = norm is not None and j == 0
                if first:
                    order = [(u, h) for h in range(2) for u in range(2)]
                for u, h in order:
                    if h == 0:
                        pe.wait_ge(w_split, ph.piece(c, 2 * j + u) + 1)
                    tile = c * 2 + (T_F[l] + j)
                    if not isinstance(tile, int) or tile:
                        pe.wait_ge(mul_done if u else silu_done, c * 4 + (2 * (T_F[l] + j) + h - 1))
                    product(ph, c, 2 * j + u, h, 2 * u + h, u_done if u else g_done, norm if first and u == 0 else None)
                    if first and (u, h) == (0, 0):
                        norm_sum(pe, norm, 1)
                    if first and (u, h) == (1, 0):
                        norm_spread(pe, norm, 1)

        def ffn(l, norm, last_norm):
            gate_up(l, 0, norm)
            add_products(PH_F[l], 0, 4, D_F[l], A_F[l])
            with pe.Fori(1, F_CHUNKS - 1) as c:
                gate_up(l, c)
                add_products(PH_F[l], c, 4, D_F[l], A_F[l])
            gate_up(l, F_CHUNKS - 1)
            add_products(PH_F[l], F_CHUNKS - 1, 4, D_F[l], A_F[l], last_norm)

        ffn(0, 1, 2)

        def gated(c, norm=None):
            for j in range(2):
                order = [(i, h) for i in range(3) for h in range(2)]
                first = norm is not None and j == 0
                if first:
                    order = [(i, h) for h in range(2) for i in range(3)]
                for i, h in order:
                    if h == 0:
                        pe.wait_ge(w_split, PH_C.piece(c, 3 * j + i) + 1)
                    start = not isinstance(c, int) or c > 0 or j > 0
                    if i == 2:
                        pe.wait_ge(bc_copied, c * 8 + (4 * j + h + 1))
                    elif i == 1 and start:
                        pe.wait_ge(bc_copied, c * 8 + (4 * j + h - 1))
                    elif start:
                        pe.wait_ge(z_done, c * 4 + (2 * j + h - 1))
                    product(PH_C, c, 3 * j + i, h, (0, 2, 0)[i] + h, (b_done, c_done, u_done)[i],
                            norm if first and i == 0 else None)
                    if first and (i, h) == (0, 0):
                        norm_sum(pe, norm, 1)
                    if first and (i, h) == (1, 0):
                        norm_spread(pe, norm, 1)

        gated(0, 2)
        add_products(PH_C, 0, 6, D_C, A_C)
        with pe.Fori(1, C_CHUNKS - 1) as c:
            gated(c)
            add_products(PH_C, c, 6, D_C, A_C)
        gated(C_CHUNKS - 1)
        add_products(PH_C, C_CHUNKS - 1, 6, D_C, A_C, 3)

        ffn(1, 3, None)

        for b in range(NBLK):
            if b % HB == 0:
                pe.wait_ge(add_done, D_F1 + 16 * F_CHUNKS - (8 if b == 0 else 0))
            for q in range(2):
                i = 2 * b + q
                if i >= 4:
                    pe.wait_ge(t_dve if q else t_act, b - 1)
                for j in range(4):
                    mm = nc.tensor.transpose(PS[:, i % 4, blk(j)], X[:, 4 * q + j, blk(b)], IDN[:])
                mm.then_inc(t_done, 1)

    def scalar_program(act):
        def take_x(b):
            act.wait_ge(x_tr, 2 * b + 1)
            nc.scalar.activation(X[:, 0:4, blk(b)], PS[:, (2 * b) % 4, :].rearrange("p (k n) -> p k n", n=P),
                                 ACT.Copy).then_inc(x_act, 1)

        for b in range(HB):
            take_x(b)
        act.wait_ge(x_act, HB)
        act.wait_ge(x_dve, HB)
        for m in range(KT):
            norm_square(act, 0, 0, m)
        for j in range(2):
            split_hi(act, PH_Q, 0, j)
        for b in range(HB, NBLK):
            take_x(b)
        act.wait_ge(s_gt_sb, 1)
        norm_act_split(act, 0, 0)
        split_hi(act, PH_Q, 0, 2)
        act.wait_ge(x_act, NBLK)
        act.wait_ge(x_dve, NBLK)
        for m in range(KT):
            norm_square(act, 0, 1, m)
        split_hi(act, PH_Q, 0, 3)
        norm_act_split(act, 0, 1)

        def take_qkv(c, b):
            act.wait_ge(q_done, c * 7 + (b + 1))
            nc.scalar.activation(QKV[:, b, bass.ds(c * HALF, HALF)], PS[:, b, :], ACT.Copy).then_inc(q_act, 1)

        for c in range(QKVW // HALF):
            for j in range(4):
                if 4 * c + j > 0 and 4 * c + j + 3 < Q_PIECES:
                    split_hi(act, PH_Q, c, j + 3)
            for b in range(0, NBLK, 2):
                take_qkv(c, b)

        act.wait_ge(c_bc, 1)
        nc.scalar.activation(GBC[:], PS[:, 7, 0:2 * HD + HQ], ACT.Copy).then_inc(c_pool, 1)
        act.wait_ge(c_dve, C_ANGLES)
        nc.scalar.activation(SIN[:, :, 0:ROT // 2], angle(0), ACT.Sin, scale=-1.0).then_inc(c_trig, 1)
        nc.scalar.activation(SIN[:, :, ROT // 2:ROT], angle(0), ACT.Sin).then_inc(c_trig, 1)
        nc.scalar.activation(COS[:, :, 0:ROT // 2], angle(1), ACT.Sin).then_inc(c_trig, 1)
        nc.scalar.activation(COS[:, :, ROT // 2:ROT], angle(1), ACT.Sin).then_inc(c_trig, 1)

        def square_heads(b):
            if b:
                act.wait_ge(f_red, b)
            act.wait_ge(c_trig, 4)
            nc.scalar.activation(ASQ[:], QKV[:, b, 0:QKW], ACT.Square).then_inc(f_sq, 1)

        def heads_hi(b, g):
            act.wait_ge(f_rot, b + 1)
            if g < HKV:
                if b:
                    act.wait_ge(r_done, 6 * (b - 1) + g + 1)
                src = QKV[:, b, HD * GRP * g:HD * GRP * (g + 1)].rearrange("p (j n) -> p j n", n=HD)
                nc.scalar.activation(QS[:, GRP * g:GRP * (g + 1), 0:HD], src, ACT.Copy).then_inc(qs_hi, 1)
            else:
                if b:
                    act.wait_ge(r_done, 6 * b)
                src = QKV[:, b, HD * HQ:QKW].rearrange("p (j n) -> p j n", n=HD)
                src = src.unsqueeze(2).broadcast_to([P, HKV, 2, HD])
                dst = QS[:, HQ:HQ + HKV, :].rearrange("p j (s n) -> p j s n", s=2)
                nc.scalar.activation(dst, src, ACT.Copy).then_inc(qs_hi, 1)

        def take_round(b, r):
            act.wait_ge(r_done, 6 * b + r + 1)
            dst = QT[:, 4 * r:4 * r + 4, :] if r < 4 else KTT[:, 0, :, b % 2, :]
            nc.scalar.activation(dst, PS[:, 0, :].rearrange("p (j n) -> p j n", n=P), ACT.Copy).then_inc(r_act, 1)

        def exponentials(n):
            w = P if n < HKV else 2 * P
            act.wait_ge(a_nm, 2 * (n + 1))
            for j in range(GRP):
                nc.scalar.activation(PR[:, n % 2, j, 0:w], PR[:, n % 2, j, 0:w], ACT.Exp,
                                     bias=STAT[:, n % 2, 1, j:j + 1], accum_out=STAT[:, n % 2, 3, j:j + 1])
            nc.scalar.activation(STAT[:, n % 2, 4, :], STAT[:, n % 2, 2, :], ACT.Exp).then_inc(a_exp, 1)

        def take_probs(n):
            act.wait_ge(a_pt, pt_count(n, 0))
            if n >= 2:
                act.wait_ge(a_pv, n - 1)
            nc.scalar.activation(PT[:, n % 2, 0, :], PS[:, 5, :], ACT.Copy).then_inc(a_pt_act, 1)

        def out_hi(n):
            b, g = n // HKV, n % HKV
            act.wait_ge(a_pv, n + 1)
            nc.scalar.activation(H[:, 0, 2 * g:2 * g + 2, blk(b)], PS[:, 7, 0:2 * P].rearrange("p (k n) -> p k n", n=P),
                                 ACT.Copy).then_inc(o_hi, 1)

        for b in range(2):
            square_heads(b)
        for g in range(HKV + 1):
            heads_hi(0, g)
        for r in range(0, 6, 2):
            take_round(0, r)
        heads_hi(1, 0)
        n_groups = NBLK * HKV
        for n in range(n_groups + 2):
            b, g = n // HKV, n % HKV
            if 1 <= n <= n_groups:
                take_probs(n - 1)
            if n < n_groups:
                if b + 1 < NBLK and g % 2 == 0:
                    take_round(b + 1, g)
                exponentials(n)
                if g == 1 and b + 2 < NBLK:
                    square_heads(b + 2)
                if g < HKV - 1 and b + 1 < NBLK:
                    heads_hi(b + 1, g + 1)
                if g == HKV - 1:
                    if b + 1 < NBLK:
                        heads_hi(b + 1, HKV)
                        take_round(b + 1, 4)
                    if b + 2 < NBLK:
                        heads_hi(b + 2, 0)
            if n >= 2:
                out_hi(n - 2)

        act.wait_ge(o_lo, n_groups)
        for j in range(AHEAD):
            split_hi(act, PH_O, 0, j)

        def squares(norm, h, d0):
            for m in range(KT):
                act.wait_ge(add_done, d0 + KT * h + m + 1)
                norm_square(act, norm, h, m)

        for c in range(4):
            split_ahead(split_hi, act, PH_O, 0, 2 * c)
            if c == 3:
                squares(1, 0, D_O + 48)
                norm_act_split(act, 1, 0)
            if c < 3:
                split_ahead(split_hi, act, PH_O, 0, 2 * c + 1)
        squares(1, 1, D_O + 48)
        split_ahead(split_hi, act, PH_O, 0, 7)
        norm_act_split(act, 1, 1)

        def silu(l, c, j, h):
            i = c * 4 + (2 * (T_F[l] + j) + h)
            if h == 0:
                act.wait_ge(g_done, c * 2 + (T_F[l] + j + 1))
            else:
                act.wait_ge(w_used, PH_F[l].piece(c, 2 * j) + 1)
            if not isinstance(i, int) or i >= 2:
                act.wait_ge(mul_done, i - 1)
            nc.scalar.activation(SG[:, h, :], PS[:, h, :], ACT.Silu).then_inc(silu_done, 1)

        def inner_hi(c, j, h, wait, tiles):
            act.wait_ge(wait, c * 4 + (2 * j + h + 1))
            nc.scalar.activation(A[:, j, 0, half(h)], A32[:, h, :], ACT.Copy).then_inc(a_hi, 1)

        def inner_hi_of(c, j, h, done, first):
            act.wait_ge(done, c * 4 + (first + 2 * j + h + 1))
            nc.scalar.activation(A[:, j, 0, half(h)], A32[:, h, :], ACT.Copy).then_inc(a_hi, 1)

        def ffn_chunk(l, c, norm=None, ahead=True):
            ph = PH_F[l]
            for j in range(2):
                split_ahead(split_hi, act, ph, c, 2 * j)
                silu(l, c, j, 0)
                silu(l, c, j, 1)
                if ahead or j == 0:
                    split_ahead(split_hi, act, ph, c, 2 * j + 1)
                inner_hi_of(c, j, 0, mul_done, 2 * T_F[l])
                inner_hi_of(c, j, 1, mul_done, 2 * T_F[l])
            if ahead:
                split_ahead(split_hi, act, ph, c, 4)
            if norm is not None:
                d0 = D_F[l] + 16 * c
                squares(norm, 0, d0)
                norm_act_split(act, norm, 0)
                squares(norm, 1, d0)
            if ahead:
                split_ahead(split_hi, act, ph, c, 5)
            if norm is not None:
                norm_act_split(act, norm, 1)

        ffn_chunk(0, 0)
        with act.Fori(1, F_CHUNKS - 1) as c:
            ffn_chunk(0, c)
        ffn_chunk(0, F_CHUNKS - 1, norm=2)

        def copy_gate(c, j, i, h):
            if h == 0:
                act.wait_ge((b_done, c_done)[i], c * 2 + (j + 1))
            else:
                act.wait_ge(w_used, PH_C.piece(c, 3 * j + i) + 1)
            act.wait_ge(a_ready, c * 4 + (2 * (A_C + j) + h - 1))
            nc.scalar.activation((BG, CG)[i][:, half(h)], PS[:, 2 * i + h, :], ACT.Copy).then_inc(bc_copied, 1)

        def conv_chunk(c, norm=None):
            for j in range(2):
                for i in range(2):
                    split_ahead(split_hi, act, PH_C, c, 3 * j + i)
                    copy_gate(c, j, i, 0)
                    copy_gate(c, j, i, 1)
                split_ahead(split_hi, act, PH_C, c, 3 * j + 2)
                inner_hi_of(c, j, 0, y_done, 0)
                inner_hi_of(c, j, 1, y_done, 0)
            split_ahead(split_hi, act, PH_C, c, 6)
            if norm is not None:
                d0 = D_C + 16 * c
                squares(norm, 0, d0)
                norm_act_split(act, norm, 0)
                squares(norm, 1, d0)
            split_ahead(split_hi, act, PH_C, c, 7)
            if norm is not None:
                norm_act_split(act, norm, 1)

        with act.Fori(0, C_CHUNKS - 1) as c:
            conv_chunk(c)
        conv_chunk(C_CHUNKS - 1, norm=3)
        with act.Fori(0, F_CHUNKS - 1) as c:
            ffn_chunk(1, c)
        ffn_chunk(1, F_CHUNKS - 1, ahead=False)
        for b in range(NBLK):
            act.wait_ge(t_done, 2 * b + 1)
            nc.scalar.activation(OUTB[:, b, 0:HALF], PS[:, (2 * b) % 4, :], ACT.Copy).then_inc(t_act, 1)

    def vector_program(dve):
        nc.vector.memset(ONE[:], 1.0).then_inc(s_one, 1)
        dve.wait_ge(s_gt_ps, 1)
        nc.vector.tensor_copy(GT[:], PS[:, 7, 0:G_ROWS]).then_inc(s_gt_sb, 1)

        def take_x(b):
            dve.wait_ge(x_tr, 2 * b + 2)
            nc.vector.tensor_copy(X[:, 4:8, blk(b)],
                                  PS[:, (2 * b + 1) % 4, :].rearrange("p (k n) -> p k n", n=P)).then_inc(x_dve, 1)

        for b in range(HB):
            take_x(b)
        for j in range(2):
            split_lo(dve, PH_Q, 0, j)
        dve.wait_ge(s_gt_sb, 1)
        norm_mean(dve, 0, 0)
        norm_diagonal(dve, 0, 0)
        for b in range(HB, NBLK):
            take_x(b)
        norm_dve_split(dve, 0, 0)
        split_lo(dve, PH_Q, 0, 2)
        norm_mean(dve, 0, 1)
        norm_diagonal(dve, 0, 1)
        split_lo(dve, PH_Q, 0, 3)
        norm_dve_split(dve, 0, 1)

        def take_qkv(c, b):
            if b == NBLK - 1:
                dve.wait_ge(w_used, 4 * c + 4)
            else:
                dve.wait_ge(q_done, c * 7 + (b + 1))
            nc.vector.tensor_copy(QKV[:, b, bass.ds(c * HALF, HALF)], PS[:, b, :]).then_inc(q_dve, 1)

        for c in range(QKVW // HALF):
            for j in range(4):
                if 4 * c + j > 0 and 4 * c + j + 3 < Q_PIECES:
                    split_lo(dve, PH_Q, c, j + 3)
            for b in range(1, NBLK, 2):
                take_qkv(c, b)

        dve.wait_ge(s_pos, 16)
        nc.vector.tensor_copy(POSF[0:NBLK, :], POSI[0:NBLK, :]).then_inc(c_pos, 1)
        for f in range(ROT // 2):
            nc.vector.memset(INVF[:, f:f + 1], float(INV_FREQ[f])).then_inc(c_inv, 1)
        dve.wait_ge(c_post, 1)
        count = [0]

        def step(v):
            v.then_inc(c_dve, 1)
            count[0] += 1
            dve.wait_ge(c_dve, count[0])

        def tile(i):
            return ANG[:, i, :, :]

        step(nc.vector.tensor_copy(POST[:], PS[:, 6, 0:NBLK]))
        dve.wait_ge(c_inv, ROT // 2)
        pos = POST[:].unsqueeze(2).broadcast_to([P, NBLK, ROT // 2])
        inv = INVF[:].unsqueeze(1).broadcast_to([P, NBLK, ROT // 2])
        for i in range(2):
            step(nc.vector.tensor_tensor(angle(i), pos, inv, ALU.mult))
        for i in range(2):
            step(nc.vector.tensor_scalar(ANG[:, 1, i, :], ANG[:, 0, i, :], 1 / (2 * np.pi), 0.25 * i, ALU.mult, ALU.add))
        step(nc.vector.tensor_scalar(tile(1), tile(1), ROUND, None, ALU.add))
        step(nc.vector.tensor_scalar(tile(1), tile(1), -ROUND, None, ALU.add))
        for part in TWO_PI:
            step(nc.vector.scalar_tensor_tensor(tile(0), tile(1), -float(part), tile(0), ALU.mult, ALU.add))
        step(nc.vector.tensor_scalar(ANG[:, 0, 1, :], ANG[:, 0, 1, :], float(np.float32(np.pi / 2)), None, ALU.add))
        step(nc.vector.tensor_scalar(tile(0), tile(0), PI_IN, -PI_IN, ALU.min, ALU.max))
        assert count[0] == C_ANGLES
        dve.wait_ge(c_trig, 4)

        def sum_heads(b):
            dve.wait_ge(f_sq, b + 1)
            nc.vector.tensor_reduce(SSQ[:, b, :], ASQ[:].rearrange("p (j n) -> p j n", n=HD), AX_X, ALU.add).then_inc(f_red, 1)
            dve.wait_ge(f_red, b + 1)
            nc.vector.tensor_scalar(SSQ[:, b, :], SSQ[:, b, :], 1.0 / HD, EPS, ALU.mult, ALU.add).then_inc(f_v, 1)

        def scale_heads(b):
            dve.wait_ge(f_rr, b + 1)
            dve.wait_ge(f_g, 2 * b + 2)
            x = QKV[:, b, 0:QKW].rearrange("p (j n) -> p j n", n=HD)
            nc.vector.tensor_tensor(x, x, RR[:, b, :].unsqueeze(2).broadcast_to([P, NQK, HD]), ALU.mult).then_inc(f_qn, 1)

        def heads_lo(b, g):
            dve.wait_ge(qs_hi, 5 * b + g + 1)
            if g < HKV:
                src = QKV[:, b, HD * GRP * g:HD * GRP * (g + 1)].rearrange("p (j n) -> p j n", n=HD)
                s = slice(GRP * g, GRP * (g + 1))
                nc.vector.tensor_tensor(QS[:, s, HD:P], src, QS[:, s, 0:HD].bitcast(F32), ALU.subtract).then_inc(qs_ready, 1)
            else:
                src = QKV[:, b, HD * HQ:QKW].rearrange("p (j n) -> p j n", n=HD)
                src = src.unsqueeze(2).broadcast_to([P, HKV, 2, HD])
                hi = QS[:, HQ:HQ + HKV, :].rearrange("p j (s n) -> p j s n", s=2)
                lo = QS[:, HQ + HKV:HQ + 2 * HKV, :].rearrange("p j (s n) -> p j s n", s=2)
                nc.vector.tensor_tensor(lo, src, hi.bitcast(F32), ALU.subtract).then_inc(qs_ready, 1)

        def take_round(b, r):
            dve.wait_ge(r_done, 6 * b + r + 1)
            dst = QT[:, 4 * r:4 * r + 4, :] if r < 4 else KTT[:, 1, :, b % 2, :]
            nc.vector.tensor_copy(dst, PS[:, 0, :].rearrange("p (j n) -> p j n", n=P)).then_inc(r_dve, 1)

        def scores_masked(n):
            b, g = n // HKV, n % HKV
            w = P if b == 0 else 2 * P
            at = P if b % 2 == 0 else 0
            dve.wait_ge(a_sc, n + 1)
            if n >= 2:
                dve.wait_ge(a_pt, pt_count(n - 2, 1))
            for j in range(GRP):
                src = PS[:, 1 + 2 * (n % 2) + j // 2, (j % 2) * 2 * P:(j % 2) * 2 * P + w]
                h = 2 * HD + GRP * g + j
                nc.vector.tensor_tensor_reduce(
                    out=PR[:, n % 2, j, 0:w], in0=src, in1=MASK[:, at:at + w], scale=HD ** -0.5,
                    scalar=GBC[:, h:h + 1], op0=ALU.add, op1=ALU.max,
                    accum_out=STAT[:, n % 2, 0, j:j + 1]).then_inc(a_ttr, 1)
            dve.wait_ge(a_ttr, 4 * (n + 1))
            sink = GBC[:, 2 * HD + GRP * g:2 * HD + GRP * (g + 1)]
            nc.vector.tensor_scalar(STAT[:, n % 2, 1, :], STAT[:, n % 2, 0, :], -1.0, None, ALU.mult).then_inc(a_nm, 1)
            nc.vector.tensor_tensor(STAT[:, n % 2, 2, :], sink, STAT[:, n % 2, 0, :], ALU.subtract).then_inc(a_nm, 1)

        def probs(n):
            w = P if n < HKV else 2 * P
            dve.wait_ge(a_exp, n + 1)
            nc.vector.tensor_tensor(STAT[:, n % 2, 3, :], STAT[:, n % 2, 3, :], STAT[:, n % 2, 4, :], ALU.add).then_inc(a_den, 1)
            dve.wait_ge(a_den, 2 * n + 1)
            nc.vector.reciprocal(STAT[:, n % 2, 5, :], STAT[:, n % 2, 3, :]).then_inc(a_den, 1)
            dve.wait_ge(a_den, 2 * n + 2)
            for j in range(GRP):
                v = nc.vector.tensor_scalar(PR[:, n % 2, j, 0:w], PR[:, n % 2, j, 0:w], STAT[:, n % 2, 5, j:j + 1],
                                            None, ALU.mult)
            v.then_inc(a_p, 1)

        def take_probs(n):
            if n < HKV:
                return
            dve.wait_ge(a_pt, pt_count(n, 1))
            if n >= 2:
                dve.wait_ge(a_pv, n - 1)
            nc.vector.tensor_copy(PT[:, n % 2, 1, :], PS[:, 6, :]).then_inc(a_pt_dve, 1)

        def out_lo(n):
            b, g = n // HKV, n % HKV
            dve.wait_ge(o_hi, n + 1)
            nc.vector.tensor_tensor(H[:, 1, 2 * g:2 * g + 2, blk(b)], PS[:, 7, 0:2 * P].rearrange("p (k n) -> p k n", n=P),
                                    H[:, 0, 2 * g:2 * g + 2, blk(b)].bitcast(F32), ALU.subtract).then_inc(o_lo, 1)

        dve.wait_ge(c_pool, 1)
        for b in range(2):
            sum_heads(b)
        scale_heads(0)
        for g in range(HKV + 1):
            heads_lo(0, g)
        for r in range(1, 6, 2):
            take_round(0, r)
        scale_heads(1)
        heads_lo(1, 0)
        dve.wait_ge(c_mask, 2)
        n_groups = NBLK * HKV
        for n in range(n_groups + 2):
            b, g = n // HKV, n % HKV
            if 1 <= n <= n_groups:
                probs(n - 1)
            if n < n_groups:
                scores_masked(n)
                if b + 1 < NBLK and g % 2 == 1:
                    take_round(b + 1, g)
            if 1 <= n <= n_groups:
                take_probs(n - 1)
            if n < n_groups:
                if g == 2 and b + 2 < NBLK:
                    sum_heads(b + 2)
                if g < HKV - 1 and b + 1 < NBLK:
                    heads_lo(b + 1, g + 1)
                if g == HKV - 1:
                    if b + 1 < NBLK:
                        heads_lo(b + 1, HKV)
                        take_round(b + 1, 5)
                    if b + 2 < NBLK:
                        scale_heads(b + 2)
                        heads_lo(b + 2, 0)
            if n >= 2:
                out_lo(n - 2)

        for j in range(AHEAD):
            split_lo(dve, PH_O, 0, j)

        def add(ph, c, last, d0, h, m):
            i = KT * h + m
            if i == 15:
                dve.wait_ge(w_used, ph.piece(c, last) + 1)
            else:
                dve.wait_ge(d_done, c * 15 + (d0 // 16 * 15 + i + 1))
            nc.vector.tensor_tensor(X[:, m, half(h)], X[:, m, half(h)], PS[:, 4 + i % 2, :], ALU.add).then_inc(add_done, 1)

        def adds(ph, c, last, d0, norm=None):
            for m in range(KT):
                add(ph, c, last, d0, 0, m)
            for m in range(KT):
                add(ph, c, last, d0, 1, m)
                if norm is None:
                    continue
                if m == 3:
                    norm_mean(dve, norm, 0)
                if m == 4:
                    norm_diagonal(dve, norm, 0)

        def last_norm(norm):
            norm_dve_split(dve, norm, 0)
            norm_mean(dve, norm, 1)
            norm_diagonal(dve, norm, 1)

        for c in range(4):
            split_ahead(split_lo, dve, PH_O, 0, 2 * c)
            adds(PH_O, 0, 2 * c + 1, D_O + 16 * c, norm=1 if c == 3 else None)
            if c == 3:
                last_norm(1)
            split_ahead(split_lo, dve, PH_O, 0, 2 * c + 1)
        norm_dve_split(dve, 1, 1)

        def inner_lo(c, j, h, tiles):
            dve.wait_ge(a_hi, c * 4 + (2 * (tiles + j) + h + 1))
            nc.vector.tensor_tensor(A[:, j, 1, half(h)], A32[:, h, :], A[:, j, 0, half(h)].bitcast(F32),
                                    ALU.subtract).then_inc(a_ready, 1)

        def multiply(l, c, j, h):
            i = c * 4 + (2 * (T_F[l] + j) + h)
            if h == 0:
                dve.wait_ge(u_done, c * 2 + (U_F[l] + j + 1))
            else:
                dve.wait_ge(w_used, PH_F[l].piece(c, 2 * j + 1) + 1)
            dve.wait_ge(silu_done, i + 1)
            first = c * 4 + (2 * (A_F[l] + j) + h)
            if not isinstance(first, int) or first >= 2:
                dve.wait_ge(a_ready, first - 1)
            nc.vector.tensor_tensor(A32[:, h, :], SG[:, h, :], PS[:, 2 + h, :], ALU.mult).then_inc(mul_done, 1)

        def ffn_chunk(l, c, norm=None, ahead=True):
            ph = PH_F[l]
            for j in range(2):
                split_ahead(split_lo, dve, ph, c, 2 * j)
                if ahead or j == 0:
                    split_ahead(split_lo, dve, ph, c, 2 * j + 1)
                multiply(l, c, j, 0)
                multiply(l, c, j, 1)
                inner_lo(c, j, 0, A_F[l])
                inner_lo(c, j, 1, A_F[l])
            if ahead:
                split_ahead(split_lo, dve, ph, c, 4)
            adds(ph, c, 5, D_F[l] + (0 if not isinstance(c, int) else 0), norm)
            if norm is not None:
                last_norm(norm)
            if ahead:
                split_ahead(split_lo, dve, ph, c, 5)
            if norm is not None:
                norm_dve_split(dve, norm, 1)

        ffn_chunk(0, 0)
        with dve.Fori(1, F_CHUNKS - 1) as c:
            ffn_chunk(0, c)
        ffn_chunk(0, F_CHUNKS - 1, norm=2)

        nc.vector.memset(ZC[:, 0:CW - 1], 0.0).then_inc(z_halo, 1)

        def tap(c, j, i):
            at = G_CONV + i * KT
            return GT[:, bass.ds(c * 2 + (at + j), 1)]

        def convolve(c, j, h):
            if h == 0:
                dve.wait_ge(u_done, c * 2 + (2 * F_CHUNKS + j + 1))
            else:
                dve.wait_ge(w_used, PH_C.piece(c, 3 * j + 2) + 1)
            n = c * 4 + (2 * j + h)
            dve.wait_ge(bc_copied, c * 8 + (4 * j + 2 + h + 1))
            if h == 0:
                dve.wait_ge(a_ready, c * 4 + 2 * (A_C + j))
            else:
                dve.wait_ge(y_done, n)
            nc.vector.tensor_tensor(ZC[:, CW - 1 + h * HALF:CW - 1 + (h + 1) * HALF], CG[:, half(h)],
                                    PS[:, h, :], ALU.mult).then_inc(z_done, 1)
            dve.wait_ge(z_done, n + 1)
            dve.wait_ge(z_halo, 1)
            z = [ZC[:, h * HALF + i:(h + 1) * HALF + i] for i in range(CW)]
            nc.vector.tensor_scalar(YC[:], z[0], tap(c, j, 0), None, ALU.mult).then_inc(y_step, 1)
            dve.wait_ge(y_step, c * 12 + (6 * j + 3 * h + 1))
            nc.vector.scalar_tensor_tensor(YC[:], z[1], tap(c, j, 1), YC[:], ALU.mult, ALU.add).then_inc(y_step, 1)
            dve.wait_ge(y_step, c * 12 + (6 * j + 3 * h + 2))
            nc.vector.scalar_tensor_tensor(YC[:], z[2], tap(c, j, 2), YC[:], ALU.mult, ALU.add).then_inc(y_step, 1)
            dve.wait_ge(y_step, c * 12 + (6 * j + 3 * h + 3))
            dve.wait_ge(a_ready, c * 4 + (2 * (A_C + j) + h - 1))
            nc.vector.tensor_tensor(A32[:, h, :], BG[:, half(h)], YC[:], ALU.mult).then_inc(y_done, 1)

        def conv_chunk(c, norm=None):
            for j in range(2):
                for i in range(3):
                    split_ahead(split_lo, dve, PH_C, c, 3 * j + i)
                convolve(c, j, 0)
                convolve(c, j, 1)
                inner_lo(c, j, 0, A_C)
                inner_lo(c, j, 1, A_C)
            split_ahead(split_lo, dve, PH_C, c, 6)
            adds(PH_C, c, 7, D_C, norm)
            if norm is not None:
                last_norm(norm)
            split_ahead(split_lo, dve, PH_C, c, 7)
            if norm is not None:
                norm_dve_split(dve, norm, 1)

        with dve.Fori(0, C_CHUNKS - 1) as c:
            conv_chunk(c)
        conv_chunk(C_CHUNKS - 1, norm=3)
        with dve.Fori(0, F_CHUNKS - 1) as c:
            ffn_chunk(1, c)
        ffn_chunk(1, F_CHUNKS - 1, ahead=False)
        for b in range(NBLK):
            dve.wait_ge(t_done, 2 * b + 2)
            nc.vector.tensor_copy(OUTB[:, b, HALF:D], PS[:, (2 * b + 1) % 4, :]).then_inc(t_dve, 1)

    def pool_program(pool):
        nc.gpsimd.memset(IDN[:], 0.0).then_inc(s_idn0, 1)
        pool.wait_ge(s_idn0, 1)
        nc.gpsimd.affine_select(out=IDN[:], in_=IDN[:], compare_op=ALU.not_equal, fill=1.0, base=0,
                                pattern=[[-1, P]], channel_multiplier=1).then_inc(s_idn, 1)
        nc.gpsimd.memset(NS[:, 8:12], -0.5).then_inc(s_half, 1)
        pool.wait_ge(s_half, 1)
        norm_pool(pool, 0, 0)
        norm_pool(pool, 0, 1)

        pool.wait_ge(n_lo, 2 * KT)
        nc.gpsimd.memset(MASK[:], 0.0).then_inc(c_mask0, 1)
        nc.gpsimd.memset(MH[:], -0.5).then_inc(c_mask0, 1)
        pool.wait_ge(c_mask0, 2)
        nc.gpsimd.affine_select(out=MASK[:, P:2 * P], in_=MASK[:, P:2 * P], compare_op=ALU.is_ge, fill=NEG, base=0,
                                pattern=[[-1, P]], channel_multiplier=1).then_inc(c_mask, 1)
        for at in (0, 2 * P):
            m = nc.gpsimd.affine_select(out=MASK[:, at:at + P], in_=MASK[:, at:at + P], compare_op=ALU.is_gt,
                                        fill=NEG, base=0, pattern=[[1, P]], channel_multiplier=-1)
        m.then_inc(c_mask, 1)

        def gains(b):
            pool.wait_ge(f_sq, b + 1)
            for lo, n, g in ((0, HQ, 0), (HQ * HD, HKV, HD)):
                x = QKV[:, b, lo:lo + n * HD].rearrange("p (j n) -> p j n", n=HD)
                nc.gpsimd.tensor_tensor(x, x, GBC[:, g:g + HD].unsqueeze(1).broadcast_to([P, n, HD]),
                                        ALU.mult).then_inc(f_g, 1)

        def roots(b):
            pool.wait_ge(f_v, b + 1)
            nc.gpsimd.tensor_tensor(RR[:, b, :], SSQ[:, b, :], MH[:], ALU.pow).then_inc(f_rr, 1)

        def rotate(b):
            pool.wait_ge(f_qn, b + 1)
            x = QKV[:, b, 0:QKW].rearrange("p (j n) -> p j n", n=HD)
            hr = ROT // 2
            cos = COS[:, b, :].unsqueeze(1).broadcast_to([P, NQK, ROT])
            sin = [SIN[:, b, i * hr:(i + 1) * hr].unsqueeze(1).broadcast_to([P, NQK, hr]) for i in range(2)]
            nc.gpsimd.tensor_tensor(RT[:], x[:, :, 0:ROT], cos, ALU.mult).then_inc(f_ru, 1)
            nc.gpsimd.tensor_tensor(RU[:, :, 0:hr], x[:, :, hr:ROT], sin[0], ALU.mult).then_inc(f_ru, 1)
            nc.gpsimd.tensor_tensor(RU[:, :, hr:ROT], x[:, :, 0:hr], sin[1], ALU.mult).then_inc(f_ru, 1)
            pool.wait_ge(f_ru, 3 * b + 3)
            nc.gpsimd.tensor_tensor(x[:, :, 0:ROT], RT[:], RU[:], ALU.add).then_inc(f_rot, 1)
            pool.wait_ge(f_rot, b + 1)

        pool.wait_ge(c_pool, 1)
        pool.wait_ge(c_trig, 4)
        pool.wait_ge(q_act, 12)
        pool.wait_ge(q_dve, 12)
        for b in range(NBLK):
            gains(b)
            roots(b)
            rotate(b)
        for n in range(1, 4):
            for h in range(2):
                norm_pool(pool, n, h)

    block = ctx.enter_context(nc.Block())
    block.sync(sync_program)
    block.gpsimd(pool_program)
    block.scalar(scalar_program)
    block.vector(vector_program)
    block.tensor(tensor_program)


NAMES = ["x", "positions", "mix_norm", "ffn_norm", "a_w_qkv", "a_q_norm", "a_k_norm", "a_sinks", "a_w_o",
         "b_w_in", "b_conv_w", "b_w_out", "f_w_gate_up", "f_w_down"]


def kernel(**inputs):
    from contextlib import ExitStack

    import concourse.bacc as bacc
    from concourse.bass_utils import run_bass_kernel_spmd

    nc = bacc.Bacc("TRN2", target_bir_lowering=False, num_devices=1)
    arrays, tensors = {}, {}
    for name in NAMES:
        a = np.ascontiguousarray(inputs[name])
        arrays["in_" + name] = a
        tensors[name] = nc.dram_tensor("in_" + name, a.shape, mybir.dt.from_np(a.dtype), kind="ExternalInput").ap()
    out = nc.dram_tensor("out_x", (1, S, D), F32, kind="ExternalOutput").ap()
    with ExitStack() as ctx:
        decoder_kernel(nc, ctx, tensors, out)
    return run_bass_kernel_spmd(nc, [arrays], core_ids=[0]).results[0]["out_x"]
```

```python
import concourse.bass as bass
import numpy as np
from concourse import mybir

F32 = mybir.dt.float32
F32R = mybir.dt.float32r
I32 = mybir.dt.int32
ALU = mybir.AluOpType
ACT = mybir.ActivationFunctionType
AX_X = mybir.AxisListType.X

P = 128
D = 1024
S = 1024
KT = D // P
NBLK = S // P
HALF = 512
HB = HALF // P
EPS = 1e-6
FF = ((8 * D + 767) // 768) * 256
HQ, HKV, HD = 16, 4, 64
GRP = HQ // HKV
NQK = HQ + HKV
QKW = NQK * HD
QKVW = (HQ + 2 * HKV) * HD
ROT = HD // 4
THETA = 500000.0
CW = 3
PIECE = 1024
NEG = -1e30

AHEAD = 3
Q_PIECES = QKVW * D // P // PIECE
O_PIECES = D // P
F_CHUNKS = FF // P // 2
F_PER = 6
C_CHUNKS = D // P // 2
C_PER = 8


class Phase:

    def __init__(self, base, n, per, ring, stages, landed):
        self.base, self.n, self.per, self.ring, self.stages = base, n, per, ring, stages
        self.landed = list(landed)
        self.after = [v + (n // stages if s < stages else 0) for s, v in enumerate(landed)]

    def piece(self, c, j):
        return c * self.per + (self.base + j)

    def slot(self, j):
        return j % self.ring

    def stage(self, j):
        return j % self.stages

    def arrival(self, c, j):
        return c * (16 * (self.per // self.stages)) + 16 * (self.landed[j % self.stages] + j // self.stages + 1)


PH_Q = Phase(0, Q_PIECES, 4, 4, 4, [0, 0, 0, 0])
PH_O = Phase(PH_Q.base + PH_Q.n, O_PIECES, 4, 4, 4, PH_Q.after)
PH_F0 = Phase(PH_O.base + PH_O.n, F_CHUNKS * F_PER, F_PER, 6, 3, PH_O.after)
PH_C = Phase(PH_F0.base + PH_F0.n, C_CHUNKS * C_PER, C_PER, 4, 4, PH_F0.after)
PH_F1 = Phase(PH_C.base + PH_C.n, F_CHUNKS * F_PER, F_PER, 6, 3, PH_C.after)
PH_F = [PH_F0, PH_F1]
N_PIECES = PH_F1.base + PH_F1.n

D_O, D_F0 = 0, 16 * 4
D_C = D_F0 + 16 * F_CHUNKS
D_F1 = D_C + 16 * C_CHUNKS
D_F = [D_F0, D_F1]
T_F = [0, 2 * F_CHUNKS]
A_F = [0, 2 * F_CHUNKS + 2 * C_CHUNKS]
A_C = 2 * F_CHUNKS
U_C = 2 * 2 * F_CHUNKS

U_F = [0, 2 * F_CHUNKS + 2 * C_CHUNKS]
INV_FREQ = np.float32(THETA) ** (-np.arange(0, ROT, 2, dtype=np.float32) / np.float32(ROT))
ROUND = 1.5 * 2.0 ** 23
PI_IN = 3.1415925
C_ANGLES = 12


def parts_of(x, bits, n):
    out = []
    for _ in range(n):
        e = 2.0 ** (np.floor(np.log2(abs(x))) - bits + 1)
        out.append(np.round(x / e) * e)
        x -= out[-1]
    return out


TWO_PI = parts_of(2 * np.pi, 8, 4)


def pt_count(n, last):
    done = min(n, HKV) + 2 * max(n - HKV, 0)
    return done + (1 if n < HKV or not last else 2)


HEAD_GROUP = (0, 1, 2, None, 3)
HEAD_COLUMNS = (0, 0, 1, 2, 1)
HEADS_USED = (1, 2, 3, 5, 6)
ROUNDS = 6
ROUND_HEADS = (0, 1, 2, 3, 3, 4)
ROUND_TILE = (0, 1, 2, 4, 5, 3)
ROUND_ACT = (1, 4)


def round_count(b, i):
    mine = [r for r in range(ROUNDS) if (r in ROUND_ACT) == (i in ROUND_ACT)]
    return len(mine) * b + mine.index(i) + 1


def rounds_beside(s):
    b, g = s // HKV, s % HKV
    if s >= NBLK * HKV or (g and b + 1 == NBLK):
        return None, None
    return (((b, 5), None), ((b + 1, 0), (b + 1, 1)), ((b + 1, 2), None), ((b + 1, 3), (b + 1, 4)))[g]


def heads_beside(s):
    b, g = s // HKV + 1, s % HKV
    if s < 0:
        return []
    return [(b, i) for i in ((0, 1), (2,), (3,), (4,))[g]] if b < NBLK else []


def split_ahead(split, eng, ph, c, j):
    split(eng, ph, c, j + AHEAD)


G_MIX, G_FFN, G_CONV, G_ROWS = 0, 2 * KT, 4 * KT, 4 * KT + CW * KT


def decoder_kernel(nc, ctx, t, out):
    KB = 1024
    base = (nc.sbuf_base + 127) // 128 * 128

    def sb(name, shape, dt, kb):
        return nc.alloc_sbuf_tensor_at(name, [P] + shape, dt, offset=int(base + kb * KB))

    X = sb("X", [KT, S], F32, 0)
    H = sb("H", [2, KT, S], F32R, 32)
    STG = sb("STG", [4, PIECE], F32, 96)
    WR = sb("WR", [6, 2, PIECE], F32R, 112)
    A = sb("A", [2, 2, S], F32R, 160)
    SG = sb("SG", [2, HALF], F32, 176)
    A32 = sb("A32", [2, HALF], F32, 180)
    BG = sb("BG", [S], F32, 144)
    CG = sb("CG", [S], F32, 148)
    ZC = sb("ZC", [CW - 1 + S], F32, 152)
    YC = sb("YC", [HALF], F32, 157)
    XN = sb("XN", [NBLK, D], F32, 144)
    QKV = sb("QKV", [NBLK, QKVW], F32, 144)
    QS = sb("QS", [24, P], F32R, 96)
    QT = sb("QT", [HQ, P], F32R, 108)
    KTT = sb("KTT", [2, HKV, 2, P], F32R, 116)
    PR = sb("PR", [3, GRP, 2 * P], F32, 124)
    PT = sb("PT", [2, 2, GRP * P], F32, 136)
    SQ = sb("SQ", [2, HALF], F32, 192)
    ACC = sb("ACC", [2, HALF], F32, 184)
    DG = sb("DG", [2, HALF], F32, 188)
    RS = sb("RS", [2, HALF], F32, 200)
    NS = sb("NS", [12], F32, 204)
    IDN = sb("IDN", [P], F32, 206)
    ONE = sb("ONE", [P], F32, 206.5)
    GT = sb("GT", [G_ROWS], F32, 207)
    ASQ = sb("ASQ", [2, HALF], F32, 192)
    COS = sb("COS", [NBLK, ROT], F32, 196)
    SIN = sb("SIN", [NBLK, ROT], F32, 196.5)
    MASK = sb("MASK", [3 * P], F32, 197)
    GBC = sb("GBC", [2 * HD + HQ], F32, 198.5)
    RT = sb("RT", [HALF // HD, ROT], F32, 199.125)
    RU = sb("RU", [HALF // HD, ROT], F32, 199.625)
    SSQ = sb("SSQ", [3, NBLK, HALF // HD], F32, 200.125)
    RR = sb("RR", [3, NBLK, HALF // HD], F32, 200.875)
    MH = sb("MH", [HALF // HD], F32, 201.625)
    TOK = sb("TOK", [2, NBLK], F32, 201.75)
    STAT = sb("STAT", [3, 5, GRP], F32, 205.625)
    ANG = sb("ANG", [2, 2, NBLK * ROT // 2], F32, 202.25)
    POST = sb("POST", [NBLK], F32, 203.25)
    INVF = sb("INVF", [ROT // 2], F32, 203.375)
    ROWS = sb("ROWS", [2 * HD + HQ], F32, 203.5)
    POSI = sb("POSI", [P], I32, 204.125)
    POSF = sb("POSF", [P], F32, 204.625)
    GRAW = sb("GRAW", [P], F32, 205.125)

    OUTB = sb("OUTB", [NBLK, D], F32, 32)

    PS = nc.alloc_psum_tensor("PS", [P, 8, HALF], F32)

    def sem(name):
        return ctx.enter_context(nc.semaphore(name))

    s_x = [sem(f"s_x{b}") for b in range(NBLK)]
    s_row, s_pos, s_gain = sem("s_row"), sem("s_pos"), sem("s_gain")
    s_idn0, s_idn, s_one = sem("s_idn0"), sem("s_idn"), sem("s_one")
    s_gt_sb, s_half = sem("s_gt_sb"), sem("s_half")
    stg = [sem(f"stg{s}") for s in range(4)]
    w_hi, w_split, w_used = sem("w_hi"), sem("w_split"), sem("w_used")
    x_tr, x_act, x_dve = sem("x_tr"), sem("x_act"), sem("x_dve")
    n_sq, n_acc, n_ss, n_v, n_r, n_dg, n_bc, n_rs, n_hi, n_lo = (
        sem("n_" + s) for s in "sq acc ss v r dg bc rs hi lo".split())
    t_sq, t_v, t_r = (sem("tok_" + s) for s in "sq v r".split())
    q_done, q_act, q_dve = sem("q_done"), sem("q_act"), sem("q_dve")
    c_bc, c_pos, c_dve, c_trig, c_gbc, c_inv = (sem("c_" + s) for s in "bc pos dve trig gbc inv".split())
    f_sq, f_red, f_v, f_g, f_rr, f_qn, f_rot, f_ru = (sem("f_" + s) for s in "sq red v g rr qn rot ru".split())
    qs_hi, qs_ready, r_done, r_act, r_dve = (sem(s) for s in "qs_hi qs_ready r_done r_act r_dve".split())
    a_sc, a_ttr, a_nm, a_exp, a_den, a_p, a_pt, a_pt_sb, a_pv, o_hi, o_lo = (
        sem(s) for s in "a_sc a_ttr a_nm a_exp a_den a_p a_pt a_pt_sb a_pv o_hi o_lo".split())
    g_done, u_done, g_scaled, silu_done, silu_scaled, mul_done, a_hi, a_ready = (
        sem(s) for s in "g_done u_done g_scaled silu_done silu_scaled mul_done a_hi a_ready".split())
    b_done, c_done, bc_copied, bc_scaled, z_halo, z_done, y_done = (
        sem(s) for s in "b_done c_done bc_copied bc_scaled z_halo z_done y_done".split())
    d_done, add_done = sem("d_done"), sem("add_done")
    t_done, t_act, t_dve, s_out = sem("t_done"), sem("t_act"), sem("t_dve"), sem("s_out")

    c_mask0, c_mask, y_step = (sem(s) for s in "c_mask0 c_mask y_step".split())

    def round_target(b, i):
        r = ROUND_TILE[i]
        return QT[:, 4 * r:4 * r + 4, :] if r < 4 else KTT[:, r - 4, :, b % 2, :]

    def angle(i):
        return ANG[:, 0, i, :].rearrange("p (b f) -> p b f", b=NBLK)

    def half(h):
        return slice(h * HALF, (h + 1) * HALF)

    def blk(b):
        return slice(b * P, (b + 1) * P)

    w_qkv, w_o = t["a_w_qkv"][0], t["a_w_o"][0]
    w_gu, w_dn = t["f_w_gate_up"], t["f_w_down"]
    w_in, w_out = t["b_w_in"][0], t["b_w_out"][0]
    x_dram, out_dram = t["x"][0], out[0]

    def sync_program(sp):
        def load(ph, c, j, src, cols=None):
            p = ph.piece(c, j)
            if not isinstance(p, int) or p >= AHEAD:
                sp.wait_ge(w_split, p + (1 - AHEAD))
            dst = STG[:, ph.stage(j), :]
            if cols:
                dst = dst.rearrange("p (k n) -> p k n", n=cols)
            sp.dma_start(dst, src).then_inc(stg[ph.stage(j)], 16)

        def columns(w, at, n):
            return w[:, bass.ds(at, n)].rearrange("(k p) n -> p k n", p=P)

        def load_q(c, j):
            rows = w_qkv[j * 2 * P:(j + 1) * 2 * P, c * HALF:(c + 1) * HALF]
            load(PH_Q, c, j, rows.rearrange("(k p) n -> p k n", p=P), HALF)

        sp.dma_start(GRAW[0:2 * KT, :], t["mix_norm"].rearrange("l (k p) -> (l k) p", p=P)).then_inc(s_gain, 16)
        sp.dma_start(GRAW[G_FFN:G_CONV, :], t["ffn_norm"].rearrange("l (k p) -> (l k) p", p=P)).then_inc(s_gain, 16)
        sp.dma_start(GRAW[G_CONV:G_ROWS, :], t["b_conv_w"][0].rearrange("l (k p) -> (l k) p", p=P)).then_inc(s_gain, 16)
        sp.dma_start(POSI[0:NBLK, :], t["positions"][0].rearrange("(b p) -> b p", p=P)).then_inc(s_pos, 16)
        sp.dma_start(ROWS[0:1, 0:HD], t["a_q_norm"]).then_inc(s_row, 16)
        sp.dma_start(ROWS[0:1, HD:2 * HD], t["a_k_norm"]).then_inc(s_row, 16)
        sp.dma_start(ROWS[0:1, 2 * HD:2 * HD + HQ], t["a_sinks"]).then_inc(s_row, 16)
        for b in range(NBLK):
            sp.dma_start(XN[:, b, :], x_dram[blk(b), :]).then_inc(s_x[b], 16)
            if b == HB - 1:
                for j in range(AHEAD):
                    load_q(0, j)
        for n in range(AHEAD, Q_PIECES):
            load_q(n // 4, n % 4)
        sp.wait_ge(r_done, 6 * NBLK)
        for n in range(O_PIECES):
            if n == AHEAD:
                sp.wait_ge(a_sc, NBLK * HKV)
            load(PH_O, n // 4, n % 4, w_o[n * P:(n + 1) * P, :])

        def load_ffn(l):
            with sp.Fori(0, F_CHUNKS) as c:
                for j in range(2):
                    load(PH_F[l], c, 2 * j, columns(w_gu[l], c * (2 * P) + j * P, P), P)
                    load(PH_F[l], c, 2 * j + 1, columns(w_gu[l], c * (2 * P) + (FF + j * P), P), P)
                for j in range(2):
                    load(PH_F[l], c, 4 + j, w_dn[l][bass.ds(c * (2 * P) + j * P, P), :])

        load_ffn(0)
        with sp.Fori(0, C_CHUNKS) as c:
            for j in range(2):
                for i in range(3):
                    load(PH_C, c, 3 * j + i, columns(w_in, c * (2 * P) + (i * D + j * P), P), P)
            for j in range(2):
                load(PH_C, c, 6 + j, w_out[bass.ds(c * (2 * P) + j * P, P), :])
        load_ffn(1)
        for b in range(NBLK):
            sp.wait_ge(t_act, b + 1)
            sp.wait_ge(t_dve, b + 1)
            sp.dma_start(out_dram[blk(b), :], OUTB[:, b, :]).then_inc(s_out, 16)
        sp.wait_ge(s_out, 16 * NBLK)

    def split_hi(act, ph, c, j):
        p = ph.piece(c, j)
        act.wait_ge(stg[ph.stage(j)], ph.arrival(c, j))
        back = 4 if isinstance(c, int) and c == 0 and j < 6 else ph.ring
        if not isinstance(p, int) or p >= back:
            act.wait_ge(w_used, p - (back - 1))
        nc.scalar.activation(WR[:, ph.slot(j), 0, :], STG[:, ph.stage(j), :], ACT.Copy).then_inc(w_hi, 1)

    def split_lo(dve, ph, c, j):
        dve.wait_ge(w_hi, ph.piece(c, j) + 1)
        nc.vector.tensor_tensor(WR[:, ph.slot(j), 1, :], STG[:, ph.stage(j), :],
                                WR[:, ph.slot(j), 0, :].bitcast(F32), ALU.subtract).then_inc(w_split, 1)

    def gain(n, k):
        at = (G_FFN if n % 2 else G_MIX) + (n // 2) * KT + k
        return GT[:, at:at + 1]

    def operand_hi(act, n, h, k):
        nc.scalar.activation(H[:, 0, k, half(h)], X[:, k, half(h)], ACT.Copy, scale=gain(n, k)).then_inc(n_hi, 1)

    def operand_lo(dve, n, h, k):
        dve.wait_ge(n_hi, KT * (2 * n + h) + k + 1)
        nc.vector.scalar_tensor_tensor(H[:, 1, k, half(h)], X[:, k, half(h)], gain(n, k),
                                       H[:, 0, k, half(h)].bitcast(F32), ALU.mult, ALU.subtract).then_inc(n_lo, 1)

    def norm_square(act, n, h, m):
        i = 2 * (n - 1) + h
        if m == 0:
            if i >= 2:
                act.wait_ge(n_ss, i - 1)
            nc.scalar.activation(ACC[:, h, :], X[:, m, half(h)], ACT.Square).then_inc(n_sq, 1)
        else:
            slot = 7 * i + m - 1
            if slot >= 2:
                act.wait_ge(n_acc, slot - 1)
            nc.scalar.activation(SQ[:, slot % 2, :], X[:, m, half(h)], ACT.Square).then_inc(n_sq, 1)

    def norm_accumulate(pool, n, h):
        i = 2 * (n - 1) + h
        for m in range(1, KT):
            pool.wait_ge(n_sq, KT * i + m + 1)
            if m > 1:
                pool.wait_ge(n_acc, 7 * i + m - 1)
            nc.gpsimd.tensor_tensor(ACC[:, h, :], ACC[:, h, :], SQ[:, (7 * i + m - 1) % 2, :], ALU.add).then_inc(n_acc, 1)

    def norm_root(pool, n, h):
        pool.wait_ge(n_v, 2 * (n - 1) + h + 1)
        nc.gpsimd.tensor_tensor(NS[:, 4:8], NS[:, 0:4], NS[:, 8:12], ALU.pow).then_inc(n_r, 1)

    def norm_sum(pe, n, h):
        i = 2 * (n - 1) + h
        pe.wait_ge(n_acc, 7 * (i + 1))
        if i:
            pe.wait_ge(n_v, i)
        for j in range(HB):
            mm = nc.tensor.matmul(PS[:, 6, j:j + 1], ACC[:, h, blk(j)], ONE[:, 0:1], start=True, stop=True)
        mm.then_inc(n_ss, 1)

    def norm_mean(dve, n, h):
        i = 2 * (n - 1) + h
        dve.wait_ge(n_ss, i + 1)
        if i:
            dve.wait_ge(n_r, i)
        nc.vector.tensor_scalar(NS[:, 0:4], PS[:, 6, 0:4], 1.0 / D, EPS, ALU.mult, ALU.add).then_inc(n_v, 1)

    def norm_diagonal(dve, n, h):
        i = 2 * (n - 1) + h
        dve.wait_ge(n_r, i + 1)
        if i >= 2:
            dve.wait_ge(n_bc, i - 1)
        for j in range(HB):
            v = nc.vector.tensor_scalar(DG[:, h, blk(j)], IDN[:], NS[:, 4 + j:5 + j], None, ALU.mult)
        v.then_inc(n_dg, 1)

    def norm_spread(pe, n, h):
        i = 2 * (n - 1) + h
        pe.wait_ge(n_dg, i + 1)
        if i:
            pe.wait_ge(n_rs, i)
        nc.tensor.matmul(PS[:, 7, :], ONE[:], DG[:, h, :], start=True, stop=True).then_inc(n_bc, 1)

    def norm_take(act, n, h):
        act.wait_ge(n_bc, 2 * (n - 1) + h + 1)
        nc.scalar.activation(RS[:, h, :], PS[:, 7, :], ACT.Copy).then_inc(n_rs, 1)

    PASSES = ((0, 0), (0, 1), (1, 0))

    def tensor_program(pe):
        pe.wait_ge(s_idn, 1)
        pe.wait_ge(s_one, 1)
        pe.wait_ge(s_gain, 48)
        nc.tensor.transpose(PS[:, 7, 0:G_ROWS], GRAW[0:G_ROWS, :], IDN[0:G_ROWS, 0:G_ROWS]).then_inc(c_bc, 1)
        pe.wait_ge(c_pos, 1)
        nc.tensor.transpose(PS[:, 6, 0:NBLK], POSF[0:NBLK, :], IDN[0:NBLK, 0:NBLK]).then_inc(c_bc, 1)
        pe.wait_ge(s_row, 48)
        nc.tensor.matmul(PS[:, 5, 0:2 * HD + HQ], ONE[0:1, :], ROWS[0:1, :], start=True, stop=True).then_inc(c_bc, 1)

        def transpose_x(b):
            pe.wait_ge(s_x[b], 16)
            for q in range(2):
                i = 2 * b + q
                if i >= 4:
                    pe.wait_ge(x_dve if q else x_act, i // 2 - 1)
                for j in range(4):
                    mm = nc.tensor.transpose(PS[:, 4 + i % 4, blk(j)], XN[:, b, blk(4 * q + j)], IDN[:])
                mm.then_inc(x_tr, 1)

        pe.wait_ge(c_gbc, 2)
        for b in range(HB):
            transpose_x(b)

        def qkv_product(c, kp, b, normed=None):
            for k in (2 * kp, 2 * kp + 1):
                if normed is not None:
                    pe.wait_ge(n_lo, normed + k + 1)
                for w, a in PASSES:
                    mm = nc.tensor.matmul(
                        PS[:, b, :], H[:, a, k, blk(b)],
                        WR[:, PH_Q.slot(kp), w, (k % 2) * HALF:(k % 2 + 1) * HALF],
                        start=(k == 0 and (w, a) == (0, 0)), stop=(k == KT - 1 and (w, a) == (1, 0)))
            if b == NBLK - 1:
                mm.then_inc(w_used, 1)
            elif kp == 3:
                mm.then_inc(q_done, 1)

        for h in range(2):
            for kp in range(4):
                if h == 0:
                    pe.wait_ge(w_split, PH_Q.piece(0, kp) + 1)
                if (h, kp) == (1, 0):
                    pe.wait_ge(x_act, NBLK)
                    pe.wait_ge(x_dve, NBLK)
                for b in range(h * HB, (h + 1) * HB):
                    qkv_product(0, kp, b, normed=KT * h if b % HB == 0 else None)
                if h == 0 and kp < 2:
                    transpose_x(HB + 2 * kp)
                    transpose_x(HB + 2 * kp + 1)
        with pe.Fori(1, QKVW // HALF) as c:
            for kp in range(4):
                pe.wait_ge(w_split, PH_Q.piece(c, kp) + 1)
                for b in range(NBLK):
                    if kp == 0:
                        pe.wait_ge(q_dve if b % 2 else q_act, c * 4 + (b // 2 - 3))
                    qkv_product(c, kp, b)

        pe.wait_ge(q_act, 12)
        pe.wait_ge(q_dve, 12)
        def round_trip(b, i):
            pe.wait_ge(qs_ready, 5 * b + ROUND_HEADS[i] + 1)
            at, last = (b, i - 1) if i else (b - 1, ROUNDS - 1)
            if at >= 0:
                pe.wait_ge(r_act if last in ROUND_ACT else r_dve, round_count(at, last))
            for j in range(4):
                mm = nc.tensor.transpose(PS[:, 0, blk(j)], QS[:, 4 * ROUND_TILE[i] + j, :].bitcast(F32), IDN[:])
            mm.then_inc(r_done, 1)

        def scores(n):
            b, g = n // HKV, n % HKV
            width = P if b == 0 else 2 * P
            for i in ((0, 3, 4), (1,), (2,), (5,))[g]:
                pe.wait_ge(r_act if i in ROUND_ACT else r_dve, round_count(b, i))
            if n >= 2:
                pe.wait_ge(a_ttr, 4 * (n - 1))
            for j in range(GRP):
                dst = PS[:, 1 + 2 * (n % 2) + j // 2, (j % 2) * 2 * P:(j % 2) * 2 * P + width]
                for part in range(2):
                    k = KTT[:, part, g, :, :].rearrange("p s n -> p (s n)")[:, 0:width]
                    mm = nc.tensor.matmul(dst, QT[:, GRP * g + j, :], k, start=(part == 0), stop=(part == 1))
            mm.then_inc(a_sc, 1)

        def slots(b):
            return (0,) if b == 0 else (0, 1)

        def probs_transposed(n):
            pe.wait_ge(a_p, n + 1)
            for s in slots(n // HKV):
                if n > (HKV - 1 if s else 0):
                    pe.wait_ge(a_pt_sb, pt_count(n - 1, s))
                for i, j in enumerate((0, 2, 1, 3)):
                    mm = nc.tensor.transpose(PS[:, 5 + s, blk(i)], PR[:, n % 3, j, blk(s)], IDN[:])
                mm.then_inc(a_pt, 1)

        def values(n):
            b, g = n // HKV, n % HKV
            pe.wait_ge(a_pt_sb, pt_count(n, 1))
            if n:
                pe.wait_ge(o_lo, n)
            for s in slots(b):
                of = b if s == b % 2 else b - 1
                v = QKV[:, of, QKW + HD * g:QKW + HD * (g + 1)]
                for odd in range(2):
                    mm = nc.tensor.matmul(PS[HD * odd:HD * (odd + 1), 7, 0:2 * P], v,
                                          PT[:, n % 2, s, 2 * P * odd:2 * P * (odd + 1)],
                                          start=(s == 0), stop=(s == slots(b)[-1]))
            mm.then_inc(a_pv, 1)

        n_groups = NBLK * HKV
        for i in range(ROUNDS - 1):
            round_trip(0, i)
        for n in range(-2, n_groups + 1):
            if n >= 1:
                probs_transposed(n - 1)
            if n + 2 < n_groups:
                scores(n + 2)
            first, second = rounds_beside(n + 2)
            if first:
                round_trip(*first)
            if n >= 1:
                values(n - 1)
            if second:
                round_trip(*second)

        def add_product(ph, c, j0, d0, h, m, operand):
            i = HB * 2 * h + m
            d = c * 16 + (d0 + i)
            if not (isinstance(d, int) and d < 2):
                pe.wait_ge(add_done, d - 1)
            for j in range(2):
                for w, a in PASSES:
                    mm = nc.tensor.matmul(PS[:, 4 + i % 2, :], WR[:, ph.slot(j0 + j), w, blk(m)],
                                          operand(j, a, h), start=(j == 0 and (w, a) == (0, 0)),
                                          stop=(j == 1 and (w, a) == (1, 0)))
            if i == 15:
                mm.then_inc(w_used, 2)
            else:
                mm.then_inc(d_done, 1)

        def inner(j, a, h):
            return A[:, j, a, half(h)]

        def add_products(ph, c, j0, d0, tiles, norm=None, last=False):
            pe.wait_ge(w_split, ph.piece(c, j0 + 1) + 1)
            for h in range(2):
                pe.wait_ge(a_ready, c * 4 + (2 * tiles + 3 + h))
                for m in range(KT):
                    add_product(ph, c, j0, d0, h, m, inner)
                    if last and h == 1 and m % 2:
                        transpose_out(m // 2)
            if norm is not None:
                norm_sum(pe, norm, 0)

        def transpose_out(b):
            pe.wait_ge(add_done, D_F1 + 16 * F_CHUNKS - (0 if b >= HB else 8))
            for q in range(2):
                i = 2 * b + q
                if b < 2:
                    pe.wait_ge(mul_done if q else silu_done, 2 * (T_F[1] + 2 * F_CHUNKS))
                    pe.wait_ge(mul_done, 2 * (T_F[1] + 2 * F_CHUNKS))
                else:
                    pe.wait_ge(t_dve if q else t_act, b - 1)
                for j in range(4):
                    mm = nc.tensor.transpose(PS[:, i % 4, blk(j)], X[:, 4 * q + j, blk(b)], IDN[:])
                mm.then_inc(t_done, 1)

        for c in range(4):
            pe.wait_ge(w_split, PH_O.piece(0, 2 * c + 1) + 1)
            for h in range(2):
                if c == 0:
                    pe.wait_ge(o_lo, n_groups // (2 - h))
                for m in range(KT):
                    add_product(PH_O, 0, 2 * c, D_O + 16 * c, h, m, lambda j, a, h: H[:, a, 2 * c + j, half(h)])
        norm_sum(pe, 1, 0)

        def product(ph, c, j, h, bank, done, norm=None):
            for k in range(KT):
                if norm is not None:
                    pe.wait_ge(n_lo, KT * (2 * norm + h) + k + 1)
                for w, a in PASSES:
                    mm = nc.tensor.matmul(PS[:, bank, :], WR[:, ph.slot(j), w, blk(k)], H[:, a, k, half(h)],
                                          start=(k == 0 and (w, a) == (0, 0)), stop=(k == KT - 1 and (w, a) == (1, 0)))
            mm.then_inc(*((done, 1) if h == 0 else (w_used, 1)))

        def gate_up(l, c, norm=None):
            ph = PH_F[l]
            for j in range(2):
                order = [(u, h) for u in range(2) for h in range(2)]
                first = norm is not None and j == 0
                if first:
                    order = [(u, h) for h in range(2) for u in range(2)]
                for u, h in order:
                    if h == 0:
                        pe.wait_ge(w_split, ph.piece(c, 2 * j + u) + 1)
                    tile = c * 2 + (T_F[l] + j)
                    if not isinstance(tile, int) or tile:
                        pe.wait_ge(mul_done if u else silu_done, c * 4 + (2 * (T_F[l] + j) + h - 1))
                    product(ph, c, 2 * j + u, h, 2 * u + h, u_done if u else g_done, norm if first and u == 0 else None)
                    if first and (u, h) == (0, 0):
                        norm_sum(pe, norm, 1)
                        norm_spread(pe, norm, 0)
                    if first and (u, h) == (1, 0):
                        norm_spread(pe, norm, 1)

        def ffn(l, norm, last_norm):
            gate_up(l, 0, norm)
            add_products(PH_F[l], 0, 4, D_F[l], A_F[l])
            with pe.Fori(1, F_CHUNKS - 1) as c:
                gate_up(l, c)
                add_products(PH_F[l], c, 4, D_F[l], A_F[l])
            gate_up(l, F_CHUNKS - 1)
            add_products(PH_F[l], F_CHUNKS - 1, 4, D_F[l], A_F[l], last_norm, last=l == 1)

        ffn(0, 1, 2)

        def gated(c, norm=None):
            for j in range(2):
                order = [(i, h) for i in range(3) for h in range(2)]
                first = norm is not None and j == 0
                if first:
                    order = [(i, h) for h in range(2) for i in range(3)]
                for i, h in order:
                    if h == 0:
                        pe.wait_ge(w_split, PH_C.piece(c, 3 * j + i) + 1)
                    start = not isinstance(c, int) or c > 0 or j > 0
                    if i == 2:
                        pe.wait_ge(bc_copied, c * 8 + (4 * j + h + 1))
                    elif i == 1 and start:
                        pe.wait_ge(bc_copied, c * 8 + (4 * j + h - 1))
                    elif start:
                        pe.wait_ge(z_done, c * 4 + (2 * j + h - 1))
                    product(PH_C, c, 3 * j + i, h, (0, 2, 0)[i] + h, (b_done, c_done, u_done)[i],
                            norm if first and i == 0 else None)
                    if first and (i, h) == (0, 0):
                        norm_sum(pe, norm, 1)
                        norm_spread(pe, norm, 0)
                    if first and (i, h) == (1, 0):
                        norm_spread(pe, norm, 1)

        gated(0, 2)
        add_products(PH_C, 0, 6, D_C, A_C)
        with pe.Fori(1, C_CHUNKS - 1) as c:
            gated(c)
            add_products(PH_C, c, 6, D_C, A_C)
        gated(C_CHUNKS - 1)
        add_products(PH_C, C_CHUNKS - 1, 6, D_C, A_C, 3)

        ffn(1, 3, None)

        for b in range(HB, NBLK):
            transpose_out(b)

    def scalar_program(act):
        def take_x(b):
            act.wait_ge(x_tr, 2 * b + 1)
            nc.scalar.activation(X[:, 0:4, blk(b)], PS[:, 4 + (2 * b) % 4, :].rearrange("p (k n) -> p k n", n=P),
                                 ACT.Copy).then_inc(x_act, 1)

        for b in range(HB):
            take_x(b)
        split_hi(act, PH_Q, 0, 0)
        act.wait_ge(s_gt_sb, 1)
        act.wait_ge(x_dve, HB)
        act.wait_ge(x_act, HB)
        for k in range(4):
            operand_hi(act, 0, 0, k)
        split_hi(act, PH_Q, 0, 1)
        for k in range(4, KT):
            operand_hi(act, 0, 0, k)
        for b in range(HB, NBLK):
            take_x(b)
            if b == HB + 1:
                split_hi(act, PH_Q, 0, 2)
        act.wait_ge(x_dve, NBLK)
        act.wait_ge(x_act, NBLK)
        for k in range(KT):
            operand_hi(act, 0, 1, k)
        split_hi(act, PH_Q, 0, 3)
        for b in range(NBLK):
            act.wait_ge(s_x[b], 16)
            if b:
                act.wait_ge(t_sq, b)
            nc.scalar.activation(ASQ[:], XN[:, b, :].rearrange("p (j n) -> p j n", j=2), ACT.Square,
                                 accum_out=TOK[:, 0, b:b + 1]).then_inc(t_sq, 1)

        act.wait_ge(c_dve, C_ANGLES)
        nc.scalar.activation(SIN[:, :, 0:ROT // 2], angle(0), ACT.Sin, scale=-1.0).then_inc(c_trig, 1)
        nc.scalar.activation(SIN[:, :, ROT // 2:ROT], angle(0), ACT.Sin).then_inc(c_trig, 1)
        nc.scalar.activation(COS[:, :, 0:ROT // 2], angle(1), ACT.Sin).then_inc(c_trig, 1)
        nc.scalar.activation(COS[:, :, ROT // 2:ROT], angle(1), ACT.Sin).then_inc(c_trig, 1)

        def take_qkv(c, b):
            act.wait_ge(q_done, c * 7 + (b + 1))
            if c == 0 and b == 0:
                act.wait_ge(t_r, 1)
            nc.scalar.activation(QKV[:, b, c * HALF:(c + 1) * HALF], PS[:, b, :], ACT.Copy,
                                 scale=TOK[:, 1, b:b + 1]).then_inc(q_act, 1)

        def square_heads(c, b):
            i = NBLK * c + b
            w = HALF if c < 2 else HKV * HD
            if b % 2:
                act.wait_ge(q_dve, 4 * c + b // 2 + 1)
            else:
                act.wait_ge(q_act, 4 * c + b // 2 + 1)
            if i >= 2:
                act.wait_ge(f_red, i - 1)
            nc.scalar.activation(ASQ[:, i % 2, 0:w], QKV[:, b, HALF * c:HALF * c + w], ACT.Square).then_inc(f_sq, 1)

        for c in range(QKVW // HALF):
            for j in range(4):
                if 4 * c + j > 0 and 4 * c + j + 3 < Q_PIECES:
                    split_hi(act, PH_Q, c, j + 3)
                if c:
                    square_heads(c - 1, 2 * j)
                    square_heads(c - 1, 2 * j + 1)
            for b in range(0, NBLK, 2):
                take_qkv(c, b)
                if c == 2 and b:
                    square_heads(c, b - 2)
                    square_heads(c, b - 1)
        for b in (NBLK - 2, NBLK - 1):
            square_heads(2, b)

        def heads_hi(b, g):
            act.wait_ge(f_rot, NBLK * HEAD_COLUMNS[g] + b + 1)
            if b:
                act.wait_ge(r_done, ROUNDS * (b - 1) + HEADS_USED[g])
            q = HEAD_GROUP[g]
            if q is not None:
                src = QKV[:, b, HD * GRP * q:HD * GRP * (q + 1)].rearrange("p (j n) -> p j n", n=HD)
                nc.scalar.activation(QS[:, GRP * q:GRP * (q + 1), 0:HD], src, ACT.Copy).then_inc(qs_hi, 1)
            else:
                src = QKV[:, b, HD * HQ:QKW].rearrange("p (j n) -> p j n", n=HD)
                src = src.unsqueeze(2).broadcast_to([P, HKV, 2, HD])
                dst = QS[:, HQ:HQ + HKV, :].rearrange("p j (s n) -> p j s n", s=2)
                nc.scalar.activation(dst, src, ACT.Copy).then_inc(qs_hi, 1)

        def take_round(b, i):
            act.wait_ge(r_done, ROUNDS * b + i + 1)
            nc.scalar.activation(round_target(b, i), PS[:, 0, :].rearrange("p (j n) -> p j n", n=P),
                                 ACT.Copy).then_inc(r_act, 1)

        def exponentials(n):
            w = P if n < HKV else 2 * P
            act.wait_ge(a_nm, n + 1)
            for j in range(GRP):
                nc.scalar.activation(PR[:, n % 3, j, 0:w], PR[:, n % 3, j, 0:w], ACT.Exp, scale=-1.0,
                                     bias=STAT[:, n % 3, 0, j:j + 1], accum_out=STAT[:, n % 3, 2, j:j + 1])
            nc.scalar.activation(STAT[:, n % 3, 3, :], STAT[:, n % 3, 1, :], ACT.Exp).then_inc(a_exp, 1)

        def take_probs(n):
            for s in ((0,) if n < HKV else (0, 1)):
                act.wait_ge(a_pt, pt_count(n, s))
                if n >= 2:
                    act.wait_ge(a_pv, n - 1)
                nc.scalar.activation(PT[:, n % 2, s, :], PS[:, 5 + s, :], ACT.Copy).then_inc(a_pt_sb, 1)

        def out_hi(n):
            b, g = n // HKV, n % HKV
            act.wait_ge(a_pv, n + 1)
            nc.scalar.activation(H[:, 0, 2 * g:2 * g + 2, blk(b)], PS[:, 7, 0:2 * P].rearrange("p (k n) -> p k n", n=P),
                                 ACT.Copy).then_inc(o_hi, 1)

        n_groups = NBLK * HKV
        for g in range(HKV + 1):
            heads_hi(0, g)
        for i in ROUND_ACT:
            take_round(0, i)
        for n in range(-2, n_groups + 1):
            if n >= 1:
                take_probs(n - 1)
            if 0 <= n + 1 < n_groups:
                exponentials(n + 1)
            if n >= 1:
                out_hi(n - 1)
            for r in rounds_beside(n + 2):
                if r and r[1] in ROUND_ACT:
                    take_round(*r)
            for step in heads_beside(n + 2):
                heads_hi(*step)
            if n >= n_groups - 2:
                split_hi(act, PH_O, 0, n - (n_groups - 2))

        def finished(norm, h, d0):
            for m in range(KT):
                act.wait_ge(add_done, d0 + KT * h + (KT if norm == 1 and m >= KT - 2 else m + 1))
                operand_hi(act, norm, h, m)
                norm_square(act, norm, h, m)

        for c in range(4):
            split_ahead(split_hi, act, PH_O, 0, 2 * c)
            if c == 3:
                finished(1, 0, D_O + 48)
            if c < 3:
                split_ahead(split_hi, act, PH_O, 0, 2 * c + 1)
        finished(1, 1, D_O + 48)
        split_ahead(split_hi, act, PH_O, 0, 7)
        norm_take(act, 1, 0)
        norm_take(act, 1, 1)

        def silu(l, c, j, h):
            i = c * 4 + (2 * (T_F[l] + j) + h)
            act.wait_ge(g_scaled, i + 1)
            if not isinstance(i, int) or i >= 2:
                act.wait_ge(mul_done, i - 1)
            nc.scalar.activation(SG[:, h, :], PS[:, h, :], ACT.Silu).then_inc(silu_done, 1)

        def inner_hi_of(c, j, h, done, first):
            act.wait_ge(done, c * 4 + (first + 2 * j + h + 1))
            nc.scalar.activation(A[:, j, 0, half(h)], A32[:, h, :], ACT.Copy).then_inc(a_hi, 1)

        def ffn_chunk(l, c, norm=None, ahead=True):
            ph = PH_F[l]
            for j in range(2):
                split_ahead(split_hi, act, ph, c, 2 * j)
                silu(l, c, j, 0)
                silu(l, c, j, 1)
                if ahead or j == 0:
                    split_ahead(split_hi, act, ph, c, 2 * j + 1)
                inner_hi_of(c, j, 0, mul_done, 2 * T_F[l])
                inner_hi_of(c, j, 1, mul_done, 2 * T_F[l])
            if ahead:
                split_ahead(split_hi, act, ph, c, 4)
            if norm is not None:
                finished(norm, 0, D_F[l] + 16 * c)
                finished(norm, 1, D_F[l] + 16 * c)
            if ahead:
                split_ahead(split_hi, act, ph, c, 5)
            if norm is not None:
                norm_take(act, norm, 0)
                norm_take(act, norm, 1)

        ffn_chunk(0, 0)
        with act.Fori(1, F_CHUNKS - 1) as c:
            ffn_chunk(0, c)
        ffn_chunk(0, F_CHUNKS - 1, norm=2)

        def copy_gate(c, j, i, h):
            if h == 0:
                act.wait_ge((b_done, c_done)[i], c * 2 + (j + 1))
            else:
                act.wait_ge(w_used, PH_C.piece(c, 3 * j + i) + 1)
            act.wait_ge(a_ready, c * 4 + (2 * (A_C + j) + h - 1))
            nc.scalar.activation((BG, CG)[i][:, half(h)], PS[:, 2 * i + h, :], ACT.Copy).then_inc(bc_copied, 1)

        def conv_chunk(c, norm=None):
            for j in range(2):
                for i in range(2):
                    split_ahead(split_hi, act, PH_C, c, 3 * j + i)
                    copy_gate(c, j, i, 0)
                    copy_gate(c, j, i, 1)
                split_ahead(split_hi, act, PH_C, c, 3 * j + 2)
                inner_hi_of(c, j, 0, y_done, 0)
                inner_hi_of(c, j, 1, y_done, 0)
            split_ahead(split_hi, act, PH_C, c, 6)
            if norm is not None:
                finished(norm, 0, D_C + 16 * c)
                finished(norm, 1, D_C + 16 * c)
            split_ahead(split_hi, act, PH_C, c, 7)
            if norm is not None:
                norm_take(act, norm, 0)
                norm_take(act, norm, 1)

        with act.Fori(0, C_CHUNKS - 1) as c:
            conv_chunk(c)
        conv_chunk(C_CHUNKS - 1, norm=3)
        ffn_chunk(1, 0)
        with act.Fori(1, F_CHUNKS - 1) as c:
            ffn_chunk(1, c)
        ffn_chunk(1, F_CHUNKS - 1, ahead=False)
        for b in range(NBLK):
            act.wait_ge(t_done, 2 * b + 1)
            nc.scalar.activation(OUTB[:, b, 0:HALF], PS[:, (2 * b) % 4, :], ACT.Copy).then_inc(t_act, 1)

    def vector_program(dve):
        nc.vector.memset(ONE[:], 1.0).then_inc(s_one, 1)
        dve.wait_ge(s_pos, 16)
        nc.vector.tensor_copy(POSF[0:NBLK, :], POSI[0:NBLK, :]).then_inc(c_pos, 1)
        for f in range(ROT // 2):
            nc.vector.memset(INVF[:, f:f + 1], float(INV_FREQ[f])).then_inc(c_inv, 1)
        dve.wait_ge(c_bc, 3)
        nc.vector.tensor_copy(GT[:], PS[:, 7, 0:G_ROWS]).then_inc(s_gt_sb, 1)
        nc.vector.tensor_copy(POST[:], PS[:, 6, 0:NBLK]).then_inc(c_inv, 1)
        nc.vector.tensor_copy(GBC[:, 0:2 * HD], PS[:, 5, 0:2 * HD]).then_inc(c_gbc, 1)
        nc.vector.tensor_scalar(GBC[:, 2 * HD:2 * HD + HQ], PS[:, 5, 2 * HD:2 * HD + HQ], -1.0, None,
                                ALU.mult).then_inc(c_gbc, 1)

        def take_x(b):
            dve.wait_ge(x_tr, 2 * b + 2)
            nc.vector.tensor_copy(X[:, 4:8, blk(b)],
                                  PS[:, 4 + (2 * b + 1) % 4, :].rearrange("p (k n) -> p k n", n=P)).then_inc(x_dve, 1)

        for b in range(HB):
            take_x(b)
        split_lo(dve, PH_Q, 0, 0)
        dve.wait_ge(s_gt_sb, 1)
        for k in range(4):
            operand_lo(dve, 0, 0, k)
        split_lo(dve, PH_Q, 0, 1)
        for k in range(4, KT):
            operand_lo(dve, 0, 0, k)
        for b in range(HB, NBLK):
            take_x(b)
            if b == HB + 1:
                split_lo(dve, PH_Q, 0, 2)
        for k in range(KT):
            operand_lo(dve, 0, 1, k)
        split_lo(dve, PH_Q, 0, 3)

        count = [0]

        def step(v):
            v.then_inc(c_dve, 1)
            count[0] += 1
            dve.wait_ge(c_dve, count[0])

        def tile(i):
            return ANG[:, i, :, :]

        dve.wait_ge(c_inv, ROT // 2 + 1)
        pos = POST[:].unsqueeze(2).broadcast_to([P, NBLK, ROT // 2])
        inv = INVF[:].unsqueeze(1).broadcast_to([P, NBLK, ROT // 2])
        for i in range(2):
            step(nc.vector.tensor_tensor(angle(i), pos, inv, ALU.mult))
        for i in range(2):
            step(nc.vector.tensor_scalar(ANG[:, 1, i, :], ANG[:, 0, i, :], 1 / (2 * np.pi), 0.25 * i, ALU.mult, ALU.add))
        step(nc.vector.tensor_scalar(tile(1), tile(1), ROUND, None, ALU.add))
        step(nc.vector.tensor_scalar(tile(1), tile(1), -ROUND, None, ALU.add))
        for part in TWO_PI:
            step(nc.vector.scalar_tensor_tensor(tile(0), tile(1), -float(part), tile(0), ALU.mult, ALU.add))
        step(nc.vector.tensor_scalar(ANG[:, 0, 1, :], ANG[:, 0, 1, :], float(np.float32(np.pi / 2)), None, ALU.add))
        step(nc.vector.tensor_scalar(tile(0), tile(0), PI_IN, -PI_IN, ALU.min, ALU.max))
        assert count[0] == C_ANGLES
        dve.wait_ge(t_sq, NBLK)
        nc.vector.tensor_scalar(TOK[:, 0, :], TOK[:, 0, :], 1.0 / D, EPS, ALU.mult, ALU.add).then_inc(t_v, 1)
        dve.wait_ge(t_r, 1)

        def take_qkv(c, b):
            if b == NBLK - 1:
                dve.wait_ge(w_used, 4 * c + 4)
            else:
                dve.wait_ge(q_done, c * 7 + (b + 1))
            nc.vector.tensor_scalar(QKV[:, b, c * HALF:(c + 1) * HALF], PS[:, b, :], TOK[:, 1, b:b + 1], None,
                                    ALU.mult).then_inc(q_dve, 1)

        def mean_heads(c, b):
            i = NBLK * c + b
            n = HALF // HD if c < 2 else HKV
            dve.wait_ge(f_sq, i + 1)
            nc.vector.tensor_reduce(SSQ[:, c, b, 0:n], ASQ[:, i % 2, 0:n * HD].rearrange("p (j n) -> p j n", n=HD),
                                    AX_X, ALU.add).then_inc(f_red, 1)
            dve.wait_ge(f_red, i + 1)
            nc.vector.tensor_scalar(SSQ[:, c, b, 0:n], SSQ[:, c, b, 0:n], 1.0 / HD, EPS,
                                    ALU.mult, ALU.add).then_inc(f_v, 1)
            x = QKV[:, b, HALF * c:HALF * c + n * HD].rearrange("p (j n) -> p j n", n=HD)
            g = HD if c == 2 else 0
            nc.vector.tensor_tensor(x, x, GBC[:, g:g + HD].unsqueeze(1).broadcast_to([P, n, HD]), ALU.mult).then_inc(f_g, 1)

        for c in range(QKVW // HALF):
            for j in range(4):
                if 4 * c + j > 0 and 4 * c + j + 3 < Q_PIECES:
                    split_lo(dve, PH_Q, c, j + 3)
                if c:
                    mean_heads(c - 1, 2 * j)
                    mean_heads(c - 1, 2 * j + 1)
            for b in range(1, NBLK, 2):
                take_qkv(c, b)
                if c == 2 and b > 1:
                    mean_heads(c, b - 3)
                    mean_heads(c, b - 2)
        for b in (NBLK - 2, NBLK - 1):
            mean_heads(2, b)

        def heads_lo(b, g):
            dve.wait_ge(qs_hi, 5 * b + g + 1)
            q = HEAD_GROUP[g]
            if q is not None:
                src = QKV[:, b, HD * GRP * q:HD * GRP * (q + 1)].rearrange("p (j n) -> p j n", n=HD)
                s = slice(GRP * q, GRP * (q + 1))
                nc.vector.tensor_tensor(QS[:, s, HD:P], src, QS[:, s, 0:HD].bitcast(F32), ALU.subtract).then_inc(qs_ready, 1)
            else:
                src = QKV[:, b, HD * HQ:QKW].rearrange("p (j n) -> p j n", n=HD)
                src = src.unsqueeze(2).broadcast_to([P, HKV, 2, HD])
                hi = QS[:, HQ:HQ + HKV, :].rearrange("p j (s n) -> p j s n", s=2)
                lo = QS[:, HQ + HKV:HQ + 2 * HKV, :].rearrange("p j (s n) -> p j s n", s=2)
                nc.vector.tensor_tensor(lo, src, hi.bitcast(F32), ALU.subtract).then_inc(qs_ready, 1)

        def take_round(b, i):
            dve.wait_ge(r_done, ROUNDS * b + i + 1)
            nc.vector.tensor_copy(round_target(b, i), PS[:, 0, :].rearrange("p (j n) -> p j n", n=P)).then_inc(r_dve, 1)

        def scores_masked(n):
            b, g = n // HKV, n % HKV
            w = P if b == 0 else 2 * P
            at = P if b % 2 == 0 else 0
            dve.wait_ge(a_sc, n + 1)
            if n >= 3:
                dve.wait_ge(a_pt, pt_count(n - 3, 1))
            for j in range(GRP):
                src = PS[:, 1 + 2 * (n % 2) + j // 2, (j % 2) * 2 * P:(j % 2) * 2 * P + w]
                h = 2 * HD + GRP * g + j
                nc.vector.tensor_tensor_reduce(
                    out=PR[:, n % 3, j, 0:w], in0=src, in1=MASK[:, at:at + w], scale=-(HD ** -0.5),
                    scalar=GBC[:, h:h + 1], op0=ALU.add, op1=ALU.min,
                    accum_out=STAT[:, n % 3, 0, j:j + 1]).then_inc(a_ttr, 1)
            dve.wait_ge(a_ttr, 4 * (n + 1))
            sink = GBC[:, 2 * HD + GRP * g:2 * HD + GRP * (g + 1)]
            nc.vector.tensor_tensor(STAT[:, n % 3, 1, :], STAT[:, n % 3, 0, :], sink, ALU.subtract).then_inc(a_nm, 1)

        def probs(n):
            w = P if n < HKV else 2 * P
            dve.wait_ge(a_exp, n + 1)
            nc.vector.tensor_tensor(STAT[:, n % 3, 2, :], STAT[:, n % 3, 2, :], STAT[:, n % 3, 3, :], ALU.add).then_inc(a_den, 1)
            dve.wait_ge(a_den, 2 * n + 1)
            nc.vector.reciprocal(STAT[:, n % 3, 4, :], STAT[:, n % 3, 2, :]).then_inc(a_den, 1)
            dve.wait_ge(a_den, 2 * n + 2)
            for j in range(GRP):
                v = nc.vector.tensor_scalar(PR[:, n % 3, j, 0:w], PR[:, n % 3, j, 0:w], STAT[:, n % 3, 4, j:j + 1],
                                            None, ALU.mult)
            v.then_inc(a_p, 1)

        def out_lo(n):
            b, g = n // HKV, n % HKV
            dve.wait_ge(o_hi, n + 1)
            nc.vector.tensor_tensor(H[:, 1, 2 * g:2 * g + 2, blk(b)], PS[:, 7, 0:2 * P].rearrange("p (k n) -> p k n", n=P),
                                    H[:, 0, 2 * g:2 * g + 2, blk(b)].bitcast(F32), ALU.subtract).then_inc(o_lo, 1)

        n_groups = NBLK * HKV
        for g in range(HKV + 1):
            heads_lo(0, g)
        for i in range(ROUNDS - 1):
            if i not in ROUND_ACT:
                take_round(0, i)
        dve.wait_ge(c_mask, 2)
        for n in range(-2, n_groups + 2):
            if n >= 2:
                out_lo(n - 2)
            for step in heads_beside(n + 1):
                heads_lo(*step)
            if 0 <= n + 1 < n_groups:
                scores_masked(n + 1)
            for r in rounds_beside(n + 2):
                if r and r[1] not in ROUND_ACT:
                    take_round(*r)
            if 0 <= n < n_groups:
                probs(n)
            if n >= n_groups - 1:
                split_lo(dve, PH_O, 0, n - (n_groups - 1))

        def add(ph, c, last, d0, h, m):
            i = KT * h + m
            if i == 15:
                dve.wait_ge(w_used, ph.piece(c, last) + 1)
            else:
                dve.wait_ge(d_done, c * 15 + (d0 // 16 * 15 + i + 1))
            nc.vector.tensor_tensor(X[:, m, half(h)], X[:, m, half(h)], PS[:, 4 + i % 2, :], ALU.add).then_inc(add_done, 1)

        def adds(ph, c, last, d0, norm=None, begin=0, beside=()):
            for i in range(begin, 2 * KT + (2 if norm else 0)):
                if i < 2 * KT:
                    add(ph, c, last, d0, i // KT, i % KT)
                if norm and i >= 2:
                    operand_lo(dve, norm, (i - 2) // KT, (i - 2) % KT)
                for at, j in beside:
                    if at == i:
                        split_ahead(split_lo, dve, ph, c, j)

        def norm_factors(norm):
            for h in range(2):
                norm_mean(dve, norm, h)
                norm_diagonal(dve, norm, h)

        for c in range(4):
            adds(PH_O, 0, 2 * c + 1, D_O + 16 * c, norm=1 if c == 3 else None, beside=[(1, 2 * c)])
            split_ahead(split_lo, dve, PH_O, 0, 2 * c + 1)
        norm_factors(1)

        def inner_lo(c, j, h, tiles):
            dve.wait_ge(a_hi, c * 4 + (2 * (tiles + j) + h + 1))
            nc.vector.tensor_tensor(A[:, j, 1, half(h)], A32[:, h, :], A[:, j, 0, half(h)].bitcast(F32),
                                    ALU.subtract).then_inc(a_ready, 1)

        def scale_gate(l, c, j, h):
            if h == 0:
                dve.wait_ge(g_done, c * 2 + (T_F[l] + j + 1))
            else:
                dve.wait_ge(w_used, PH_F[l].piece(c, 2 * j) + 1)
            dve.wait_ge(n_rs, 4 * l + h + 1)
            nc.vector.tensor_tensor(PS[:, h, :], PS[:, h, :], RS[:, h, :], ALU.mult).then_inc(g_scaled, 1)

        def multiply(l, c, j, h):
            i = c * 4 + (2 * (T_F[l] + j) + h)
            if h == 0:
                dve.wait_ge(u_done, c * 2 + (U_F[l] + j + 1))
            else:
                dve.wait_ge(w_used, PH_F[l].piece(c, 2 * j + 1) + 1)
            dve.wait_ge(silu_scaled, i + 1)
            first = c * 4 + (2 * (A_F[l] + j) + h)
            if not isinstance(first, int) or first >= 2:
                dve.wait_ge(a_ready, first - 1)
            nc.vector.tensor_tensor(A32[:, h, :], SG[:, h, :], PS[:, 2 + h, :], ALU.mult).then_inc(mul_done, 1)

        def ffn_chunk(l, c, norm=None, ahead=True):
            ph = PH_F[l]
            for j in range(2):
                split_ahead(split_lo, dve, ph, c, 2 * j)
                scale_gate(l, c, j, 0)
                scale_gate(l, c, j, 1)
                if ahead or j == 0:
                    split_ahead(split_lo, dve, ph, c, 2 * j + 1)
                for h in range(2):
                    multiply(l, c, j, h)
                    inner_lo(c, j, h, A_F[l])
            if norm is not None:
                adds(ph, c, 5, D_F[l], norm, beside=[(1, 4)])
                split_ahead(split_lo, dve, ph, c, 5)
                norm_factors(norm)
            elif ahead:
                adds(ph, c, 5, D_F[l], beside=[(1, 4), (9, 5)])

        ffn_chunk(0, 0)
        with dve.Fori(1, F_CHUNKS - 1) as c:
            ffn_chunk(0, c)
        ffn_chunk(0, F_CHUNKS - 1, norm=2)

        nc.vector.memset(ZC[:, 0:CW - 1], 0.0).then_inc(z_halo, 1)

        def tap(c, j, i):
            at = G_CONV + i * KT
            return GT[:, bass.ds(c * 2 + (at + j), 1)]

        def convolve(c, j, h, beside=lambda step: None):
            if h == 0:
                dve.wait_ge(u_done, c * 2 + (2 * F_CHUNKS + j + 1))
            else:
                dve.wait_ge(w_used, PH_C.piece(c, 3 * j + 2) + 1)
            n = c * 4 + (2 * j + h)
            dve.wait_ge(bc_scaled, c * 12 + (6 * j + 2 + 2 * h + 2))
            if h == 0:
                dve.wait_ge(a_ready, c * 4 + 2 * (A_C + j))
            else:
                dve.wait_ge(y_done, n)
            nc.vector.tensor_tensor(ZC[:, CW - 1 + h * HALF:CW - 1 + (h + 1) * HALF], CG[:, half(h)],
                                    PS[:, h, :], ALU.mult).then_inc(z_done, 1)
            beside(0)
            dve.wait_ge(z_done, n + 1)
            dve.wait_ge(z_halo, 1)
            z = [ZC[:, h * HALF + i:(h + 1) * HALF + i] for i in range(CW)]
            nc.vector.tensor_scalar(YC[:], z[0], tap(c, j, 0), None, ALU.mult).then_inc(y_step, 1)
            beside(1)
            dve.wait_ge(y_step, c * 12 + (6 * j + 3 * h + 1))
            nc.vector.scalar_tensor_tensor(YC[:], z[1], tap(c, j, 1), YC[:], ALU.mult, ALU.add).then_inc(y_step, 1)
            dve.wait_ge(y_step, c * 12 + (6 * j + 3 * h + 2))
            nc.vector.scalar_tensor_tensor(YC[:], z[2], tap(c, j, 2), YC[:], ALU.mult, ALU.add).then_inc(y_step, 1)
            beside(2)
            dve.wait_ge(y_step, c * 12 + (6 * j + 3 * h + 3))
            dve.wait_ge(a_ready, c * 4 + (2 * (A_C + j) + h - 1))
            nc.vector.tensor_tensor(A32[:, h, :], BG[:, half(h)], YC[:], ALU.mult).then_inc(y_done, 1)

        def conv_chunk(c, norm=None):
            for j in range(2):
                for i in range(3):
                    split_ahead(split_lo, dve, PH_C, c, 3 * j + i)
                for h in range(2):
                    def first_adds(step):
                        if (j, h) == (1, 1) and step >= 1:
                            add(PH_C, c, 7, D_C, 0, step - 1)

                    convolve(c, j, h, first_adds)
                    if (j, h) == (1, 1):
                        add(PH_C, c, 7, D_C, 0, 2)
                    inner_lo(c, j, h, A_C)
            if norm is not None:
                operand_lo(dve, norm, 0, 0)
            adds(PH_C, c, 7, D_C, norm, begin=3, beside=[(4, 6)])
            split_ahead(split_lo, dve, PH_C, c, 7)
            if norm is not None:
                norm_factors(norm)

        with dve.Fori(0, C_CHUNKS - 1) as c:
            conv_chunk(c)
        conv_chunk(C_CHUNKS - 1, norm=3)
        ffn_chunk(1, 0)
        with dve.Fori(1, F_CHUNKS - 1) as c:
            ffn_chunk(1, c)
        ffn_chunk(1, F_CHUNKS - 1, ahead=False)

        def take_out(b):
            dve.wait_ge(t_done, 2 * b + 2)
            nc.vector.tensor_copy(OUTB[:, b, HALF:D], PS[:, (2 * b + 1) % 4, :]).then_inc(t_dve, 1)

        for i in range(2 * KT):
            add(PH_F1, F_CHUNKS - 1, 5, D_F1, i // KT, i % KT)
            if i > KT + 1 and i % 2 == 0:
                take_out((i - KT) // 2 - 1)
        for b in range(HB - 1, NBLK):
            take_out(b)

    def pool_program(pool):
        nc.gpsimd.memset(IDN[:], 0.0).then_inc(s_idn0, 1)
        pool.wait_ge(s_idn0, 1)
        nc.gpsimd.affine_select(out=IDN[:], in_=IDN[:], compare_op=ALU.not_equal, fill=1.0, base=0,
                                pattern=[[-1, P]], channel_multiplier=1).then_inc(s_idn, 1)
        nc.gpsimd.memset(MASK[:], 0.0).then_inc(c_mask0, 1)
        nc.gpsimd.memset(MH[:], -0.5).then_inc(c_mask0, 1)
        pool.wait_ge(c_mask0, 2)
        nc.gpsimd.affine_select(out=MASK[:, P:2 * P], in_=MASK[:, P:2 * P], compare_op=ALU.is_ge, fill=NEG, base=0,
                                pattern=[[-1, P]], channel_multiplier=1).then_inc(c_mask, 1)
        for at in (0, 2 * P):
            m = nc.gpsimd.affine_select(out=MASK[:, at:at + P], in_=MASK[:, at:at + P], compare_op=ALU.is_gt,
                                        fill=NEG, base=0, pattern=[[1, P]], channel_multiplier=-1)
        m.then_inc(c_mask, 1)
        pool.wait_ge(t_v, 1)
        nc.gpsimd.tensor_tensor(TOK[:, 1, :], TOK[:, 0, :], MH[:], ALU.pow).then_inc(t_r, 1)
        pool.wait_ge(t_r, 1)

        def heads(c, b):
            i = NBLK * c + b
            n = HALF // HD if c < 2 else HKV
            x = QKV[:, b, HALF * c:HALF * c + n * HD].rearrange("p (j n) -> p j n", n=HD)
            pool.wait_ge(f_v, i + 1)
            nc.gpsimd.tensor_tensor(RR[:, c, b, 0:n], SSQ[:, c, b, 0:n], MH[:, 0:n], ALU.pow).then_inc(f_rr, 1)
            pool.wait_ge(f_rr, i + 1)
            pool.wait_ge(f_g, i + 1)
            nc.gpsimd.tensor_tensor(x, x, RR[:, c, b, 0:n].unsqueeze(2).broadcast_to([P, n, HD]), ALU.mult).then_inc(f_qn, 1)
            pool.wait_ge(f_qn, i + 1)
            hr = ROT // 2
            cos = COS[:, b, :].unsqueeze(1).broadcast_to([P, n, ROT])
            sin = [SIN[:, b, s * hr:(s + 1) * hr].unsqueeze(1).broadcast_to([P, n, hr]) for s in range(2)]
            nc.gpsimd.tensor_tensor(RT[:, 0:n, :], x[:, :, 0:ROT], cos, ALU.mult).then_inc(f_ru, 1)
            nc.gpsimd.tensor_tensor(RU[:, 0:n, 0:hr], x[:, :, hr:ROT], sin[0], ALU.mult).then_inc(f_ru, 1)
            nc.gpsimd.tensor_tensor(RU[:, 0:n, hr:ROT], x[:, :, 0:hr], sin[1], ALU.mult).then_inc(f_ru, 1)
            pool.wait_ge(f_ru, 3 * i + 3)
            nc.gpsimd.tensor_tensor(x[:, :, 0:ROT], RT[:, 0:n, :], RU[:, 0:n, :], ALU.add).then_inc(f_rot, 1)
            pool.wait_ge(f_rot, i + 1)

        pool.wait_ge(c_trig, 4)
        for c in range(3):
            for b in range(NBLK):
                heads(c, b)

        pool.wait_ge(o_lo, NBLK * HKV)
        nc.gpsimd.memset(NS[:, 8:12], -0.5).then_inc(s_half, 1)
        pool.wait_ge(s_half, 1)

        def both_halves(n):
            for h in range(2):
                norm_accumulate(pool, n, h)
            for h in range(2):
                norm_root(pool, n, h)

        def scale_silu(l):
            pool.wait_ge(n_rs, 4 * l + 2)
            with pool.Fori(0, 2 * F_CHUNKS) as i:
                for h in range(2):
                    pool.wait_ge(silu_done, i * 2 + (2 * T_F[l] + h + 1))
                    nc.gpsimd.tensor_tensor(SG[:, h, :], SG[:, h, :], RS[:, h, :], ALU.mult).then_inc(silu_scaled, 1)

        def scale_gated():
            pool.wait_ge(n_rs, 4)
            with pool.Fori(0, 2 * C_CHUNKS) as i:
                for h in range(2):
                    pool.wait_ge(bc_copied, i * 4 + (h + 1))
                    nc.gpsimd.tensor_tensor(BG[:, half(h)], BG[:, half(h)], RS[:, h, :], ALU.mult).then_inc(bc_scaled, 1)
                for h in range(2):
                    for twice in range(2):
                        pool.wait_ge(bc_scaled, i * 6 + (2 + 2 * h + twice))
                        if not twice:
                            pool.wait_ge(bc_copied, i * 4 + (h + 3))
                        nc.gpsimd.tensor_tensor(CG[:, half(h)], CG[:, half(h)], RS[:, h, :], ALU.mult).then_inc(bc_scaled, 1)

        both_halves(1)
        scale_silu(0)
        both_halves(2)
        scale_gated()
        both_halves(3)
        scale_silu(1)

    block = ctx.enter_context(nc.Block())
    block.sync(sync_program)
    block.gpsimd(pool_program)
    block.scalar(scalar_program)
    block.vector(vector_program)
    block.tensor(tensor_program)


NAMES = ["x", "positions", "mix_norm", "ffn_norm", "a_w_qkv", "a_q_norm", "a_k_norm", "a_sinks", "a_w_o",
         "b_w_in", "b_conv_w", "b_w_out", "f_w_gate_up", "f_w_down"]


def kernel(**inputs):
    from contextlib import ExitStack

    import concourse.bacc as bacc
    from concourse.bass_utils import run_bass_kernel_spmd

    nc = bacc.Bacc("TRN2", target_bir_lowering=False, num_devices=1)
    arrays, tensors = {}, {}
    for name in NAMES:
        a = np.ascontiguousarray(inputs[name])
        arrays["in_" + name] = a
        tensors[name] = nc.dram_tensor("in_" + name, a.shape, mybir.dt.from_np(a.dtype), kind="ExternalInput").ap()
    out = nc.dram_tensor("out_x", (1, S, D), F32, kind="ExternalOutput").ap()
    with ExitStack() as ctx:
        decoder_kernel(nc, ctx, tensors, out)
    return run_bass_kernel_spmd(nc, [arrays], core_ids=[0]).results[0]["out_x"]
```

```python
import concourse.bass as bass
import numpy as np
from concourse import mybir

F32 = mybir.dt.float32
F32R = mybir.dt.float32r
I32 = mybir.dt.int32
ALU = mybir.AluOpType
ACT = mybir.ActivationFunctionType
AX_X = mybir.AxisListType.X

P = 128
D = 1024
S = 1024
KT = D // P
NBLK = S // P
HALF = 512
HB = HALF // P
EPS = 1e-6
FF = ((8 * D + 767) // 768) * 256
HQ, HKV, HD = 16, 4, 64
GRP = HQ // HKV
NQK = HQ + HKV
QKW = NQK * HD
QKVW = (HQ + 2 * HKV) * HD
ROT = HD // 4
THETA = 500000.0
CW = 3
PIECE = 1024
NEG = -1e30

LAG = 4
AHEAD = 3
Q_PIECES = QKVW * D // P // PIECE
O_PIECES = D // P
F_CHUNKS = FF // P // 2
F_PER = 6
C_CHUNKS = D // P // 2
C_PER = 8


class Phase:

    def __init__(self, base, n, per, ring, stages, landed):
        self.base, self.n, self.per, self.ring, self.stages = base, n, per, ring, stages
        self.landed = list(landed)
        self.after = [v + (n // stages if s < stages else 0) for s, v in enumerate(landed)]

    def piece(self, c, j):
        return c * self.per + (self.base + j)

    def slot(self, j):
        return j % self.ring

    def stage(self, j):
        return j % self.stages

    def arrival(self, c, j):
        return c * (16 * (self.per // self.stages)) + 16 * (self.landed[j % self.stages] + j // self.stages + 1)


PH_Q = Phase(0, Q_PIECES, 4, 4, 4, [0, 0, 0, 0])
PH_O = Phase(PH_Q.base + PH_Q.n, O_PIECES, 4, 4, 4, PH_Q.after)
PH_F0 = Phase(PH_O.base + PH_O.n, F_CHUNKS * F_PER, F_PER, 6, 3, PH_O.after)
PH_C = Phase(PH_F0.base + PH_F0.n, C_CHUNKS * C_PER, C_PER, 4, 4, PH_F0.after)
PH_F1 = Phase(PH_C.base + PH_C.n, F_CHUNKS * F_PER, F_PER, 6, 3, PH_C.after)
PH_F = [PH_F0, PH_F1]

D_O, D_F0 = 0, 16 * 4
D_C = D_F0 + 16 * F_CHUNKS
D_F1 = D_C + 16 * C_CHUNKS
D_F = [D_F0, D_F1]
T_F = [0, 2 * F_CHUNKS]
A_F = [0, 2 * F_CHUNKS + 2 * C_CHUNKS]
A_C = 2 * F_CHUNKS
U_F = [0, 2 * F_CHUNKS + 2 * C_CHUNKS]

INV_FREQ = np.float32(THETA) ** (-np.arange(0, ROT, 2, dtype=np.float32) / np.float32(ROT))
ROUND = 1.5 * 2.0 ** 23
PI_IN = 3.1415925
C_ANGLES = 12


def parts_of(x, bits, n):
    out = []
    for _ in range(n):
        e = 2.0 ** (np.floor(np.log2(abs(x))) - bits + 1)
        out.append(np.round(x / e) * e)
        x -= out[-1]
    return out


TWO_PI = parts_of(2 * np.pi, 8, 4)


def pt_count(n, last):
    done = min(n, HKV) + 2 * max(n - HKV, 0)
    return done + (1 if n < HKV or not last else 2)


HEAD_GROUP = (0, 1, 2, None, 3)
HEAD_COLUMNS = (0, 0, 1, 2, 1)
HEADS_USED = (1, 2, 3, 5, 6)
ROUNDS = 6
ROUND_HEADS = (0, 1, 2, 3, 3, 4)
ROUND_TILE = (0, 1, 2, 4, 5, 3)
ROUND_ACT = (1, 4)


def round_count(b, i):
    mine = [r for r in range(ROUNDS) if (r in ROUND_ACT) == (i in ROUND_ACT)]
    return len(mine) * b + mine.index(i) + 1


def rounds_beside(s):
    b, g = s // HKV, s % HKV
    if s >= NBLK * HKV or (g and b + 1 == NBLK):
        return None, None
    return (((b, 5), None), ((b + 1, 0), (b + 1, 1)), ((b + 1, 2), None), ((b + 1, 3), (b + 1, 4)))[g]


O_SPLITS_HI = (NBLK * HKV - 2, NBLK * HKV - 1, NBLK * HKV)
O_SPLITS_LO = (NBLK * HKV - 2, NBLK * HKV - 1)


def heads_beside(s):
    b, g = s // HKV + 1, s % HKV
    if s < 0:
        return []
    return [(b, i) for i in ((0, 1), (2,), (3,), (4,))[g]] if b < NBLK else []


def out_count(b, q):
    return 2 * b + q + 1 if b < HB else (2 + q) * HB + (b - HB) + 1


def round_bank(b, i):
    return i if b == 0 and i < 5 else 4


def score_bank(n, j):
    return 1 + (2 * n + j // 2) % 3


def split_ahead(split, eng, ph, c, j):
    split(eng, ph, c, j + AHEAD)


G_MIX, G_FFN, G_CONV, G_ROWS = 0, 2 * KT, 4 * KT, 4 * KT + CW * KT


def decoder_kernel(nc, ctx, t, out):
    KB = 1024
    base = (nc.sbuf_base + 127) // 128 * 128

    def sb(name, shape, dt, kb):
        return nc.alloc_sbuf_tensor_at(name, [P] + shape, dt, offset=int(base + kb * KB))

    X = sb("X", [KT, S], F32, 0)
    H = sb("H", [2, KT, S], F32R, 32)
    STG = sb("STG", [4, PIECE], F32, 96)
    WR = sb("WR", [6, 2, PIECE], F32R, 112)
    A = sb("A", [2, 2, S], F32R, 160)
    SG = sb("SG", [2, HALF], F32, 176)
    A32 = sb("A32", [2, HALF], F32, 180)
    BG = sb("BG", [S], F32, 144)
    CG = sb("CG", [S], F32, 148)
    ZC = sb("ZC", [CW - 1 + S], F32, 152)
    YC = sb("YC", [HALF], F32, 157)
    XN = sb("XN", [NBLK, D], F32, 144)
    QKV = sb("QKV", [NBLK, QKVW], F32, 144)
    QS = sb("QS", [24, P], F32R, 96)
    QT = sb("QT", [HQ, P], F32R, 112)
    KTT = sb("KTT", [2, HKV, 2, P], F32R, 120)
    PR = sb("PR", [2, GRP, 2 * P], F32, 128)
    PT = sb("PT", [2, 2, GRP * P], F32, 136)
    OT = sb("OT", [2, GRP * HD], F32, 108)
    SQ = sb("SQ", [2, HALF], F32, 192)
    ACC = sb("ACC", [2, HALF], F32, 184)
    DG = sb("DG", [2, HALF], F32, 188)
    RS = sb("RS", [2, HALF], F32, 200)
    NS = sb("NS", [12], F32, 204)
    IDN = sb("IDN", [P], F32, 206)
    ONE = sb("ONE", [P], F32, 206.5)
    GT = sb("GT", [G_ROWS], F32, 207)
    ASQ = sb("ASQ", [2, HALF], F32, 192)
    COS = sb("COS", [NBLK, ROT], F32, 196)
    SIN = sb("SIN", [NBLK, ROT], F32, 196.5)
    MASK = sb("MASK", [3 * P], F32, 197)
    GBC = sb("GBC", [2 * HD + HQ], F32, 198.5)
    RT = sb("RT", [HALF // HD, ROT], F32, 199.125)
    RU = sb("RU", [HALF // HD, ROT], F32, 199.625)
    SSQ = sb("SSQ", [3, NBLK, HALF // HD], F32, 200.125)
    RR = sb("RR", [3, NBLK, HALF // HD], F32, 200.875)
    MH = sb("MH", [HALF // HD], F32, 201.625)
    TOK = sb("TOK", [2, NBLK], F32, 201.75)
    STAT = sb("STAT", [3, 5, GRP], F32, 205.625)
    ANG = sb("ANG", [2, 2, NBLK * ROT // 2], F32, 202.25)
    POST = sb("POST", [NBLK], F32, 203.25)
    INVF = sb("INVF", [ROT // 2], F32, 203.375)
    ROWS = sb("ROWS", [2 * HD + HQ], F32, 203.5)
    POSI = sb("POSI", [P], I32, 204.125)
    POSF = sb("POSF", [P], F32, 204.625)
    GRAW = sb("GRAW", [P], F32, 205.125)

    OUTB = sb("OUTB", [NBLK, D], F32, 32)

    PS = nc.alloc_psum_tensor("PS", [P, 8, HALF], F32)

    def sem(name):
        return ctx.enter_context(nc.semaphore(name))

    x_landed = [sem(f"x_landed{b}") for b in range(NBLK)]
    piece_landed = [sem(f"piece_landed{s}") for s in range(4)]
    w_hi = sem("w_hi")
    w_split = sem("w_split")
    w_used = sem("w_used")
    rows_landed = sem("rows_landed")
    pos_landed = sem("pos_landed")
    gains_landed = sem("gains_landed")
    idn_cleared = sem("idn_cleared")
    idn_ready = sem("idn_ready")
    one_ready = sem("one_ready")
    gt_ready = sem("gt_ready")
    const_on_psum = sem("const_on_psum")
    gbc_ready = sem("gbc_ready")
    pos_float = sem("pos_float")
    angle_inputs = sem("angle_inputs")
    angle_step = sem("angle_step")
    trig_ready = sem("trig_ready")
    mask_cleared = sem("mask_cleared")
    mask_ready = sem("mask_ready")
    x_turned = sem("x_turned")
    x_taken_act = sem("x_taken_act")
    x_taken_dve = sem("x_taken_dve")
    tok_squared = sem("tok_squared")
    tok_mean_ready = sem("tok_mean_ready")
    tok_rms_ready = sem("tok_rms_ready")
    norm_squared = sem("norm_squared")
    norm_added = sem("norm_added")
    norm_summed = sem("norm_summed")
    norm_mean_ready = sem("norm_mean_ready")
    norm_root_ready = sem("norm_root_ready")
    norm_diagonal_ready = sem("norm_diagonal_ready")
    norm_spread_done = sem("norm_spread_done")
    rs_ready = sem("rs_ready")
    h_hi = sem("h_hi")
    h_ready = sem("h_ready")
    exponent_ready = sem("exponent_ready")
    qkv_done = sem("qkv_done")
    qkv_taken_act = sem("qkv_taken_act")
    qkv_taken_dve = sem("qkv_taken_dve")
    head_squared = sem("head_squared")
    head_summed = sem("head_summed")
    head_mean_ready = sem("head_mean_ready")
    head_gained = sem("head_gained")
    head_root_ready = sem("head_root_ready")
    head_normed = sem("head_normed")
    rotation_terms = sem("rotation_terms")
    head_rotated = sem("head_rotated")
    qs_hi = sem("qs_hi")
    qs_ready = sem("qs_ready")
    round_done = sem("round_done")
    round_taken_act = sem("round_taken_act")
    round_taken_dve = sem("round_taken_dve")
    scores_done = sem("scores_done")
    scores_read = sem("scores_read")
    max_ready = sem("max_ready")
    exp_done = sem("exp_done")
    den_steps = sem("den_steps")
    probs_turned = sem("probs_turned")
    probs_taken = sem("probs_taken")
    values_done = sem("values_done")
    ot_ready = sem("ot_ready")
    out_turned = sem("out_turned")
    out_hi_ready = sem("out_hi_ready")
    out_ready = sem("out_ready")
    sum_product_done = sem("sum_product_done")
    add_done = sem("add_done")
    g_done = sem("g_done")
    u_done = sem("u_done")
    g_scaled = sem("g_scaled")
    silu_done = sem("silu_done")
    silu_scaled = sem("silu_scaled")
    mul_done = sem("mul_done")
    a_hi = sem("a_hi")
    a_ready = sem("a_ready")
    b_done = sem("b_done")
    c_done = sem("c_done")
    bc_copied = sem("bc_copied")
    bc_scaled = sem("bc_scaled")
    z_halo = sem("z_halo")
    z_done = sem("z_done")
    y_step = sem("y_step")
    y_done = sem("y_done")
    result_turned = sem("result_turned")
    result_left = sem("result_left")
    result_right = sem("result_right")
    stored = sem("stored")

    def round_target(b, i):
        r = ROUND_TILE[i]
        return QT[:, 4 * r:4 * r + 4, :] if r < 4 else KTT[:, r - 4, :, b % 2, :]

    def angle(i):
        return ANG[:, 0, i, :].rearrange("p (b f) -> p b f", b=NBLK)

    def half(h):
        return slice(h * HALF, (h + 1) * HALF)

    def blk(b):
        return slice(b * P, (b + 1) * P)

    w_qkv, w_o = t["a_w_qkv"][0], t["a_w_o"][0]
    w_gu, w_dn = t["f_w_gate_up"], t["f_w_down"]
    w_in, w_out = t["b_w_in"][0], t["b_w_out"][0]
    x_dram, out_dram = t["x"][0], out[0]

    def sync_program(sp):
        def load(ph, c, j, src, cols=None):
            p = ph.piece(c, j)
            if not isinstance(p, int) or p >= AHEAD:
                sp.wait_ge(w_split, p + (1 - AHEAD))
            dst = STG[:, ph.stage(j), :]
            if cols:
                dst = dst.rearrange("p (k n) -> p k n", n=cols)
            sp.dma_start(dst, src).then_inc(piece_landed[ph.stage(j)], 16)

        def columns(w, at, n):
            return w[:, bass.ds(at, n)].rearrange("(k p) n -> p k n", p=P)

        def load_q(c, j):
            rows = w_qkv[j * 2 * P:(j + 1) * 2 * P, c * HALF:(c + 1) * HALF]
            load(PH_Q, c, j, rows.rearrange("(k p) n -> p k n", p=P), HALF)

        for b in range(NBLK):
            sp.dma_start(XN[:, b, :], x_dram[blk(b), :]).then_inc(x_landed[b], 16)
            if b == 1:
                sp.dma_start(GRAW[0:2 * KT, :],
                             t["mix_norm"].rearrange("l (k p) -> (l k) p", p=P)).then_inc(gains_landed, 16)
                sp.dma_start(GRAW[G_FFN:G_CONV, :],
                             t["ffn_norm"].rearrange("l (k p) -> (l k) p", p=P)).then_inc(gains_landed, 16)
                sp.dma_start(GRAW[G_CONV:G_ROWS, :],
                             t["b_conv_w"][0].rearrange("l (k p) -> (l k) p", p=P)).then_inc(gains_landed, 16)
                sp.dma_start(POSI[0:NBLK, :], t["positions"][0].rearrange("(b p) -> b p", p=P)).then_inc(pos_landed, 16)
                sp.dma_start(ROWS[0:1, 0:HD], t["a_q_norm"]).then_inc(rows_landed, 16)
                sp.dma_start(ROWS[0:1, HD:2 * HD], t["a_k_norm"]).then_inc(rows_landed, 16)
                sp.dma_start(ROWS[0:1, 2 * HD:2 * HD + HQ], t["a_sinks"]).then_inc(rows_landed, 16)
            if b == HB - 1:
                for j in range(AHEAD):
                    load_q(0, j)
        for n in range(AHEAD, Q_PIECES):
            load_q(n // 4, n % 4)
        sp.wait_ge(round_done, 6 * NBLK)
        for n in range(O_PIECES):
            if n == AHEAD:
                sp.wait_ge(out_turned, NBLK * HKV)
            load(PH_O, n // 4, n % 4, w_o[n * P:(n + 1) * P, :])

        def load_ffn(l):
            with sp.Fori(0, F_CHUNKS) as c:
                for j in range(2):
                    load(PH_F[l], c, 2 * j, columns(w_gu[l], c * (2 * P) + j * P, P), P)
                    load(PH_F[l], c, 2 * j + 1, columns(w_gu[l], c * (2 * P) + (FF + j * P), P), P)
                for j in range(2):
                    load(PH_F[l], c, 4 + j, w_dn[l][bass.ds(c * (2 * P) + j * P, P), :])

        load_ffn(0)
        with sp.Fori(0, C_CHUNKS) as c:
            for j in range(2):
                for i in range(3):
                    load(PH_C, c, 3 * j + i, columns(w_in, c * (2 * P) + (i * D + j * P), P), P)
            for j in range(2):
                load(PH_C, c, 6 + j, w_out[bass.ds(c * (2 * P) + j * P, P), :])
        load_ffn(1)
        for b in range(HB):
            sp.wait_ge(result_left, b + 1)
            sp.wait_ge(result_right, b + 1)
            sp.dma_start(out_dram[blk(b), :], OUTB[:, b, :]).then_inc(stored, 16)
        for q, taken in enumerate((result_left, result_right)):
            for b in range(HB, NBLK):
                sp.wait_ge(taken, b + 1)
                sp.dma_start(out_dram[blk(b), half(q)], OUTB[:, b, half(q)]).then_inc(stored, 16)
        sp.wait_ge(stored, 16 * (HB + 2 * (NBLK - HB)))

    def split_hi(act, ph, c, j):
        p = ph.piece(c, j)
        act.wait_ge(piece_landed[ph.stage(j)], ph.arrival(c, j))
        back = 4 if isinstance(c, int) and c == 0 and j < 6 else ph.ring
        if not isinstance(p, int) or p >= back:
            act.wait_ge(w_used, p - (back - 1))
        nc.scalar.activation(WR[:, ph.slot(j), 0, :], STG[:, ph.stage(j), :], ACT.Copy).then_inc(w_hi, 1)

    def split_lo(dve, ph, c, j):
        dve.wait_ge(w_hi, ph.piece(c, j) + 1)
        nc.vector.tensor_tensor(WR[:, ph.slot(j), 1, :], STG[:, ph.stage(j), :],
                                WR[:, ph.slot(j), 0, :].bitcast(F32), ALU.subtract).then_inc(w_split, 1)

    def gain(n, k):
        at = (G_FFN if n % 2 else G_MIX) + (n // 2) * KT + k
        return GT[:, at:at + 1]

    def operand_hi(act, n, h, k):
        nc.scalar.activation(H[:, 0, k, half(h)], X[:, k, half(h)], ACT.Copy, scale=gain(n, k)).then_inc(h_hi, 1)

    def operand_lo(dve, n, h, k):
        dve.wait_ge(h_hi, KT * (2 * n + h) + k + 1)
        nc.vector.scalar_tensor_tensor(H[:, 1, k, half(h)], X[:, k, half(h)], gain(n, k),
                                       H[:, 0, k, half(h)].bitcast(F32), ALU.mult, ALU.subtract).then_inc(h_ready, 1)

    def norm_square(act, n, h, m):
        i = 2 * (n - 1) + h
        if m == 0:
            if i >= 2:
                act.wait_ge(norm_summed, i - 1)
            nc.scalar.activation(ACC[:, h, :], X[:, m, half(h)], ACT.Square).then_inc(norm_squared, 1)
        else:
            slot = 7 * i + m - 1
            if slot >= 2:
                act.wait_ge(norm_added, slot - 1)
            nc.scalar.activation(SQ[:, slot % 2, :], X[:, m, half(h)], ACT.Square).then_inc(norm_squared, 1)

    def norm_accumulate(pool, n, h):
        i = 2 * (n - 1) + h
        for m in range(1, KT):
            pool.wait_ge(norm_squared, KT * i + m + 1)
            if m > 1:
                pool.wait_ge(norm_added, 7 * i + m - 1)
            nc.gpsimd.tensor_tensor(ACC[:, h, :], ACC[:, h, :], SQ[:, (7 * i + m - 1) % 2, :],
                                    ALU.add).then_inc(norm_added, 1)

    def norm_root(pool, n, h):
        pool.wait_ge(norm_mean_ready, 2 * (n - 1) + h + 1)
        nc.gpsimd.tensor_tensor(NS[:, 4:8], NS[:, 0:4], NS[:, 8:12], ALU.pow).then_inc(norm_root_ready, 1)

    def norm_sum(pe, n, h):
        i = 2 * (n - 1) + h
        pe.wait_ge(norm_added, 7 * (i + 1))
        if i:
            pe.wait_ge(norm_mean_ready, i)
        for j in range(HB):
            mm = nc.tensor.matmul(PS[:, 6, j:j + 1], ACC[:, h, blk(j)], ONE[:, 0:1], start=True, stop=True)
        mm.then_inc(norm_summed, 1)

    def norm_mean(dve, n, h):
        i = 2 * (n - 1) + h
        dve.wait_ge(norm_summed, i + 1)
        if i:
            dve.wait_ge(norm_root_ready, i)
        nc.vector.tensor_scalar(NS[:, 0:4], PS[:, 6, 0:4], 1.0 / D, EPS, ALU.mult, ALU.add).then_inc(norm_mean_ready, 1)

    def norm_diagonal(dve, n, h):
        i = 2 * (n - 1) + h
        dve.wait_ge(norm_root_ready, i + 1)
        if i >= 2:
            dve.wait_ge(norm_spread_done, i - 1)
        for j in range(HB):
            v = nc.vector.tensor_scalar(DG[:, h, blk(j)], IDN[:], NS[:, 4 + j:5 + j], None, ALU.mult)
        v.then_inc(norm_diagonal_ready, 1)

    def norm_spread(pe, n, h):
        i = 2 * (n - 1) + h
        pe.wait_ge(norm_diagonal_ready, i + 1)
        if i:
            pe.wait_ge(rs_ready, i)
        nc.tensor.matmul(PS[:, 7, :], ONE[:], DG[:, h, :], start=True, stop=True).then_inc(norm_spread_done, 1)

    def norm_take(act, n, h):
        act.wait_ge(norm_spread_done, 2 * (n - 1) + h + 1)
        nc.scalar.activation(RS[:, h, :], PS[:, 7, :], ACT.Copy).then_inc(rs_ready, 1)

    PASSES = ((0, 0), (0, 1), (1, 0))

    def tensor_program(pe):
        def constants():
            pe.wait_ge(one_ready, 1)
            pe.wait_ge(gains_landed, 48)
            nc.tensor.transpose(PS[:, 3, 0:G_ROWS], GRAW[0:G_ROWS, :],
                                IDN[0:G_ROWS, 0:G_ROWS]).then_inc(const_on_psum, 1)
            pe.wait_ge(pos_float, 1)
            nc.tensor.transpose(PS[:, 2, 0:NBLK], POSF[0:NBLK, :], IDN[0:NBLK, 0:NBLK]).then_inc(const_on_psum, 1)
            pe.wait_ge(rows_landed, 48)
            nc.tensor.matmul(PS[:, 1, 0:2 * HD + HQ], ONE[0:1, :], ROWS[0:1, :], start=True,
                             stop=True).then_inc(const_on_psum, 1)

        def transpose_x(b):
            pe.wait_ge(x_landed[b], 16)
            for q in range(2):
                i = 2 * b + q
                if i >= 4:
                    pe.wait_ge(x_taken_dve if q else x_taken_act, i // 2 - 1)
                for j in range(4):
                    mm = nc.tensor.transpose(PS[:, 4 + i % 4, blk(j)], XN[:, b, blk(4 * q + j)], IDN[:])
                mm.then_inc(x_turned, 1)

        pe.wait_ge(idn_ready, 1)
        for b in range(HB):
            transpose_x(b)
            if b == 1:
                constants()
        pe.wait_ge(gbc_ready, 2)

        def columns_copied(c, b):
            pe.wait_ge(qkv_taken_dve if b % 2 else qkv_taken_act, c * 4 + b // 2 + 1)

        def qkv_product(c, kp, b, normed=None):
            for k in (2 * kp, 2 * kp + 1):
                if normed is not None:
                    pe.wait_ge(h_ready, normed + k + 1)
                for w, a in PASSES:
                    mm = nc.tensor.matmul(
                        PS[:, b, :], H[:, a, k, blk(b)],
                        WR[:, PH_Q.slot(kp), w, (k % 2) * HALF:(k % 2 + 1) * HALF],
                        start=(k == 0 and (w, a) == (0, 0)), stop=(k == KT - 1 and (w, a) == (1, 0)))
            if b == NBLK - 1:
                mm.then_inc(w_used, 1)
            elif kp == 3:
                mm.then_inc(qkv_done, 1)

        last = QKVW // HALF - 1
        for c in range(last):
            for h in range(2):
                for kp in range(4):
                    if h == 0:
                        pe.wait_ge(w_split, PH_Q.piece(c, kp) + 1)
                    if (c, h, kp) == (0, 1, 0):
                        pe.wait_ge(x_taken_act, NBLK)
                        pe.wait_ge(x_taken_dve, NBLK)
                    for b in range(h * HB, (h + 1) * HB):
                        if c and kp == 0:
                            columns_copied(c - 1, b)
                        qkv_product(c, kp, b, normed=KT * h if c == 0 and b % HB == 0 else None)
                    if (c, h) == (0, 0) and kp < 2:
                        transpose_x(HB + 2 * kp)
                        transpose_x(HB + 2 * kp + 1)

        def round_trip(b, i):
            pe.wait_ge(qs_ready, 5 * b + ROUND_HEADS[i] + 1)
            if b == 0 and i < 5:
                columns_copied(last, i)
            else:
                at, before = (b, i - 1) if i else (b - 1, ROUNDS - 1)
                pe.wait_ge(round_taken_act if before in ROUND_ACT else round_taken_dve, round_count(at, before))
            for j in range(4):
                mm = nc.tensor.transpose(PS[:, round_bank(b, i), blk(j)],
                                         QS[:, 4 * ROUND_TILE[i] + j, :].bitcast(F32), IDN[:])
            mm.then_inc(round_done, 1)

        for b in range(NBLK):
            if b == NBLK - 1:
                for i in range(ROUNDS - 1):
                    round_trip(0, i)
            columns_copied(last - 1, b)
            for kp in range(4):
                if b == 0:
                    pe.wait_ge(w_split, PH_Q.piece(last, kp) + 1)
                qkv_product(last, kp, b)

        def scores(n):
            b, g = n // HKV, n % HKV
            width = P if b == 0 else 2 * P
            for i in ((0, 1, 2, 3, 4), (), (), (5,))[g] if b == 0 else ((0, 3, 4), (1,), (2,), (5,))[g]:
                pe.wait_ge(round_taken_act if i in ROUND_ACT else round_taken_dve, round_count(b, i))
            for j in range(GRP):
                if j % 2 == 0 and 4 * n + j >= 6:
                    pe.wait_ge(scores_read, 4 * n + j - 4)
                dst = PS[:, score_bank(n, j), (j % 2) * 2 * P:(j % 2) * 2 * P + width]
                for part in range(2):
                    k = KTT[:, part, g, :, :].rearrange("p s n -> p (s n)")[:, 0:width]
                    mm = nc.tensor.matmul(dst, QT[:, GRP * g + j, :], k, start=(part == 0), stop=(part == 1))
            mm.then_inc(scores_done, 1)

        def slots(b):
            return (0,) if b == 0 else (0, 1)

        def probs_transposed(n):
            pe.wait_ge(exp_done, n + 1)
            for s in slots(n // HKV):
                if n > (HKV - 1 if s else 0):
                    pe.wait_ge(probs_taken, pt_count(n - 1, s))
                for j in range(GRP):
                    mm = nc.tensor.transpose(PS[:, 5 + s, blk(j)], PR[:, n % 2, j, blk(s)], IDN[:])
                mm.then_inc(probs_turned, 1)

        def values(n):
            b, g = n // HKV, n % HKV
            pe.wait_ge(probs_taken, pt_count(n, 1))
            if n:
                pe.wait_ge(ot_ready, n)
            for j in range(GRP):
                for s in slots(b):
                    of = b if s == b % 2 else b - 1
                    mm = nc.tensor.matmul(PS[:, 7, HD * j:HD * (j + 1)], PT[:, n % 2, s, blk(j)],
                                          QKV[:, of, QKW + HD * g:QKW + HD * (g + 1)],
                                          start=(s == 0), stop=(s == slots(b)[-1]))
            mm.then_inc(values_done, 1)

        def out_transposed(n):
            pe.wait_ge(ot_ready, n + 1)
            if n:
                pe.wait_ge(out_ready, n)
            for j in range(2):
                mm = nc.tensor.transpose(PS[:, 0, blk(j)], OT[:, n % 2, blk(j)], IDN[:])
            mm.then_inc(out_turned, 1)

        def add_product(ph, c, j0, d0, h, m, operand):
            i = HB * 2 * h + m
            d = c * 16 + (d0 + i)
            if not (isinstance(d, int) and d < 2):
                pe.wait_ge(add_done, d - 1)
            for j in range(2):
                for w, a in PASSES:
                    mm = nc.tensor.matmul(PS[:, 4 + i % 2, :], WR[:, ph.slot(j0 + j), w, blk(m)],
                                          operand(j, a, h), start=(j == 0 and (w, a) == (0, 0)),
                                          stop=(j == 1 and (w, a) == (1, 0)))
            if i == 15:
                mm.then_inc(w_used, 2)
            else:
                mm.then_inc(sum_product_done, 1)

        def o_product(c, h, m):
            add_product(PH_O, 0, 2 * c, D_O + 16 * c, h, m, lambda j, a, h: H[:, a, 2 * c + j, half(h)])

        n_groups = NBLK * HKV
        for n in range(-2, n_groups + 2):
            if n == 0:
                pe.wait_ge(qkv_taken_act, 4 * (last + 1))
                pe.wait_ge(qkv_taken_dve, 4 * (last + 1))
            if 0 <= n < n_groups:
                probs_transposed(n)
            if n == n_groups + 1:
                pe.wait_ge(w_split, PH_O.piece(0, 1) + 1)
                pe.wait_ge(out_ready, n_groups // 2)
                for m in range(2):
                    o_product(0, 0, m)
            if n >= 2:
                out_transposed(n - 2)
            if n + 2 < n_groups:
                scores(n + 2)
            first, second = rounds_beside(n + 2)
            if first:
                round_trip(*first)
            if 0 <= n < n_groups:
                values(n)
            if second:
                round_trip(*second)

        def inner(j, a, h):
            return A[:, j, a, half(h)]

        def add_products(ph, c, j0, d0, tiles, norm=None, last=False):
            pe.wait_ge(w_split, ph.piece(c, j0 + 1) + 1)
            for h in range(2):
                pe.wait_ge(a_ready, c * 4 + (2 * tiles + 3 + h))
                for m in range(KT):
                    add_product(ph, c, j0, d0, h, m, inner)
                    if last and h == 1:
                        if m < HB:
                            transpose_out(m, 0)
                            transpose_out(m, 1)
                        else:
                            transpose_out(m, 0)
            if norm is not None:
                norm_sum(pe, norm, 0)

        def transpose_out(b, q):
            sums = 16 * F_CHUNKS - (8 if b < HB else 4 if q == 0 else 0)
            pe.wait_ge(add_done, D_F1 + sums)
            if b < 2:
                pe.wait_ge(mul_done, 2 * (T_F[1] + 2 * F_CHUNKS))
            else:
                pe.wait_ge(result_right if q else result_left, b - 1)
            for j in range(4):
                mm = nc.tensor.transpose(PS[:, (2 * b + q) % 4, blk(j)], X[:, 4 * q + j, blk(b)], IDN[:])
            mm.then_inc(result_turned, 1)

        for c in range(4):
            pe.wait_ge(w_split, PH_O.piece(0, 2 * c + 1) + 1)
            for h in range(2):
                if (c, h) == (0, 1):
                    pe.wait_ge(out_ready, n_groups)
                for m in range(2 if (c, h) == (0, 0) else 0, KT):
                    o_product(c, h, m)
        norm_sum(pe, 1, 0)

        def product(ph, c, j, h, bank, done, norm=None):
            for k in range(KT):
                if norm is not None:
                    pe.wait_ge(h_ready, KT * (2 * norm + h) + k + 1)
                for w, a in PASSES:
                    mm = nc.tensor.matmul(PS[:, bank, :], WR[:, ph.slot(j), w, blk(k)], H[:, a, k, half(h)],
                                          start=(k == 0 and (w, a) == (0, 0)), stop=(k == KT - 1 and (w, a) == (1, 0)))
            mm.then_inc(*((done, 1) if h == 0 else (w_used, 1)))

        def norm_beside(norm, i, h):
            if (i, h) == (0, 0):
                norm_sum(pe, norm, 1)
            if (i, h) == (1, 0):
                norm_spread(pe, norm, 0)
            if (i, h) == (0, 1):
                norm_spread(pe, norm, 1)

        def gate_up(l, c, norm=None):
            ph = PH_F[l]
            for j in range(2):
                order = [(u, h) for u in range(2) for h in range(2)]
                first = norm is not None and j == 0
                if first:
                    order = [(u, h) for h in range(2) for u in range(2)]
                for u, h in order:
                    if h == 0:
                        pe.wait_ge(w_split, ph.piece(c, 2 * j + u) + 1)
                    tile = c * 2 + (T_F[l] + j)
                    if not isinstance(tile, int) or tile:
                        pe.wait_ge(mul_done if u else silu_done, c * 4 + (2 * (T_F[l] + j) + h - 1))
                    product(ph, c, 2 * j + u, h, 2 * u + h, u_done if u else g_done, norm if first and u == 0 else None)
                    if first:
                        norm_beside(norm, u, h)

        def ffn(l, norm, last_norm):
            gate_up(l, 0, norm)
            add_products(PH_F[l], 0, 4, D_F[l], A_F[l])
            with pe.Fori(1, F_CHUNKS - 1) as c:
                gate_up(l, c)
                add_products(PH_F[l], c, 4, D_F[l], A_F[l])
            gate_up(l, F_CHUNKS - 1)
            add_products(PH_F[l], F_CHUNKS - 1, 4, D_F[l], A_F[l], last_norm, last=l == 1)

        ffn(0, 1, 2)

        def gated(c, norm=None):
            for j in range(2):
                order = [(i, h) for i in range(3) for h in range(2)]
                first = norm is not None and j == 0
                if first:
                    order = [(i, h) for h in range(2) for i in range(2)] + [(2, 0), (2, 1)]
                for i, h in order:
                    if h == 0:
                        pe.wait_ge(w_split, PH_C.piece(c, 3 * j + i) + 1)
                    start = not isinstance(c, int) or c > 0 or j > 0
                    if i == 2:
                        pe.wait_ge(bc_copied, c * 8 + (4 * j + h + 1))
                    elif i == 1 and start:
                        pe.wait_ge(bc_copied, c * 8 + (4 * j + h - 1))
                    elif start:
                        pe.wait_ge(z_done, c * 4 + (2 * j + h - 1))
                    product(PH_C, c, 3 * j + i, h, (0, 2, 0)[i] + h, (b_done, c_done, u_done)[i],
                            norm if first and i == 0 else None)
                    if first:
                        norm_beside(norm, i, h)

        gated(0, 2)
        add_products(PH_C, 0, 6, D_C, A_C)
        with pe.Fori(1, C_CHUNKS - 1) as c:
            gated(c)
            add_products(PH_C, c, 6, D_C, A_C)
        gated(C_CHUNKS - 1)
        add_products(PH_C, C_CHUNKS - 1, 6, D_C, A_C, 3)

        ffn(1, 3, None)

        for b in range(HB, NBLK):
            transpose_out(b, 1)

    def scalar_program(act):
        def take_x(b):
            act.wait_ge(x_turned, 2 * b + 1)
            nc.scalar.activation(X[:, 0:4, blk(b)], PS[:, 4 + (2 * b) % 4, :].rearrange("p (k n) -> p k n", n=P),
                                 ACT.Copy).then_inc(x_taken_act, 1)

        for b in range(HB):
            take_x(b)
        split_hi(act, PH_Q, 0, 0)
        act.wait_ge(gt_ready, 1)
        act.wait_ge(x_taken_dve, HB)
        act.wait_ge(x_taken_act, HB)
        for k in range(4):
            operand_hi(act, 0, 0, k)
        split_hi(act, PH_Q, 0, 1)
        for k in range(4, KT):
            operand_hi(act, 0, 0, k)
        for b in range(HB, NBLK):
            take_x(b)
            if b == HB + 1:
                split_hi(act, PH_Q, 0, 2)
        split_hi(act, PH_Q, 0, 3)
        act.wait_ge(x_taken_dve, NBLK)
        act.wait_ge(x_taken_act, NBLK)
        for k in range(KT):
            operand_hi(act, 0, 1, k)
        for b in range(NBLK):
            act.wait_ge(x_landed[b], 16)
            if b:
                act.wait_ge(tok_squared, b)
            nc.scalar.activation(ASQ[:], XN[:, b, :].rearrange("p (j n) -> p j n", j=2), ACT.Square,
                                 accum_out=TOK[:, 0, b:b + 1]).then_inc(tok_squared, 1)

        act.wait_ge(angle_step, C_ANGLES)
        nc.scalar.activation(SIN[:, :, 0:ROT // 2], angle(0), ACT.Sin, scale=-1.0).then_inc(trig_ready, 1)
        nc.scalar.activation(SIN[:, :, ROT // 2:ROT], angle(0), ACT.Sin).then_inc(trig_ready, 1)
        nc.scalar.activation(COS[:, :, 0:ROT // 2], angle(1), ACT.Sin).then_inc(trig_ready, 1)
        nc.scalar.activation(COS[:, :, ROT // 2:ROT], angle(1), ACT.Sin).then_inc(trig_ready, 1)

        def take_qkv(c, b):
            act.wait_ge(qkv_done, c * 7 + (b + 1))
            if c == 0 and b == 0:
                act.wait_ge(tok_rms_ready, 1)
            nc.scalar.activation(QKV[:, b, c * HALF:(c + 1) * HALF], PS[:, b, :], ACT.Copy,
                                 scale=TOK[:, 1, b:b + 1]).then_inc(qkv_taken_act, 1)

        def square_heads(c, b):
            i = NBLK * c + b
            w = HALF if c < 2 else HKV * HD
            if b % 2:
                act.wait_ge(qkv_taken_dve, 4 * c + b // 2 + 1)
            else:
                act.wait_ge(qkv_taken_act, 4 * c + b // 2 + 1)
            if i >= 2:
                act.wait_ge(head_summed, i - 1)
            nc.scalar.activation(ASQ[:, i % 2, 0:w], QKV[:, b, HALF * c:HALF * c + w],
                                 ACT.Square).then_inc(head_squared, 1)

        for c in range(2):
            for h in range(2):
                if h:
                    for j in range(1, 5):
                        split_ahead(split_hi, act, PH_Q, c, j)
                for b in range(HB * h, HB * (h + 1), 2):
                    take_qkv(c, b)
                for b in range(HB * h, HB * (h + 1)):
                    square_heads(c, b)
        for b in range(0, NBLK, 2):
            take_qkv(2, b)
            square_heads(2, b)
            if b + 1 < NBLK - 1:
                square_heads(2, b + 1)

        def take_round(b, i):
            act.wait_ge(round_done, ROUNDS * b + i + 1)
            nc.scalar.activation(round_target(b, i), PS[:, round_bank(b, i), :].rearrange("p (j n) -> p j n", n=P),
                                 ACT.Copy).then_inc(round_taken_act, 1)

        def exponentials(n):
            w = P if n < HKV else 2 * P
            act.wait_ge(max_ready, n + 1)
            for j in range(GRP):
                nc.scalar.activation(PR[:, n % 2, j, 0:w], PR[:, n % 2, j, 0:w], ACT.Exp, scale=-1.0,
                                     bias=STAT[:, n % 3, 0, j:j + 1], accum_out=STAT[:, n % 3, 2, j:j + 1])
            nc.scalar.activation(STAT[:, n % 3, 3, :], STAT[:, n % 3, 1, :], ACT.Exp).then_inc(exp_done, 1)

        def take_probs(n):
            for s in ((0,) if n < HKV else (0, 1)):
                act.wait_ge(probs_turned, pt_count(n, s))
                if n >= 2:
                    act.wait_ge(values_done, n - 1)
                nc.scalar.activation(PT[:, n % 2, s, :], PS[:, 5 + s, :], ACT.Copy).then_inc(probs_taken, 1)

        def out_hi(n):
            b, g = n // HKV, n % HKV
            act.wait_ge(out_turned, n + 1)
            nc.scalar.activation(H[:, 0, 2 * g:2 * g + 2, blk(b)], PS[:, 0, 0:2 * P].rearrange("p (k n) -> p k n", n=P),
                                 ACT.Copy).then_inc(out_hi_ready, 1)

        n_groups = NBLK * HKV
        act.wait_ge(w_used, Q_PIECES)
        for i in ROUND_ACT:
            take_round(0, i)
        square_heads(2, NBLK - 1)
        for n in range(-2, n_groups + 2):
            if 0 <= n < n_groups:
                take_probs(n)
            if n >= 2:
                out_hi(n - 2)
            if 0 <= n + 1 < n_groups:
                exponentials(n + 1)
            for r in rounds_beside(n + 2):
                if r and r[1] in ROUND_ACT:
                    take_round(*r)
            if n in O_SPLITS_HI:
                split_hi(act, PH_O, 0, O_SPLITS_HI.index(n))

        def finished(norm, h, d0):
            for m in range(KT):
                act.wait_ge(add_done, d0 + KT * h + (KT if norm == 1 and m >= KT - 2 else m + 1))
                operand_hi(act, norm, h, m)
                norm_square(act, norm, h, m)

        for c in range(4):
            split_ahead(split_hi, act, PH_O, 0, 2 * c)
            if c == 3:
                finished(1, 0, D_O + 48)
            if c < 3:
                split_ahead(split_hi, act, PH_O, 0, 2 * c + 1)
        finished(1, 1, D_O + 48)
        split_ahead(split_hi, act, PH_O, 0, 7)
        norm_take(act, 1, 0)
        norm_take(act, 1, 1)

        def silu(l, c, j, h):
            i = c * 4 + (2 * (T_F[l] + j) + h)
            act.wait_ge(g_scaled, i + 1)
            if not isinstance(i, int) or i >= 2:
                act.wait_ge(mul_done, i - 1)
            nc.scalar.activation(SG[:, h, :], PS[:, h, :], ACT.Silu).then_inc(silu_done, 1)

        def inner_hi_of(c, j, h, done, first):
            act.wait_ge(done, c * 4 + (first + 2 * j + h + 1))
            nc.scalar.activation(A[:, j, 0, half(h)], A32[:, h, :], ACT.Copy).then_inc(a_hi, 1)

        def ffn_chunk(l, c, norm=None, ahead=True):
            ph = PH_F[l]
            for j in range(2):
                split_ahead(split_hi, act, ph, c, 2 * j)
                silu(l, c, j, 0)
                silu(l, c, j, 1)
                if ahead or j == 0:
                    split_ahead(split_hi, act, ph, c, 2 * j + 1)
                inner_hi_of(c, j, 0, mul_done, 2 * T_F[l])
                inner_hi_of(c, j, 1, mul_done, 2 * T_F[l])
            if ahead:
                split_ahead(split_hi, act, ph, c, 4)
            if norm is not None:
                finished(norm, 0, D_F[l] + 16 * c)
                finished(norm, 1, D_F[l] + 16 * c)
            if ahead:
                split_ahead(split_hi, act, ph, c, 5)
            if norm is not None:
                norm_take(act, norm, 0)
                norm_take(act, norm, 1)

        ffn_chunk(0, 0)
        with act.Fori(1, F_CHUNKS - 1) as c:
            ffn_chunk(0, c)
        ffn_chunk(0, F_CHUNKS - 1, norm=2)

        def copy_gate(c, j, i, h):
            if h == 0:
                act.wait_ge((b_done, c_done)[i], c * 2 + (j + 1))
            else:
                act.wait_ge(w_used, PH_C.piece(c, 3 * j + i) + 1)
            act.wait_ge(a_ready, c * 4 + (2 * (A_C + j) + h - 1))
            nc.scalar.activation((BG, CG)[i][:, half(h)], PS[:, 2 * i + h, :], ACT.Copy).then_inc(bc_copied, 1)

        def conv_chunk(c, norm=None):
            for j in range(2):
                for i in range(2):
                    split_ahead(split_hi, act, PH_C, c, 3 * j + i)
                    copy_gate(c, j, i, 0)
                    copy_gate(c, j, i, 1)
                split_ahead(split_hi, act, PH_C, c, 3 * j + 2)
                inner_hi_of(c, j, 0, y_done, 0)
                inner_hi_of(c, j, 1, y_done, 0)
            split_ahead(split_hi, act, PH_C, c, 6)
            if norm is not None:
                finished(norm, 0, D_C + 16 * c)
                finished(norm, 1, D_C + 16 * c)
            split_ahead(split_hi, act, PH_C, c, 7)
            if norm is not None:
                norm_take(act, norm, 0)
                norm_take(act, norm, 1)

        with act.Fori(0, C_CHUNKS - 1) as c:
            conv_chunk(c)
        conv_chunk(C_CHUNKS - 1, norm=3)
        ffn_chunk(1, 0)
        with act.Fori(1, F_CHUNKS - 1) as c:
            ffn_chunk(1, c)
        ffn_chunk(1, F_CHUNKS - 1, ahead=False)
        for b in range(NBLK):
            act.wait_ge(result_turned, out_count(b, 0))
            nc.scalar.activation(OUTB[:, b, 0:HALF], PS[:, (2 * b) % 4, :], ACT.Copy).then_inc(result_left, 1)

    def vector_program(dve):
        nc.vector.memset(ONE[:], 1.0).then_inc(one_ready, 1)
        for f in range(ROT // 2):
            nc.vector.memset(INVF[:, f:f + 1], float(INV_FREQ[f])).then_inc(angle_inputs, 1)

        def take_x(b):
            dve.wait_ge(x_turned, 2 * b + 2)
            nc.vector.tensor_copy(X[:, 4:8, blk(b)],
                                  PS[:, 4 + (2 * b + 1) % 4, :].rearrange("p (k n) -> p k n",
                                             n=P)).then_inc(x_taken_dve, 1)

        take_x(0)
        dve.wait_ge(pos_landed, 16)
        nc.vector.tensor_copy(POSF[0:NBLK, :], POSI[0:NBLK, :]).then_inc(pos_float, 1)
        take_x(1)
        dve.wait_ge(const_on_psum, 3)
        nc.vector.tensor_copy(GT[:], PS[:, 3, 0:G_ROWS]).then_inc(gt_ready, 1)
        nc.vector.tensor_copy(POST[:], PS[:, 2, 0:NBLK]).then_inc(angle_inputs, 1)
        nc.vector.tensor_copy(GBC[:, 0:2 * HD], PS[:, 1, 0:2 * HD]).then_inc(gbc_ready, 1)
        nc.vector.tensor_scalar(GBC[:, 2 * HD:2 * HD + HQ], PS[:, 1, 2 * HD:2 * HD + HQ], -1.0, None,
                                ALU.mult).then_inc(gbc_ready, 1)
        for b in range(2, HB):
            take_x(b)
        split_lo(dve, PH_Q, 0, 0)
        dve.wait_ge(gt_ready, 1)
        for k in range(4):
            operand_lo(dve, 0, 0, k)
        split_lo(dve, PH_Q, 0, 1)
        for k in range(4, KT):
            operand_lo(dve, 0, 0, k)
        for b in range(HB, NBLK):
            take_x(b)
            if b == HB + 1:
                split_lo(dve, PH_Q, 0, 2)
        split_lo(dve, PH_Q, 0, 3)
        for k in range(KT):
            operand_lo(dve, 0, 1, k)

        count = [0]

        def step(v):
            v.then_inc(angle_step, 1)
            count[0] += 1
            dve.wait_ge(angle_step, count[0])

        def tile(i):
            return ANG[:, i, :, :]

        dve.wait_ge(angle_inputs, ROT // 2 + 1)
        pos = POST[:].unsqueeze(2).broadcast_to([P, NBLK, ROT // 2])
        inv = INVF[:].unsqueeze(1).broadcast_to([P, NBLK, ROT // 2])
        for i in range(2):
            step(nc.vector.tensor_tensor(angle(i), pos, inv, ALU.mult))
        for i in range(2):
            step(nc.vector.tensor_scalar(ANG[:, 1, i, :], ANG[:, 0, i, :], 1 / (2 * np.pi), 0.25 * i,
                                         ALU.mult, ALU.add))
        step(nc.vector.tensor_scalar(tile(1), tile(1), ROUND, None, ALU.add))
        step(nc.vector.tensor_scalar(tile(1), tile(1), -ROUND, None, ALU.add))
        for part in TWO_PI:
            step(nc.vector.scalar_tensor_tensor(tile(0), tile(1), -float(part), tile(0), ALU.mult, ALU.add))
        step(nc.vector.tensor_scalar(ANG[:, 0, 1, :], ANG[:, 0, 1, :], float(np.float32(np.pi / 2)), None, ALU.add))
        step(nc.vector.tensor_scalar(tile(0), tile(0), PI_IN, -PI_IN, ALU.min, ALU.max))
        assert count[0] == C_ANGLES
        dve.wait_ge(tok_squared, NBLK)
        nc.vector.tensor_scalar(TOK[:, 0, :], TOK[:, 0, :], 1.0 / D, EPS, ALU.mult, ALU.add).then_inc(tok_mean_ready, 1)
        dve.wait_ge(tok_rms_ready, 1)

        def take_qkv(c, b):
            if b == NBLK - 1:
                dve.wait_ge(w_used, 4 * c + 4)
            else:
                dve.wait_ge(qkv_done, c * 7 + (b + 1))
            nc.vector.tensor_scalar(QKV[:, b, c * HALF:(c + 1) * HALF], PS[:, b, :], TOK[:, 1, b:b + 1], None,
                                    ALU.mult).then_inc(qkv_taken_dve, 1)

        def mean_heads(c, b):
            i = NBLK * c + b
            n = HALF // HD if c < 2 else HKV
            dve.wait_ge(head_squared, i + 1)
            nc.vector.tensor_reduce(SSQ[:, c, b, 0:n], ASQ[:, i % 2, 0:n * HD].rearrange("p (j n) -> p j n", n=HD),
                                    AX_X, ALU.add).then_inc(head_summed, 1)
            dve.wait_ge(head_summed, i + 1)
            nc.vector.tensor_scalar(SSQ[:, c, b, 0:n], SSQ[:, c, b, 0:n], 1.0 / HD, EPS,
                                    ALU.mult, ALU.add).then_inc(head_mean_ready, 1)
            x = QKV[:, b, HALF * c:HALF * c + n * HD].rearrange("p (j n) -> p j n", n=HD)
            g = HD if c == 2 else 0
            nc.vector.tensor_tensor(x, x, GBC[:, g:g + HD].unsqueeze(1).broadcast_to([P, n, HD]),
                                    ALU.mult).then_inc(head_gained, 1)

        def heads_lo(b, g):
            dve.wait_ge(qs_hi, 5 * b + g + 1)
            q = HEAD_GROUP[g]
            if q is not None:
                src = QKV[:, b, HD * GRP * q:HD * GRP * (q + 1)].rearrange("p (j n) -> p j n", n=HD)
                s = slice(GRP * q, GRP * (q + 1))
                nc.vector.tensor_tensor(QS[:, s, HD:P], src, QS[:, s, 0:HD].bitcast(F32),
                                        ALU.subtract).then_inc(qs_ready, 1)
            else:
                src = QKV[:, b, HD * HQ:QKW].rearrange("p (j n) -> p j n", n=HD)
                src = src.unsqueeze(2).broadcast_to([P, HKV, 2, HD])
                hi = QS[:, HQ:HQ + HKV, :].rearrange("p j (s n) -> p j s n", s=2)
                lo = QS[:, HQ + HKV:HQ + 2 * HKV, :].rearrange("p j (s n) -> p j s n", s=2)
                nc.vector.tensor_tensor(lo, src, hi.bitcast(F32), ALU.subtract).then_inc(qs_ready, 1)

        for c in range(2):
            for h in range(2):
                if h:
                    for j in range(1, 5):
                        split_ahead(split_lo, dve, PH_Q, c, j)
                for b in range(HB * h + 1, HB * (h + 1), 2):
                    take_qkv(c, b)
                for b in range(HB * h, HB * (h + 1)):
                    mean_heads(c, b)
        for b in range(1, NBLK, 2):
            if b == NBLK - 1:
                for g in range(HKV + 1):
                    heads_lo(0, g)
            mean_heads(2, b - 1)
            if b < NBLK - 1:
                take_qkv(2, b)
                mean_heads(2, b)

        def take_round(b, i):
            dve.wait_ge(round_done, ROUNDS * b + i + 1)
            src = PS[:, round_bank(b, i), :].rearrange("p (j n) -> p j n", n=P)
            nc.vector.tensor_copy(round_target(b, i), src).then_inc(round_taken_dve, 1)

        def scores_masked(n):
            b, g = n // HKV, n % HKV
            w = P if b == 0 else 2 * P
            at = P if b % 2 == 0 else 0
            dve.wait_ge(scores_done, n + 1)
            if n >= 2:
                dve.wait_ge(probs_turned, pt_count(n - 2, 1))
            for j in range(GRP):
                src = PS[:, score_bank(n, j), (j % 2) * 2 * P:(j % 2) * 2 * P + w]
                h = 2 * HD + GRP * g + j
                nc.vector.tensor_tensor_reduce(
                    out=PR[:, n % 2, j, 0:w], in0=src, in1=MASK[:, at:at + w], scale=-(HD ** -0.5),
                    scalar=GBC[:, h:h + 1], op0=ALU.add, op1=ALU.min,
                    accum_out=STAT[:, n % 3, 0, j:j + 1]).then_inc(scores_read, 1)
            dve.wait_ge(scores_read, 4 * (n + 1))
            sink = GBC[:, 2 * HD + GRP * g:2 * HD + GRP * (g + 1)]
            nc.vector.tensor_tensor(STAT[:, n % 3, 1, :], STAT[:, n % 3, 0, :], sink,
                                    ALU.subtract).then_inc(max_ready, 1)

        def denominators(n):
            dve.wait_ge(exp_done, n + 1)
            nc.vector.tensor_tensor(STAT[:, n % 3, 2, :], STAT[:, n % 3, 2, :], STAT[:, n % 3, 3, :],
                                    ALU.add).then_inc(den_steps, 1)

        def inverses(n):
            dve.wait_ge(den_steps, 2 * n + 1)
            nc.vector.reciprocal(STAT[:, n % 3, 4, :], STAT[:, n % 3, 2, :]).then_inc(den_steps, 1)

        def out_scaled(n):
            dve.wait_ge(values_done, n + 1)
            dve.wait_ge(den_steps, 2 * n + 2)
            if n >= 2:
                dve.wait_ge(out_turned, n - 1)
            inverse = STAT[:, n % 3, 4, :].unsqueeze(2).broadcast_to([P, GRP, HD])
            nc.vector.tensor_tensor(OT[:, n % 2, :].rearrange("p (j n) -> p j n", n=HD),
                                    PS[:, 7, 0:2 * P].rearrange("p (j n) -> p j n", n=HD), inverse,
                                    ALU.mult).then_inc(ot_ready, 1)

        def out_lo(n):
            b, g = n // HKV, n % HKV
            dve.wait_ge(out_hi_ready, n + 1)
            nc.vector.tensor_tensor(H[:, 1, 2 * g:2 * g + 2, blk(b)],
                                    PS[:, 0, 0:2 * P].rearrange("p (k n) -> p k n", n=P),
                                    H[:, 0, 2 * g:2 * g + 2, blk(b)].bitcast(F32), ALU.subtract).then_inc(out_ready, 1)

        n_groups = NBLK * HKV
        dve.wait_ge(w_used, Q_PIECES)
        for i in range(ROUNDS - 1):
            if i not in ROUND_ACT:
                take_round(0, i)
        take_qkv(2, NBLK - 1)
        mean_heads(2, NBLK - 1)
        dve.wait_ge(mask_ready, 2)
        def add(ph, c, last, d0, h, m):
            i = KT * h + m
            if i == 15:
                dve.wait_ge(w_used, ph.piece(c, last) + 1)
            else:
                dve.wait_ge(sum_product_done, c * 15 + (d0 // 16 * 15 + i + 1))
            nc.vector.tensor_tensor(X[:, m, half(h)], X[:, m, half(h)], PS[:, 4 + i % 2, :],
                                    ALU.add).then_inc(add_done, 1)

        for n in range(-2, n_groups + 2):
            for step in heads_beside(n + 1):
                heads_lo(*step)
            if 0 <= n + 1 < n_groups:
                scores_masked(n + 1)
            if 0 <= n < n_groups:
                denominators(n)
            if 0 <= n - 1 < n_groups:
                out_scaled(n - 1)
            if n == n_groups + 1:
                for m in range(2):
                    add(PH_O, 0, 1, D_O, 0, m)
            if n >= 2:
                out_lo(n - 2)
            for r in rounds_beside(n + 2):
                if r and r[1] not in ROUND_ACT:
                    take_round(*r)
            if 0 <= n < n_groups:
                inverses(n)
            if n in O_SPLITS_LO:
                split_lo(dve, PH_O, 0, O_SPLITS_LO.index(n))

        def adds(ph, c, last, d0, norm=None, begin=0, beside=()):
            for i in range(begin, 2 * KT + (LAG if norm else 0)):
                if i < 2 * KT:
                    add(ph, c, last, d0, i // KT, i % KT)
                if norm and i >= LAG:
                    operand_lo(dve, norm, (i - LAG) // KT, (i - LAG) % KT)
                for at, j in beside:
                    if at == i:
                        split_ahead(split_lo, dve, ph, c, j)

        def norm_factors(norm):
            for h in range(2):
                norm_mean(dve, norm, h)
                norm_diagonal(dve, norm, h)

        for c in range(4):
            adds(PH_O, 0, 2 * c + 1, D_O + 16 * c, norm=1 if c == 3 else None,
                 begin=0 if c else 2, beside=[(2, 2 * c - 1), (6, 2 * c)])
        split_ahead(split_lo, dve, PH_O, 0, 7)
        norm_factors(1)

        def inner_lo(c, j, h, tiles):
            dve.wait_ge(a_hi, c * 4 + (2 * (tiles + j) + h + 1))
            nc.vector.tensor_tensor(A[:, j, 1, half(h)], A32[:, h, :], A[:, j, 0, half(h)].bitcast(F32),
                                    ALU.subtract).then_inc(a_ready, 1)

        def scale_gate(l, c, j, h):
            if h == 0:
                dve.wait_ge(g_done, c * 2 + (T_F[l] + j + 1))
            else:
                dve.wait_ge(w_used, PH_F[l].piece(c, 2 * j) + 1)
            dve.wait_ge(rs_ready, 4 * l + h + 1)
            nc.vector.tensor_tensor(PS[:, h, :], PS[:, h, :], RS[:, h, :], ALU.mult).then_inc(g_scaled, 1)

        def multiply(l, c, j, h):
            i = c * 4 + (2 * (T_F[l] + j) + h)
            if h == 0:
                dve.wait_ge(u_done, c * 2 + (U_F[l] + j + 1))
            else:
                dve.wait_ge(w_used, PH_F[l].piece(c, 2 * j + 1) + 1)
            dve.wait_ge(silu_scaled, i + 1)
            first = c * 4 + (2 * (A_F[l] + j) + h)
            if not isinstance(first, int) or first >= 2:
                dve.wait_ge(a_ready, first - 1)
            nc.vector.tensor_tensor(A32[:, h, :], SG[:, h, :], PS[:, 2 + h, :], ALU.mult).then_inc(mul_done, 1)

        def ffn_chunk(l, c, norm=None, ahead=True):
            ph = PH_F[l]
            for j in range(2):
                split_ahead(split_lo, dve, ph, c, 2 * j)
                scale_gate(l, c, j, 0)
                scale_gate(l, c, j, 1)
                if ahead or j == 0:
                    split_ahead(split_lo, dve, ph, c, 2 * j + 1)
                for h in range(2):
                    multiply(l, c, j, h)
                    if (j, h) == (1, 1):
                        add(ph, c, 5, D_F[l], 0, 0)
                    inner_lo(c, j, h, A_F[l])
            if norm is not None:
                adds(ph, c, 5, D_F[l], norm, begin=1, beside=[(1, 4)])
                split_ahead(split_lo, dve, ph, c, 5)
                norm_factors(norm)
            elif ahead:
                adds(ph, c, 5, D_F[l], begin=1, beside=[(1, 4), (9, 5)])

        ffn_chunk(0, 0)
        with dve.Fori(1, F_CHUNKS - 1) as c:
            ffn_chunk(0, c)
        ffn_chunk(0, F_CHUNKS - 1, norm=2)

        nc.vector.memset(ZC[:, 0:CW - 1], 0.0).then_inc(z_halo, 1)

        def tap(c, j, i):
            at = G_CONV + i * KT
            return GT[:, bass.ds(c * 2 + (at + j), 1)]

        def convolve(c, j, h, beside=lambda step: None):
            if h == 0:
                dve.wait_ge(u_done, c * 2 + (2 * F_CHUNKS + j + 1))
            else:
                dve.wait_ge(w_used, PH_C.piece(c, 3 * j + 2) + 1)
            n = c * 4 + (2 * j + h)
            dve.wait_ge(bc_scaled, c * 12 + (6 * j + 2 + 2 * h + 2))
            if h == 0:
                dve.wait_ge(a_ready, c * 4 + 2 * (A_C + j))
            else:
                dve.wait_ge(y_done, n)
            nc.vector.tensor_tensor(ZC[:, CW - 1 + h * HALF:CW - 1 + (h + 1) * HALF], CG[:, half(h)],
                                    PS[:, h, :], ALU.mult).then_inc(z_done, 1)
            beside(0)
            dve.wait_ge(z_done, n + 1)
            dve.wait_ge(z_halo, 1)
            z = [ZC[:, h * HALF + i:(h + 1) * HALF + i] for i in range(CW)]
            nc.vector.tensor_scalar(YC[:], z[0], tap(c, j, 0), None, ALU.mult).then_inc(y_step, 1)
            beside(1)
            dve.wait_ge(y_step, c * 12 + (6 * j + 3 * h + 1))
            nc.vector.scalar_tensor_tensor(YC[:], z[1], tap(c, j, 1), YC[:], ALU.mult, ALU.add).then_inc(y_step, 1)
            beside(2)
            dve.wait_ge(y_step, c * 12 + (6 * j + 3 * h + 2))
            nc.vector.scalar_tensor_tensor(YC[:], z[2], tap(c, j, 2), YC[:], ALU.mult, ALU.add).then_inc(y_step, 1)
            dve.wait_ge(y_step, c * 12 + (6 * j + 3 * h + 3))
            dve.wait_ge(a_ready, c * 4 + (2 * (A_C + j) + h - 1))
            nc.vector.tensor_tensor(A32[:, h, :], BG[:, half(h)], YC[:], ALU.mult).then_inc(y_done, 1)

        def conv_chunk(c, norm=None):
            for j in range(2):
                for i in range(3):
                    split_ahead(split_lo, dve, PH_C, c, 3 * j + i)
                for h in range(2):
                    def first_adds(step):
                        if (j, h) == (1, 1) and step >= 1:
                            add(PH_C, c, 7, D_C, 0, step - 1)

                    convolve(c, j, h, first_adds)
                    if (j, h) == (1, 1):
                        add(PH_C, c, 7, D_C, 0, 2)
                    inner_lo(c, j, h, A_C)
            adds(PH_C, c, 7, D_C, norm, begin=3, beside=[(4, 6)])
            split_ahead(split_lo, dve, PH_C, c, 7)
            if norm is not None:
                norm_factors(norm)

        with dve.Fori(0, C_CHUNKS - 1) as c:
            conv_chunk(c)
        conv_chunk(C_CHUNKS - 1, norm=3)
        ffn_chunk(1, 0)
        with dve.Fori(1, F_CHUNKS - 1) as c:
            ffn_chunk(1, c)
        ffn_chunk(1, F_CHUNKS - 1, ahead=False)

        def take_out(b):
            dve.wait_ge(result_turned, out_count(b, 1))
            nc.vector.tensor_copy(OUTB[:, b, HALF:D], PS[:, (2 * b + 1) % 4, :]).then_inc(result_right, 1)

        for i in range(1, 2 * KT):
            add(PH_F1, F_CHUNKS - 1, 5, D_F1, i // KT, i % KT)
            if KT < i <= KT + HB:
                take_out(i - KT - 1)
        for b in range(HB, NBLK):
            take_out(b)

    def pool_program(pool):
        nc.gpsimd.memset(IDN[:], 0.0).then_inc(idn_cleared, 1)
        pool.wait_ge(idn_cleared, 1)
        nc.gpsimd.affine_select(out=IDN[:], in_=IDN[:], compare_op=ALU.not_equal, fill=1.0, base=0,
                                pattern=[[-1, P]], channel_multiplier=1).then_inc(idn_ready, 1)
        nc.gpsimd.memset(MASK[:], 0.0).then_inc(mask_cleared, 1)
        nc.gpsimd.memset(MH[:], -0.5).then_inc(mask_cleared, 1)
        pool.wait_ge(mask_cleared, 2)
        nc.gpsimd.affine_select(out=MASK[:, P:2 * P], in_=MASK[:, P:2 * P], compare_op=ALU.is_ge, fill=NEG, base=0,
                                pattern=[[-1, P]], channel_multiplier=1).then_inc(mask_ready, 1)
        for at in (0, 2 * P):
            m = nc.gpsimd.affine_select(out=MASK[:, at:at + P], in_=MASK[:, at:at + P], compare_op=ALU.is_gt,
                                        fill=NEG, base=0, pattern=[[1, P]], channel_multiplier=-1)
        m.then_inc(mask_ready, 1)
        pool.wait_ge(tok_mean_ready, 1)
        nc.gpsimd.tensor_tensor(TOK[:, 1, :], TOK[:, 0, :], MH[:], ALU.pow).then_inc(tok_rms_ready, 1)
        pool.wait_ge(tok_rms_ready, 1)

        def heads(c, b):
            i = NBLK * c + b
            n = HALF // HD if c < 2 else HKV
            x = QKV[:, b, HALF * c:HALF * c + n * HD].rearrange("p (j n) -> p j n", n=HD)
            pool.wait_ge(head_mean_ready, i + 1)
            nc.gpsimd.tensor_tensor(RR[:, c, b, 0:n], SSQ[:, c, b, 0:n], MH[:, 0:n],
                                    ALU.pow).then_inc(head_root_ready, 1)
            pool.wait_ge(head_root_ready, i + 1)
            pool.wait_ge(head_gained, i + 1)
            nc.gpsimd.tensor_tensor(x, x, RR[:, c, b, 0:n].unsqueeze(2).broadcast_to([P, n, HD]),
                                    ALU.mult).then_inc(head_normed, 1)
            pool.wait_ge(head_normed, i + 1)
            hr = ROT // 2
            cos = COS[:, b, :].unsqueeze(1).broadcast_to([P, n, ROT])
            sin = [SIN[:, b, s * hr:(s + 1) * hr].unsqueeze(1).broadcast_to([P, n, hr]) for s in range(2)]
            nc.gpsimd.tensor_tensor(RT[:, 0:n, :], x[:, :, 0:ROT], cos, ALU.mult).then_inc(rotation_terms, 1)
            nc.gpsimd.tensor_tensor(RU[:, 0:n, 0:hr], x[:, :, hr:ROT], sin[0], ALU.mult).then_inc(rotation_terms, 1)
            nc.gpsimd.tensor_tensor(RU[:, 0:n, hr:ROT], x[:, :, 0:hr], sin[1], ALU.mult).then_inc(rotation_terms, 1)
            pool.wait_ge(rotation_terms, 3 * i + 3)
            nc.gpsimd.tensor_tensor(x[:, :, 0:ROT], RT[:, 0:n, :], RU[:, 0:n, :], ALU.add).then_inc(head_rotated, 1)
            pool.wait_ge(head_rotated, i + 1)

        pool.wait_ge(trig_ready, 4)
        for c in range(2):
            for b in range(NBLK):
                heads(c, b)

        def heads_hi(b, g):
            pool.wait_ge(head_rotated, NBLK * HEAD_COLUMNS[g] + b + 1)
            if b:
                pool.wait_ge(round_done, ROUNDS * (b - 1) + HEADS_USED[g])
            q = HEAD_GROUP[g]
            if q is not None:
                src = QKV[:, b, HD * GRP * q:HD * GRP * (q + 1)].rearrange("p (j n) -> p j n", n=HD)
                nc.gpsimd.tensor_copy(QS[:, GRP * q:GRP * (q + 1), 0:HD], src).then_inc(qs_hi, 1)
            else:
                src = QKV[:, b, HD * HQ:QKW].rearrange("p (j n) -> p j n", n=HD)
                src = src.unsqueeze(2).broadcast_to([P, HKV, 2, HD])
                dst = QS[:, HQ:HQ + HKV, :].rearrange("p j (s n) -> p j s n", s=2)
                nc.gpsimd.tensor_copy(dst, src).then_inc(qs_hi, 1)

        pool.wait_ge(w_split, Q_PIECES)
        heads(2, 0)
        for g in range(HKV + 1):
            heads_hi(0, g)
        for b in range(1, NBLK):
            if b == 5:
                for step in heads_beside(0):
                    heads_hi(*step)
            heads(2, b)
        for s in range(1, NBLK * HKV):
            for step in heads_beside(s):
                heads_hi(*step)

        pool.wait_ge(out_ready, NBLK * HKV)
        nc.gpsimd.memset(NS[:, 8:12], -0.5).then_inc(exponent_ready, 1)
        pool.wait_ge(exponent_ready, 1)

        def both_halves(n):
            for h in range(2):
                norm_accumulate(pool, n, h)
            for h in range(2):
                norm_root(pool, n, h)

        def scale_silu(l):
            pool.wait_ge(rs_ready, 4 * l + 2)
            with pool.Fori(0, 2 * F_CHUNKS) as i:
                for h in range(2):
                    pool.wait_ge(silu_done, i * 2 + (2 * T_F[l] + h + 1))
                    nc.gpsimd.tensor_tensor(SG[:, h, :], SG[:, h, :], RS[:, h, :], ALU.mult).then_inc(silu_scaled, 1)

        def scale_gated():
            pool.wait_ge(rs_ready, 4)
            with pool.Fori(0, 2 * C_CHUNKS) as i:
                for h in range(2):
                    pool.wait_ge(bc_copied, i * 4 + (h + 1))
                    nc.gpsimd.tensor_tensor(BG[:, half(h)], BG[:, half(h)], RS[:, h, :],
                                            ALU.mult).then_inc(bc_scaled, 1)
                for h in range(2):
                    for twice in range(2):
                        pool.wait_ge(bc_scaled, i * 6 + (2 + 2 * h + twice))
                        if not twice:
                            pool.wait_ge(bc_copied, i * 4 + (h + 3))
                        nc.gpsimd.tensor_tensor(CG[:, half(h)], CG[:, half(h)], RS[:, h, :],
                                                ALU.mult).then_inc(bc_scaled, 1)

        both_halves(1)
        scale_silu(0)
        both_halves(2)
        scale_gated()
        both_halves(3)
        scale_silu(1)

    block = ctx.enter_context(nc.Block())
    block.sync(sync_program)
    block.gpsimd(pool_program)
    block.scalar(scalar_program)
    block.vector(vector_program)
    block.tensor(tensor_program)


NAMES = ["x", "positions", "mix_norm", "ffn_norm", "a_w_qkv", "a_q_norm", "a_k_norm", "a_sinks", "a_w_o",
         "b_w_in", "b_conv_w", "b_w_out", "f_w_gate_up", "f_w_down"]


def kernel(**inputs):
    from contextlib import ExitStack

    import concourse.bacc as bacc
    from concourse.bass_utils import run_bass_kernel_spmd

    nc = bacc.Bacc("TRN2", target_bir_lowering=False, num_devices=1)
    arrays, tensors = {}, {}
    for name in NAMES:
        a = np.ascontiguousarray(inputs[name])
        arrays["in_" + name] = a
        tensors[name] = nc.dram_tensor("in_" + name, a.shape, mybir.dt.from_np(a.dtype), kind="ExternalInput").ap()
    out = nc.dram_tensor("out_x", (1, S, D), F32, kind="ExternalOutput").ap()
    with ExitStack() as ctx:
        decoder_kernel(nc, ctx, tensors, out)
    return run_bass_kernel_spmd(nc, [arrays], core_ids=[0]).results[0]["out_x"]
```
